# Optimizing a Trainium2 kernel written in Bass

```python
import jax, jax.numpy as jnp
from jax import lax
import numpy as np

D_MODEL = 1024
BATCH = 1
SEQ = 2048
DEPTH = 1
DEC_BATCH = 8
DEC_SEQ = 1
PAST_LEN = 4096
PAGE_SIZE = 128

D_MIX = D_MODEL
D_ATT = D_MIX // 2
D_POOL = D_MIX - D_ATT
N_HEADS = 8
V_DIM = D_ATT // N_HEADS
NOPE_DIM = 64
ROPE_DIM = 32
QK_DIM = NOPE_DIM + ROPE_DIM
Q_LORA = 256
KV_LORA = 128
ROPE_BASE = 10000.0
POOL_WINDOWS = (2, 4, 8, 16)
N_POOL_GROUPS = len(POOL_WINDOWS)
POOL_GROUP = D_POOL // N_POOL_GROUPS
POOL_PREV = max(POOL_WINDOWS) - 1
Q_BLOCK = 128
EPS = 1e-6
SM_SCALE = QK_DIM ** -0.5
OFF_Q = 0
OFF_KV = OFF_Q + Q_LORA
OFF_KR = OFF_KV + KV_LORA
OFF_GA = OFF_KR + ROPE_DIM
OFF_U = OFF_GA + D_ATT
OFF_GP = OFF_U + D_POOL
D_IN = OFF_GP + D_POOL

kernel_name = "hymba_mla_pool_decode_step"

def rmsnorm(x, w):
    xf = x.astype(jnp.float32)
    y = xf * lax.rsqrt(jnp.mean(xf * xf, axis=-1, keepdims=True) + EPS)
    return (y * w.astype(jnp.float32)).astype(x.dtype)

def rope(x, pos):
    r = x.shape[-1]
    inv = ROPE_BASE ** (-jnp.arange(0, r, 2, dtype=jnp.float32) / r)
    ang = pos.astype(jnp.float32)[:, None] * inv[None, :]
    shp = (ang.shape[0],) + (1,) * (x.ndim - 3) + (r // 2,)
    cos = jnp.cos(ang).reshape(shp)
    sin = jnp.sin(ang).reshape(shp)
    xf = x.astype(jnp.float32)
    x1, x2 = xf[..., : r // 2], xf[..., r // 2:]
    return jnp.concatenate([x1 * cos - x2 * sin, x2 * cos + x1 * sin], axis=-1).astype(x.dtype)

def branch_inputs(x, c, pos, ada_w, ada_b, norm_w, w_in, q_norm_w, w_uq, kv_norm_w):
    mod = jnp.einsum('bd,de->be', jax.nn.silu(c), ada_w) + ada_b
    shift, scale, gate = jnp.split(mod, 3, axis=-1)
    h = rmsnorm(x, norm_w) * (1 + scale[:, None, :]) + shift[:, None, :]
    z = jnp.einsum('btd,de->bte', h, w_in)
    q_lat = rmsnorm(z[..., OFF_Q:OFF_KV], q_norm_w)
    ckv = rmsnorm(z[..., OFF_KV:OFF_KR], kv_norm_w)
    kr = rope(z[..., OFF_KR:OFF_GA], pos)
    g_att = z[..., OFF_GA:OFF_U]
    u = z[..., OFF_U:OFF_GP]
    g_pool = z[..., OFF_GP:]
    q = jnp.einsum('btq,qhd->bthd', q_lat, w_uq)
    q_nope = q[..., :NOPE_DIM]
    q_rope = rope(q[..., NOPE_DIM:], pos)
    return gate, q_nope, q_rope, ckv, kr, g_att, u, g_pool

def attn_prompt(q_nope, q_rope, ckv, kr, w_uk, w_uv):
    b, s = q_nope.shape[:2]
    k_nope = jnp.einsum('bsk,khd->bshd', ckv, w_uk)
    v = jnp.einsum('bsk,khv->bshv', ckv, w_uv)
    nb = s // Q_BLOCK
    qn = q_nope.reshape(b, nb, Q_BLOCK, N_HEADS, NOPE_DIM).transpose(1, 0, 2, 3, 4)
    qr = q_rope.reshape(b, nb, Q_BLOCK, N_HEADS, ROPE_DIM).transpose(1, 0, 2, 3, 4)
    kpos = jnp.arange(s)

    def block(args):
        qn_b, qr_b, i = args
        sc = (jnp.einsum('bqhd,bshd->bhqs', qn_b, k_nope)
              + jnp.einsum('bqhr,bsr->bhqs', qr_b, kr)).astype(jnp.float32) * SM_SCALE
        qpos = i * Q_BLOCK + jnp.arange(Q_BLOCK)
        sc = jnp.where(kpos[None, :] <= qpos[:, None], sc, -jnp.inf)
        p = jax.nn.softmax(sc, axis=-1).astype(v.dtype)
        return jnp.einsum('bhqs,bshv->bqhv', p, v)

    o = lax.map(block, (qn, qr, jnp.arange(nb)))
    return o.transpose(1, 0, 2, 3, 4).reshape(b, s, N_HEADS * V_DIM)

def attn_sample(q_nope, q_rope, ckv, kr, cache_ckv_l, cache_kr_l, page_table, w_uk, w_uv):
    db, t = q_nope.shape[:2]
    past_ckv = cache_ckv_l[page_table].reshape(db, -1, KV_LORA)
    past_kr = cache_kr_l[page_table].reshape(db, -1, ROPE_DIM)
    n_past = past_ckv.shape[1]
    q_abs = jnp.einsum('bthd,khd->bthk', q_nope, w_uk)
    s_past = jnp.einsum('bthk,bsk->bhts', q_abs, past_ckv) + jnp.einsum('bthr,bsr->bhts', q_rope, past_kr)
    s_new = jnp.einsum('bthk,bsk->bhts', q_abs, ckv) + jnp.einsum('bthr,bsr->bhts', q_rope, kr)
    s_new = jnp.where(jnp.tril(jnp.ones((t, t), dtype=bool)), s_new, -jnp.inf)
    sc = jnp.concatenate([s_past, s_new], axis=-1).astype(jnp.float32) * SM_SCALE
    p = jax.nn.softmax(sc, axis=-1).astype(ckv.dtype)
    o_lat = (jnp.einsum('bhts,bsk->bthk', p[..., :n_past], past_ckv)
             + jnp.einsum('bhts,bsk->bthk', p[..., n_past:], ckv))
    o = jnp.einsum('bthk,khv->bthv', o_lat, w_uv)
    return o.reshape(db, t, N_HEADS * V_DIM)

def pool_branch(u, prev, pos0, w_pool, b_pool, pool_scale):
    b, t, _ = u.shape
    u_ext = jnp.concatenate([prev, u], axis=1)
    cs = jnp.cumsum(u_ext.astype(jnp.float32), axis=1)
    cs0 = jnp.concatenate([jnp.zeros((b, 1, D_POOL), jnp.float32), cs], axis=1)
    pos = (pos0 + jnp.arange(t)).astype(jnp.float32)
    outs = []
    for g, w in enumerate(POOL_WINDOWS):
        lo, hi = g * POOL_GROUP, (g + 1) * POOL_GROUP
        wsum = (cs0[:, POOL_PREV + 1:POOL_PREV + 1 + t, lo:hi]
                - cs0[:, POOL_PREV + 1 - w:POOL_PREV + 1 - w + t, lo:hi])
        cnt = jnp.minimum(pos + 1.0, float(w))[None, :, None]
        outs.append(wsum / cnt - u[..., lo:hi].astype(jnp.float32))
    pooled = jnp.stack(outs, axis=2).astype(u.dtype)
    y = jnp.einsum('btgc,gcd->btgd', pooled, w_pool) + b_pool
    y = y.reshape(b, t, D_POOL) * pool_scale
    return y, u_ext[:, -POOL_PREV:]

def combine(x, gate, att, g_att, pool, g_pool, w_out):
    mixed = jnp.concatenate([att * jax.nn.silu(g_att), pool * jax.nn.silu(g_pool)], axis=-1)
    return x + gate[:, None, :] * jnp.einsum('bte,ed->btd', mixed, w_out)

def setup_inputs(seed: int = 0) -> dict:
    key = jax.random.key(seed)
    ks = jax.random.split(key, 32)
    n_pages = PAST_LEN // PAGE_SIZE
    n_pool_pages = (DEC_BATCH * n_pages * 5) // 4
    f32 = jnp.float32
    nrm = lambda k, shp, s=1.0: jax.random.normal(k, shp, f32) * s
    perm = jax.random.permutation(ks[7], n_pool_pages)[: DEC_BATCH * n_pages]
    return {
        "x_prompt": nrm(ks[0], (BATCH, SEQ, D_MODEL)),
        "x_sample": nrm(ks[1], (DEC_BATCH, DEC_SEQ, D_MODEL)),
        "c_prompt": nrm(ks[2], (BATCH, D_MODEL)),
        "c_sample": nrm(ks[3], (DEC_BATCH, D_MODEL)),
        "cache_ckv": nrm(ks[4], (DEPTH, n_pool_pages, PAGE_SIZE, KV_LORA)),
        "cache_krope": nrm(ks[5], (DEPTH, n_pool_pages, PAGE_SIZE, ROPE_DIM)),
        "state_pool": nrm(ks[6], (DEPTH, DEC_BATCH, POOL_PREV, D_POOL)),
        "page_table": perm.reshape(DEC_BATCH, n_pages).astype(jnp.int32),
        "ada_w": nrm(ks[8], (DEPTH, D_MODEL, 3 * D_MODEL), D_MODEL ** -0.5),
        "ada_b": nrm(ks[9], (DEPTH, 3 * D_MODEL), 0.02),
        "norm_w": 1.0 + nrm(ks[10], (DEPTH, D_MODEL), 0.02),
        "w_in": nrm(ks[11], (DEPTH, D_MODEL, D_IN), D_MODEL ** -0.5),
        "q_norm_w": 1.0 + nrm(ks[12], (DEPTH, Q_LORA), 0.02),
        "w_uq": nrm(ks[13], (DEPTH, Q_LORA, N_HEADS, QK_DIM), Q_LORA ** -0.5),
        "kv_norm_w": 1.0 + nrm(ks[14], (DEPTH, KV_LORA), 0.02),
        "w_uk": nrm(ks[15], (DEPTH, KV_LORA, N_HEADS, NOPE_DIM), KV_LORA ** -0.5),
        "w_uv": nrm(ks[16], (DEPTH, KV_LORA, N_HEADS, V_DIM), KV_LORA ** -0.5),
        "w_pool": nrm(ks[17], (DEPTH, N_POOL_GROUPS, POOL_GROUP, POOL_GROUP), POOL_GROUP ** -0.5),
        "b_pool": nrm(ks[18], (DEPTH, N_POOL_GROUPS, POOL_GROUP), 0.01),
        "pool_scale": 1.0 + nrm(ks[19], (DEPTH, D_POOL), 0.05),
        "w_out": nrm(ks[20], (DEPTH, D_MIX, D_MODEL), D_MIX ** -0.5),
        "final_norm_w": 1.0 + nrm(ks[21], (D_MODEL,), 0.02),
    }

def reference(x_prompt, x_sample, c_prompt, c_sample, cache_ckv, cache_krope, state_pool, page_table,
              ada_w, ada_b, norm_w, w_in, q_norm_w, w_uq, kv_norm_w, w_uk, w_uv,
              w_pool, b_pool, pool_scale, w_out, final_norm_w):
    pos_p = jnp.arange(x_prompt.shape[1])
    pos_s = PAST_LEN + jnp.arange(x_sample.shape[1])
    xp, xs = x_prompt, x_sample
    ckv_p_l, kr_p_l, pool_p_l, ckv_s_l, kr_s_l, pool_s_l = [], [], [], [], [], []
    for l in range(DEPTH):
        gate, qn, qr, ckv, kr, g_att, u, g_pool = branch_inputs(
            xp, c_prompt, pos_p, ada_w[l], ada_b[l], norm_w[l], w_in[l], q_norm_w[l], w_uq[l], kv_norm_w[l])
        att = attn_prompt(qn, qr, ckv, kr, w_uk[l], w_uv[l])
        prev0 = jnp.zeros((xp.shape[0], POOL_PREV, D_POOL), u.dtype)
        pool, new_prev = pool_branch(u, prev0, 0, w_pool[l], b_pool[l], pool_scale[l])
        xp = combine(xp, gate, att, g_att, pool, g_pool, w_out[l])
        ckv_p_l.append(ckv); kr_p_l.append(kr); pool_p_l.append(new_prev)
        gate, qn, qr, ckv, kr, g_att, u, g_pool = branch_inputs(
            xs, c_sample, pos_s, ada_w[l], ada_b[l], norm_w[l], w_in[l], q_norm_w[l], w_uq[l], kv_norm_w[l])
        att = attn_sample(qn, qr, ckv, kr, cache_ckv[l], cache_krope[l], page_table, w_uk[l], w_uv[l])
        pool, new_prev = pool_branch(u, state_pool[l], PAST_LEN, w_pool[l], b_pool[l], pool_scale[l])
        xs = combine(xs, gate, att, g_att, pool, g_pool, w_out[l])
        ckv_s_l.append(ckv); kr_s_l.append(kr); pool_s_l.append(new_prev)
    y_prompt = rmsnorm(xp, final_norm_w)
    y_sample = rmsnorm(xs, final_norm_w)
    return (y_prompt, y_sample,
            jnp.stack(ckv_p_l), jnp.stack(kr_p_l), jnp.stack(pool_p_l),
            jnp.stack(ckv_s_l), jnp.stack(kr_s_l), jnp.stack(pool_s_l))


_drawn_inputs = setup_inputs


def setup_inputs(seed=0):
    import zlib

    import numpy as np

    out = dict(_drawn_inputs(seed))
    spreads = {}
    factors = {'cache_ckv': 7.106,
     'cache_krope': 8.0,
     'norm_w': 3.021,
     'q_norm_w': 8.0,
     'kv_norm_w': 8.075,
     'b_pool': 8.0,
     'pool_scale': 3.213,
     'final_norm_w': 7.661}
    for name, (base, spread) in spreads.items():
        noise = np.random.default_rng([zlib.crc32(name.encode()), seed]).standard_normal(out[name].shape)
        drawn = base * np.exp(spread * noise) if base else spread * noise
        out[name] = __import__('jax').numpy.asarray(drawn.astype(out[name].dtype))
    for name, factor in factors.items():
        out[name] = (out[name] * factor).astype(out[name].dtype)
    return out
```

```python
from contextlib import ExitStack

import numpy as np

import concourse.bass as bass
from concourse import mybir

F32 = mybir.dt.float32
F32R = mybir.dt.float32r
BF16 = mybir.dt.bfloat16
I32 = mybir.dt.int32
U32 = mybir.dt.uint32
ALU = mybir.AluOpType
ACT = mybir.ActivationFunctionType
AX = mybir.AxisListType

P = 128
D = 1024
KC = D // P
S = 2048
NB = S // P
DB = 8
NC = DB + 1
H = 8
NOPE, ROPE, VD = 64, 32, 64
QK = NOPE + ROPE
QL, KVL = 256, 128
QC = QL // P
DATT = H * VD
DPOOL = 512
NG = 4
PREV = 15
OFF_KV, OFF_KR, OFF_GA = QL, QL + KVL, QL + KVL + ROPE
DIN = OFF_GA + DATT + 2 * DPOOL
LA = OFF_GA
LB = DIN - OFF_GA
OFF_U, OFF_GP = DATT, DATT + DPOOL
EPS = 1e-6
SCALE = QK ** -0.5
NPG, PG = 32, 128
QTR = 4
TPP = PG // QTR
MASKED = -1e30
BASE = 16896
GRP = 4
NGRP = NB // GRP


class Map:

    def __init__(self, nc, start):
        self.nc, self.at = nc, start

    def __call__(self, name, shape, dt):
        size = {F32: 4, F32R: 4, BF16: 2, I32: 4, U32: 4}[dt]
        n = int(np.prod(shape[1:])) * size
        t = self.nc.alloc_sbuf_tensor_at(name, list(shape), dt, offset=self.at)
        self.at += (n + 31) // 32 * 32
        assert self.at <= 229344, (name, self.at)
        return t


def exists(n, count):
    return not isinstance(n, int) or 0 <= n < count


def stage_semaphore(nc, sems, name):
    sems.append(nc.alloc_semaphore(name))
    return sems[-1]


def release(nc, sems):
    nc.clear_and_free_semaphores(sems)
    nc.all_engine_barrier()


def peeled(eng, count, body, tail=1):
    body(0)
    with eng.Fori(1, count - tail) as i:
        body(i)
    for i in range(count - tail, count):
        body(i)


def mm3(pe, out, lhs, rhs, first, last):
    pe.matmul(out, lhs[0], rhs[0], start=first, stop=False)
    pe.matmul(out, lhs[0], rhs[1], start=False, stop=False)
    return pe.matmul(out, lhs[1], rhs[0], start=False, stop=last)


def build(nc, t, o):
    x_blocks = t["x_prompt"].rearrange("a (n p) d -> p (a n) d", p=P)
    ckv_out = o[2].rearrange("a b (n p) k -> p (a b n) k", p=P)
    kr_out = o[3].rearrange("a b (n p) k -> p (a b n) k", p=P)
    w_in = t["w_in"].rearrange("a (c p) n -> p (a c) n", p=P)

    mod_d = nc.dram_tensor("mod_scratch", (NC, 3 * D), F32, kind="Internal").ap()
    zs_d = nc.dram_tensor("sample_z_scratch", (DB, DIN), F32, kind="Internal").ap()
    gate_att_d = nc.dram_tensor("gate_att_scratch", (S, DATT), F32, kind="Internal").ap()
    pool_d = nc.dram_tensor("pool_scratch", (NG, P, S), F32, kind="Internal").ap()
    att_d = nc.dram_tensor("att_scratch", (S, DATT), F32, kind="Internal").ap()
    gate_att_blocks = gate_att_d.rearrange("(n p) e -> p n e", p=P)

    keep = Map(nc, BASE)
    ident = keep("ident", [P, P], F32)
    identb = keep("identb", [P, P], BF16)
    mask_q = keep("mask_q", [P, P], BF16)
    mask_k = keep("mask_k", [P, P], BF16)
    ones = keep("ones", [P, P], F32)
    rstd = keep("rstd", [P, NB + 1], F32)
    coef_a = keep("coef_a", [P, KC, NC], F32)
    coef_b = keep("coef_b", [P, KC, NC], F32)
    vec_t = keep("vec_t", [P, 16], F32)
    lat_t = keep("lat_t", [P, 3, S], F32)
    after_lat = keep.at
    hs = [keep("hs_hi", [P, KC, P], F32R), keep("hs_lo", [P, KC, P], F32R)]
    after_hs = keep.at

    m = Map(nc, after_hs)
    wa = [m("wa_hi", [P, KC, LA], F32R), m("wa_lo", [P, KC, LA], F32R)]
    after_wa = m.at
    with ExitStack() as ctx:
        sems = []
        ctx.callback(release, nc, sems)

        def psum(name, shape):
            return ctx.enter_context(nc.psum_tensor("mod_" + name, shape, F32))

        def sem(name):
            return stage_semaphore(nc, sems, "mod_" + name)

        NX = 3
        xt = m("mod_x", [P, NX, D], F32)
        xs = m("mod_xs", [DB, D], F32)
        wa_raw = m("wa_raw", [P, KC, LA], F32)
        c_sb = m("c_sb", [NC, D], F32)
        c_act = m("c_act", [P, KC, NC], F32)
        vecs = m("vecs", [16, P], F32)
        bias = m("ada_b_rows", [NC, 3 * D], F32)
        mod = m("mod_rows", [NC, 3 * D], F32)
        NA = 5
        ada = m("ada", [P, NA, 3 * D], F32)
        ss = m("x_ss", [P, NB + 1], F32)
        masks = m("masks_f32", [P, 2, P], F32)
        junk_s = m("junk_s", [DB, D], F32)
        hs32 = m("hs32", [P, KC, DB], F32)
        ps_mod = psum("ps_mod", [P, 6, 512])
        ps_c = psum("ps_c", [P, 512])
        ps_t = psum("ps_t", [P, 512])

        const_in, masks_in, c_in, small_in, xs_in = sem("const_in"), sem("masks_in"), sem("c_in"), sem("small_in"), sem("xs_in")
        ada_in = [sem(f"ada_in{k}") for k in range(NA)]
        x_in = [sem(f"x_in{k}") for k in range(NX)]
        wa_in = sem("wa_in")
        c_turned, c_ready, vec_turned, vec_ready = sem("c_turned"), sem("c_ready"), sem("vec_turned"), sem("vec_ready")
        ada_used, mod_summed, mod_ready, mod_turned = sem("ada_used"), sem("mod_summed"), sem("mod_ready"), sem("mod_turned")
        x_squared, ss_ready, ss_zero, var_ready, sd_ready, rstd_ready = (
            sem("x_squared"), sem("ss_ready"), sem("ss_zero"), sem("var_ready"), sem("sd_ready"), sem("rstd_ready"))
        wa_hi_ready, wa_lo_ready = sem("wa_hi_ready"), sem("wa_lo_ready")
        hs_zero, xs_scaled, xs_turned, hs_done, coef_ready, mod_out = (
            sem("hs_zero"), sem("xs_scaled"), sem("xs_turned"), sem("hs_done"), sem("coef_ready"), sem("mod_out"))

        ada_rows = t["ada_w"].rearrange("a (c p) n -> p (a c) n", p=P)
        block = ctx.enter_context(nc.Block())

        @block.sync
        def _(sp):
            sp.dma_start(ident[:], t["c_ident"]).then_inc(const_in, 16)
            sp.dma_start(c_sb[0:DB, :], t["c_sample"]).then_inc(c_in, 16)
            sp.dma_start(c_sb[DB:NC, :], t["c_prompt"]).then_inc(c_in, 16)
            for k in range(KC):
                if k >= NA:
                    sp.wait_ge(ada_used, k - NA + 1)
                sp.dma_start(ada[:, k % NA, :], ada_rows[:, k, :]).then_inc(ada_in[k % NA], 16)
                if k == 0:
                    sp.dma_start(vecs[0:8, :], t["norm_w"].rearrange("a (c p) -> (a c) p", p=P)).then_inc(small_in, 16)
                    sp.dma_start(vecs[8:12, :], t["b_pool"][0]).then_inc(small_in, 16)
                    sp.dma_start(vecs[12:16, :], t["pool_scale"].rearrange("a (c p) -> (a c) p", p=P)).then_inc(small_in, 16)
                    sp.dma_start(bias[:], t["ada_b"].rearrange("a n -> (a n)").partition_broadcast(NC)).then_inc(small_in, 16)
                    sp.dma_start(masks[:, 0, :], t["c_mask_q"]).then_inc(masks_in, 16)
                    sp.dma_start(masks[:, 1, :], t["c_mask_k"]).then_inc(masks_in, 16)
            sp.wait_ge(mod_ready, 6)
            sp.dma_start(mod_d, mod[:]).then_inc(mod_out, 16)
            sp.wait_ge(mod_out, 16)

        @block.scalar
        def _(act):
            act.dma_start(xs[:], t["x_sample"].rearrange("b s d -> (b s) d")).then_inc(xs_in, 16)
            for n in range(NX):
                act.dma_start(xt[:, n, :], x_blocks[:, n, :]).then_inc(x_in[n], 16)
            act.dma_start(wa_raw[:], w_in[:, :, 0:LA]).then_inc(wa_in, 16)
            act.wait_ge(c_turned, 1)
            act.activation(c_act[:].rearrange("p c n -> p (c n)"), ps_c[:, 0:KC * NC], ACT.Silu).then_inc(c_ready, 1)
            act.wait_ge(ss_zero, 1)
            act.wait_ge(xs_in, 16)
            act.activation(junk_s[:], xs[:], ACT.Square, accum_out=ss[0:DB, NB:NB + 1]).then_inc(x_squared, 1)
            for n in range(NB):
                act.wait_ge(x_in[n % NX], 16 * (n // NX + 1))
                act.activation(xt[:, n % NX, :], xt[:, n % NX, :], ACT.Square,
                               accum_out=ss[:, n:n + 1]).then_inc(x_squared, 1)
                if n >= 1 and n - 1 + NX < NB:
                    act.wait_ge(x_squared, n + 1)
                    act.dma_start(xt[:, (n - 1) % NX, :], x_blocks[:, n - 1 + NX, :]).then_inc(x_in[(n - 1) % NX], 16)
            act.wait_ge(var_ready, 1)
            act.activation(ss[:], ss[:], ACT.Sqrt).then_inc(sd_ready, 1)
            act.wait_ge(wa_in, 16)
            act.activation(wa[0][:], wa_raw[:], ACT.Copy).then_inc(wa_hi_ready, 1)

        @block.gpsimd
        def _(pool):
            pool.memset(ones[:], 1.0)
            for part in hs:
                last = pool.memset(part[:].bitcast(F32), 0.0)
            last.then_inc(hs_zero, 1)
            pool.wait_ge(const_in, 16)
            pool.tensor_copy(identb[:], ident[:])
            pool.wait_ge(masks_in, 32)
            pool.tensor_copy(mask_q[:], masks[:, 0, :])
            pool.tensor_copy(mask_k[:], masks[:, 1, :])
            pool.wait_ge(wa_hi_ready, 1)
            pool.tensor_tensor(wa[1][:], wa_raw[:], wa[0][:].bitcast(F32), ALU.subtract).then_inc(wa_lo_ready, 1)

        @block.vector
        def _(dve):
            dve.memset(ss[:], 0.0).then_inc(ss_zero, 1)
            dve.wait_ge(vec_turned, 1)
            dve.tensor_copy(vec_t[:], ps_t[:, 0:16]).then_inc(vec_ready, 1)
            dve.wait_ge(small_in, 64)
            dve.wait_ge(x_squared, NB + 1)
            dve.tensor_scalar(ss[:], ss[:], 1.0 / D, EPS, ALU.mult, ALU.add).then_inc(var_ready, 1)
            dve.wait_ge(sd_ready, 1)
            dve.reciprocal(rstd[:], ss[:]).then_inc(rstd_ready, 1)
            dve.wait_ge(rstd_ready, 1)
            dve.tensor_scalar(xs[:], xs[:], rstd[0:DB, NB:NB + 1], None, ALU.mult).then_inc(xs_scaled, 1)
            dve.wait_ge(mod_summed, 1)
            for g in range(6):
                dve.tensor_tensor(mod[:, g * 512:(g + 1) * 512], ps_mod[0:NC, g, :], bias[:, g * 512:(g + 1) * 512],
                                  ALU.add).then_inc(mod_ready, 1)
            dve.wait_ge(vec_ready, 1)
            dve.wait_ge(mod_turned, 1)
            turned = ps_c[:, 0:2 * KC * NC].rearrange("p (k c n) -> p k c n", k=2, c=KC)
            dve.tensor_copy(coef_b[:], turned[:, 0])
            dve.scalar_tensor_tensor(out=coef_a[:], in0=turned[:, 1], scalar=1.0,
                                     in1=vec_t[:, 0:KC].unsqueeze(2).broadcast_to([P, KC, NC]),
                                     op0=ALU.add, op1=ALU.mult).then_inc(coef_ready, 1)
            dve.wait_ge(coef_ready, 1)
            dve.wait_ge(xs_turned, 1)
            xs_t = ps_t[:, 64:64 + KC * DB].rearrange("p (c b) -> p c b", c=KC)
            dve.tensor_tensor(hs32[:], xs_t, coef_a[:, :, 0:DB], ALU.mult).then_inc(hs_done, 1)
            dve.wait_ge(hs_done, 1)
            dve.tensor_tensor(hs32[:], hs32[:], coef_b[:, :, 0:DB], ALU.add).then_inc(hs_done, 1)
            dve.wait_ge(hs_done, 2)
            dve.wait_ge(hs_zero, 1)
            dve.tensor_copy(hs[0][:, :, 0:DB], hs32[:]).then_inc(hs_done, 1)
            dve.wait_ge(hs_done, 3)
            dve.tensor_tensor(hs[1][:, :, 0:DB], hs32[:], hs[0][:, :, 0:DB].bitcast(F32), ALU.subtract).then_inc(hs_done, 1)

        @block.tensor
        def _(pe):
            pe.wait_ge(const_in, 16)
            pe.wait_ge(c_in, 32)
            for k in range(KC):
                last = pe.transpose(ps_c[:, k * NC:(k + 1) * NC], c_sb[:, k * P:(k + 1) * P], ident[0:NC, 0:NC])
            last.then_inc(c_turned, 1)
            pe.wait_ge(small_in, 64)
            pe.transpose(ps_t[:, 0:16], vecs[:], ident[0:16, 0:16]).then_inc(vec_turned, 1)
            pe.wait_ge(c_ready, 1)
            for k in range(KC):
                pe.wait_ge(ada_in[k % NA], 16 * (k // NA + 1))
                for g in range(6):
                    last = pe.matmul(ps_mod[0:NC, g, :], c_act[:, k, :], ada[:, k % NA, g * 512:(g + 1) * 512],
                                     start=(k == 0), stop=(k == KC - 1))
                last.then_inc(mod_summed if k == KC - 1 else ada_used, 1)
            pe.wait_ge(xs_scaled, 1)
            pe.wait_ge(vec_ready, 1)
            for k in range(KC):
                last = pe.transpose(ps_t[:, 64 + k * DB:64 + (k + 1) * DB], xs[:, k * P:(k + 1) * P], ident[0:DB, 0:DB])
            last.then_inc(xs_turned, 1)
            pe.wait_ge(mod_ready, 4)
            for k in range(2 * KC):
                last = pe.transpose(ps_c[:, k * NC:(k + 1) * NC], mod[:, k * P:(k + 1) * P], ident[0:NC, 0:NC])
            last.then_inc(mod_turned, 1)

    wb_at = Map(nc, after_wa)
    wb = [wb_at("wb_hi", [P, KC, LB], F32R), wb_at("wb_lo", [P, KC, LB], F32R)]
    ds = bass.ds
    with ExitStack() as ctx:
        sems = []
        ctx.callback(release, nc, sems)

        def psum(name, shape):
            return ctx.enter_context(nc.psum_tensor("lat_" + name, shape, F32))

        def sem(name):
            return stage_semaphore(nc, sems, "lat_" + name)

        m = Map(nc, wb_at.at)
        xt = m("lat_x", [P, 2, D], F32)
        h32 = m("lat_h32", [P, D], F32)
        hb = [m("lat_h_hi", [P, 2, D], F32R), m("lat_h_lo", [P, 2, D], F32R)]
        wraw = m("lat_wraw", [P, LB], F32)
        lat = m("lat_rows", [P, 2, LA], F32)
        junk = m("lat_junk", [P, 2, OFF_KR], F32)
        stat = m("lat_stat", [P, 2, 2], F32)
        rot = m("lat_rot", [P, 2, ROPE], F32)
        qn_w = m("qn_w", [P, QL], F32)
        kn_w = m("kn_w", [P, KVL], F32)
        cosk = m("cosk", [P, NB, ROPE], F32)
        sink = m("sink", [P, NB, ROPE], F32)
        zs = m("zs_a", [DB, LA], F32)
        ps_x = psum("ps_x", [P, 2, 512])
        ps_z = psum("ps_z", [P, 2, 512])
        ps_l = psum("ps_l", [P, 512])
        ps_s = psum("ps_s", [P, 512])
        x_in = [sem("x_in0"), sem("x_in1")]
        tab_in, wb_in = sem("tab_in"), sem("wb_in")
        x_scaled, x_turned, h_ready, h_hi, h_lo = (
            sem("x_scaled"), sem("x_turned"), sem("h_ready"), sem("h_hi"), sem("h_lo"))
        z_done, ss_ready, var_ready, sd_ready, step_done = (
            sem("z_done"), sem("ss_ready"), sem("var_ready"), sem("sd_ready"), sem("step_done"))
        lat_ready, lat_turned, lat_kept = sem("lat_ready"), sem("lat_turned"), sem("lat_kept")
        lat_out = [sem("lat_out0"), sem("lat_out1")]
        wb_hi, wb_lo = sem("wb_hi_ready"), sem("wb_lo_ready")
        zs_done, zs_ready, zs_out = sem("zs_done"), sem("zs_ready"), sem("zs_out")
        NP2 = NB // 2
        block = ctx.enter_context(nc.Block())

        @block.sync
        def _(sp):
            for b in range(2):
                sp.dma_start(xt[:, b, :], x_blocks[:, b, :]).then_inc(x_in[b], 16)
            sp.dma_start(qn_w[:], t["q_norm_w"].rearrange("a n -> (a n)").partition_broadcast(P)).then_inc(tab_in, 16)
            sp.dma_start(kn_w[:], t["kv_norm_w"].rearrange("a n -> (a n)").partition_broadcast(P)).then_inc(tab_in, 16)
            sp.dma_start(cosk[:], t["c_rope_rows"][0]).then_inc(tab_in, 16)
            sp.dma_start(sink[:], t["c_rope_rows"][1]).then_inc(tab_in, 16)

            def body(i):
                for b in range(2):
                    n = 2 * i + b
                    if exists(n + 2, NB):
                        sp.wait_ge(x_turned, n + 1)
                        sp.dma_start(xt[:, b, :], x_blocks[:, ds(n + 2, 1), :]).then_inc(x_in[b], 16)
                if exists(i - 1, KC):
                    sp.wait_ge(wb_lo, i)
                sp.dma_start(wraw[:].unsqueeze(1), w_in[:, ds(i, 1), LA:DIN]).then_inc(wb_in, 16)
            peeled(sp, NP2, body)
            sp.wait_ge(zs_ready, 1)
            sp.dma_start(zs_d[:, 0:LA], zs[:]).then_inc(zs_out, 16)
            sp.wait_ge(zs_out, 16)

        @block.scalar
        def _(act):
            def scale_x(n, b):
                act.wait_ge(x_in[b], 16 * (n // 2 + 1) if isinstance(n, int) else 8 * (n - b) + 16)
                act.activation(xt[:, b, :], xt[:, b, :], ACT.Copy, scale=rstd[:, ds(n, 1)]).then_inc(x_scaled, 1)

            def h_high(n, b):
                act.wait_ge(h_ready, n + 1)
                if exists(n - 2, NB):
                    act.wait_ge(z_done, n - 1)
                act.activation(hb[0][:, b, :], h32[:], ACT.Copy).then_inc(h_hi, 1)

            def keep_lat(n, b):
                act.wait_ge(lat_turned, n + 1)
                act.activation(lat_t[:, :, ds(n * P, P)], ps_l[:, 0:3 * P].rearrange("p (c s) -> p c s", c=3),
                               ACT.Copy).then_inc(lat_kept, 1)
                act.dma_start(ckv_out[:, ds(n, 1), :], lat[:, b, OFF_KV:OFF_KR].unsqueeze(1)).then_inc(lat_out[b], 16)
                act.dma_start(kr_out[:, ds(n, 1), :], lat[:, b, OFF_KR:LA].unsqueeze(1)).then_inc(lat_out[b], 16)

            def body(i):
                for b in range(2):
                    n = 2 * i + b
                    if exists(n + 2, NB):
                        h_high(n + 2, b)
                    if exists(n + 3, NB):
                        scale_x(n + 3, 1 - b)
                    act.wait_ge(z_done, n + 1)
                    if exists(n - 2, NB):
                        act.wait_ge(var_ready, n - 1)
                    act.activation(junk[:, b, 0:QL], ps_z[:, b, 0:QL], ACT.Square, accum_out=stat[:, b, 0:1])
                    act.activation(junk[:, b, OFF_KV:OFF_KR], ps_z[:, b, OFF_KV:OFF_KR], ACT.Square,
                                   accum_out=stat[:, b, 1:2]).then_inc(ss_ready, 1)
                    if exists(n - 1, NB):
                        keep_lat(n - 1, 1 - b)
                    act.wait_ge(var_ready, n + 1)
                    act.activation(stat[:, b, :], stat[:, b, :], ACT.Sqrt).then_inc(sd_ready, 1)
                act.wait_ge(wb_in, 16 * i + 16)
                act.activation(wb[0][:, ds(i, 1), :], wraw[:].unsqueeze(1), ACT.Copy).then_inc(wb_hi, 1)
            scale_x(0, 0)
            scale_x(1, 1)
            h_high(0, 0)
            h_high(1, 1)
            scale_x(2, 0)
            peeled(act, NP2, body, tail=2)
            keep_lat(NB - 1, 1)
            for b in range(2):
                act.wait_ge(lat_out[b], 16 * NB)

        @block.gpsimd
        def _(pool):
            def h_low(n, b):
                pool.wait_ge(h_hi, n + 1)
                pool.tensor_tensor(hb[1][:, b, :], h32[:], hb[0][:, b, :].bitcast(F32), ALU.subtract).then_inc(h_lo, 1)

            def body(i):
                for b in range(2):
                    if exists(2 * i + b + 2, NB):
                        h_low(2 * i + b + 2, b)
                pool.wait_ge(wb_hi, i + 1)
                pool.tensor_tensor(wb[1][:, ds(i, 1), :], wraw[:].unsqueeze(1), wb[0][:, ds(i, 1), :].bitcast(F32),
                                   ALU.subtract).then_inc(wb_lo, 1)
            h_low(0, 0)
            h_low(1, 1)
            peeled(pool, NP2, body)

        @block.vector
        def _(dve):
            def h_values(n):
                dve.wait_ge(x_turned, n + 1)
                if exists(n - 1, NB):
                    dve.wait_ge(h_lo, n)
                for c in range(KC):
                    last = dve.tensor_scalar(h32[:, c * P:(c + 1) * P], ps_x[:, c // 4, (c % 4) * P:(c % 4 + 1) * P],
                                             coef_a[:, c, DB:NC], coef_b[:, c, DB:NC], ALU.mult, ALU.add)
                last.then_inc(h_ready, 1)

            def body(i):
                for b in range(2):
                    n = 2 * i + b
                    if exists(n + 2, NB):
                        h_values(n + 2)
                    dve.wait_ge(ss_ready, n + 1)
                    dve.tensor_scalar(stat[:, b, 0:1], stat[:, b, 0:1], 1.0 / QL, EPS, ALU.mult, ALU.add)
                    dve.tensor_scalar(stat[:, b, 1:2], stat[:, b, 1:2], 1.0 / KVL, EPS, ALU.mult, ALU.add).then_inc(var_ready, 1)
                    if exists(n - 2, NB):
                        dve.wait_ge(lat_turned, n - 1)
                        dve.wait_ge(lat_out[b], 32 * i if b == 0 else 32 * i)
                    z = ps_z[:, b, :]
                    dve.tensor_tensor(lat[:, b, OFF_KR:LA], z[:, OFF_KR:LA], cosk[:, ds(n, 1), :].squeeze(1), ALU.mult)
                    dve.tensor_tensor(rot[:, b, 0:16], z[:, OFF_KR + 16:LA], sink[:, ds(n, 1), 0:16].squeeze(1), ALU.mult)
                    dve.tensor_tensor(rot[:, b, 16:32], z[:, OFF_KR:OFF_KR + 16], sink[:, ds(n, 1), 16:32].squeeze(1),
                                      ALU.mult).then_inc(step_done, 1)
                    dve.wait_ge(step_done, 2 * n + 1)
                    dve.tensor_tensor(lat[:, b, OFF_KR:LA], lat[:, b, OFF_KR:LA], rot[:, b, :], ALU.add)
                    dve.wait_ge(sd_ready, n + 1)
                    dve.reciprocal(stat[:, b, :], stat[:, b, :]).then_inc(step_done, 1)
                    dve.wait_ge(step_done, 2 * n + 2)
                    dve.scalar_tensor_tensor(out=lat[:, b, 0:QL], in0=z[:, 0:QL], scalar=stat[:, b, 0:1], in1=qn_w[:],
                                             op0=ALU.mult, op1=ALU.mult)
                    dve.scalar_tensor_tensor(out=lat[:, b, OFF_KV:OFF_KR], in0=z[:, OFF_KV:OFF_KR], scalar=stat[:, b, 1:2],
                                             in1=kn_w[:], op0=ALU.mult, op1=ALU.mult).then_inc(lat_ready, 1)
            dve.wait_ge(tab_in, 64)
            h_values(0)
            h_values(1)
            peeled(dve, NP2, body)
            dve.wait_ge(zs_done, 1)
            dve.tensor_copy(zs[:], ps_s[0:DB, 0:LA]).then_inc(zs_ready, 1)

        @block.tensor
        def _(pe):
            def turn_x(n, b):
                pe.wait_ge(x_scaled, n + 1)
                if exists(n - 1, NB):
                    pe.wait_ge(h_ready, n)
                for c in range(KC):
                    last = pe.transpose(ps_x[:, c // 4, (c % 4) * P:(c % 4 + 1) * P], xt[:, b, c * P:(c + 1) * P], ident[:])
                last.then_inc(x_turned, 1)

            def turn_lat(n, b):
                pe.wait_ge(lat_ready, n + 1)
                if exists(n - 1, NB):
                    pe.wait_ge(lat_kept, n)
                for c in range(3):
                    last = pe.transpose(ps_l[:, c * P:(c + 1) * P], lat[:, b, c * P:(c + 1) * P], ident[:])
                last.then_inc(lat_turned, 1)

            def body(i):
                for b in range(2):
                    n = 2 * i + b
                    if exists(n + 2, NB):
                        turn_x(n + 2, b)
                    pe.wait_ge(h_lo, n + 1)
                    if exists(n - 2, NB):
                        pe.wait_ge(lat_ready, n - 1)
                    for c in range(KC):
                        cols = slice(c * P, (c + 1) * P)
                        last = mm3(pe, ps_z[:, b, 0:LA], [hb[0][:, b, cols], hb[1][:, b, cols]],
                                   [wa[0][:, c, :], wa[1][:, c, :]], c == 0, c == KC - 1)
                    last.then_inc(z_done, 1)
                    if exists(n - 1, NB):
                        turn_lat(n - 1, 1 - b)
            turn_x(0, 0)
            turn_x(1, 1)
            peeled(pe, NP2, body)
            turn_lat(NB - 1, 1)
            for c in range(KC):
                last = mm3(pe, ps_s[:, 0:LA], [hs[0][:, c, :], hs[1][:, c, :]],
                           [wa[0][:, c, :], wa[1][:, c, :]], c == 0, c == KC - 1)
            last.then_inc(zs_done, 1)

    T = 2 * P
    NS = S // T
    with ExitStack() as ctx:
        sems = []
        ctx.callback(release, nc, sems)

        def psum(name, shape):
            return ctx.enter_context(nc.psum_tensor("mix_" + name, shape, F32))

        def sem(name):
            return stage_semaphore(nc, sems, "mix_" + name)

        m = Map(nc, after_hs)
        u_ext = m("u_ext", [P, NG, PREV + T], F32)
        win = m("win", [P, 2, 2, PREV + T], F32)
        pooled = m("pooled", [P, NG, T], F32)
        gate_p = m("gate_p", [P, NG, T], F32)
        mixed = m("mixed", [P, NG, T], F32)
        gate_a = m("gate_a", [P, 2, DATT], F32)
        assert m.at <= after_wa
        m = Map(nc, wb_at.at)
        hb = [m("mix_h_hi", [P, 2, KC, T], F32R), m("mix_h_lo", [P, 2, KC, T], F32R)]
        xt = m("mix_x", [P, 2, D], F32)
        h32 = m("mix_h32", [P, D], F32)
        w_pool = m("w_pool", [P, NG, P], F32)
        count = m("count", [P, NG, 16], F32)
        early = m("early", [P, 16], F32)
        prev = m("prev", [PREV, DPOOL], F32)
        zs_b = xt[0:DB].rearrange("p b d -> p (b d)")[:, 0:LB]
        ps_x = psum("ps_x", [P, 2, 512])
        ps_u = psum("ps_u", [P, 2, 512])
        ps_a = psum("ps_a", [P, 2, 512])
        ps_y = psum("ps_y", [P, 2, 512])
        ps_z = [ps_a[:, 0, :], ps_a[:, 1, :]]
        x_in = [sem("x_in0"), sem("x_in1")]
        tab_in = sem("tab_in")
        x_scaled, x_turned, h_ready, h_hi, h_lo = (
            sem("x_scaled"), sem("x_turned"), sem("h_ready"), sem("h_hi"), sem("h_lo"))
        u_done, u_kept, win_step, win_ready, pooled_ready, halo_ready = (
            sem("u_done"), sem("u_kept"), sem("win_step"), sem("win_ready"), sem("pooled_ready"), sem("halo_ready"))
        a_done, a_kept, y_done, y_step, mixed_ready = (
            sem("a_done"), sem("a_kept"), sem("y_done"), sem("y_step"), sem("mixed_ready"))
        early_step = sem("early_step")
        mixed_out = [sem(f"mixed_out{g}") for g in range(NG)]
        a_out = [sem("a_out0"), sem("a_out1")]
        zs_done, zs_ready, zs_out, prev_done, prev_ready = (
            sem("zs_done"), sem("zs_ready"), sem("zs_out"), sem("prev_done"), sem("prev_ready"))
        HALF = NS // 2
        LEVELS = sum(g + 1 for g in range(NG))
        block = ctx.enter_context(nc.Block())

        @block.sync
        def _(sp):
            for b in range(2):
                sp.dma_start(xt[:, b, :], x_blocks[:, b, :]).then_inc(x_in[b], 16)
            sp.dma_start(w_pool[:], t["w_pool"].rearrange("a g c d -> c (a g) d")).then_inc(tab_in, 16)
            sp.dma_start(count[:].rearrange("p g s -> p (g s)"),
                         t["c_count"].rearrange("g s -> (g s)").partition_broadcast(P)).then_inc(tab_in, 16)

            def load_x(n, b):
                sp.wait_ge(x_turned, n - 1)
                sp.dma_start(xt[:, b, :], x_blocks[:, ds(n, 1), :]).then_inc(x_in[b], 16)

            def body(s, e):
                for b in range(2):
                    if exists(s + 2, NS):
                        load_x(2 * s + 4 + b, b)
                for b in range(2):
                    sp.wait_ge(a_kept, 2 * s + b + 1)
                    sp.dma_start(gate_att_blocks[:, ds(2 * s + b, 1), :], gate_a[:, b, :].unsqueeze(1)).then_inc(a_out[b], 16)
                for g in range(NG):
                    sp.wait_ge(mixed_ready, 4 * s + g + 1)
                    sp.dma_start(pool_d[g][:, ds(s * T, T)], mixed[:, g, :]).then_inc(mixed_out[g], 16)
            for b in range(2):
                load_x(2 + b, b)
            peeled(sp, HALF, lambda i: [body(2 * i + e, e) for e in range(2)])
            sp.wait_ge(zs_ready, 3)
            sp.dma_start(zs_d[:, LA:DIN], zs_b).then_inc(zs_out, 16)
            sp.wait_ge(prev_ready, 1)
            sp.dma_start(o[4].rearrange("a b r c -> (a b r) c"), prev[:]).then_inc(zs_out, 16)
            sp.wait_ge(zs_out, 32)
            for b in range(2):
                sp.wait_ge(a_out[b], 16 * NS)
            for g in range(NG):
                sp.wait_ge(mixed_out[g], 16 * NS)

        @block.scalar
        def _(act):
            def scale_x(n, b):
                act.wait_ge(x_in[b], 8 * (n - b) + 16)
                act.activation(xt[:, b, :], xt[:, b, :], ACT.Copy, scale=rstd[:, ds(n, 1)]).then_inc(x_scaled, 1)

            def h_high(s, e, b):
                act.wait_ge(h_ready, 2 * s + b + 1)
                if exists(s - 2, NS):
                    act.wait_ge(a_done, 2 * (s - 1))
                act.activation(hb[0][:, e, :, b * P:(b + 1) * P], h32[:].rearrange("p (c s) -> p c s", c=KC),
                               ACT.Copy).then_inc(h_hi, 1)

            def keep_u(s, g):
                act.wait_ge(u_done, 4 * s + g + 1)
                act.wait_ge(halo_ready, 4 * s + g + 1)
                act.activation(u_ext[:, g, PREV:], ps_u[:, g % 2, 0:T], ACT.Copy)
                if exists(s - 1, NS):
                    act.wait_ge(mixed_ready, 4 * (s - 1) + g + 1)
                act.activation(gate_p[:, g, :], ps_u[:, g % 2, T:2 * T], ACT.Silu).then_inc(u_kept, 1)

            def body(s, e):
                for b in range(2):
                    if exists(s + 1, NS):
                        h_high(s + 1, 1 - e, b)
                    keep_u(s, 2 * b)
                    keep_u(s, 2 * b + 1)
                for b in range(2):
                    if exists(s + 2, NS):
                        scale_x(2 * s + 4 + b, b)
                for b in range(2):
                    act.wait_ge(a_done, 2 * s + b + 1)
                    if exists(s - 1, NS):
                        act.wait_ge(a_out[b], 16 * s)
                    act.activation(gate_a[:, b, :], ps_a[:, b, :], ACT.Silu).then_inc(a_kept, 1)
            for b in range(2):
                scale_x(b, b)
            for b in range(2):
                h_high(0, 0, b)
            for b in range(2):
                scale_x(2 + b, b)
            peeled(act, HALF, lambda i: [body(2 * i + e, e) for e in range(2)])

        @block.gpsimd
        def _(pool):
            steps = [0]

            def h_low(s, e, b):
                pool.wait_ge(h_hi, 2 * s + b + 1)
                pool.tensor_tensor(hb[1][:, e, :, b * P:(b + 1) * P], h32[:].rearrange("p (c s) -> p c s", c=KC),
                                   hb[0][:, e, :, b * P:(b + 1) * P].bitcast(F32), ALU.subtract).then_inc(h_lo, 1)

            def window(s, g, done):
                pool.wait_ge(u_kept, 4 * s + g + 1)
                if g >= 2:
                    pool.wait_ge(pooled_ready, 4 * s + g - 1)
                elif exists(s - 1, NS):
                    pool.wait_ge(pooled_ready, 4 * (s - 1) + g + 3)
                src = u_ext[:, g, :]
                for level in range(g + 1):
                    shift = 1 << level
                    width = T + (1 << (g + 1)) - 2 * shift
                    if level:
                        pool.wait_ge(win_step, s * LEVELS + done + level)
                    dst = win[:, g % 2, level % 2, PREV + T - width:]
                    last = pool.tensor_tensor(dst, src[:, PREV + T - width:PREV + T],
                                              src[:, PREV + T - width - shift:PREV + T - shift], ALU.add)
                    last.then_inc(win_step, 1)
                    src = win[:, g % 2, level % 2, :]

            def body(s, e):
                done = 0
                for b in range(2):
                    if exists(s + 1, NS):
                        h_low(s + 1, 1 - e, b)
                    for g in (2 * b, 2 * b + 1):
                        window(s, g, done)
                        done += g + 1
            pool.memset(u_ext[:], 0.0).then_inc(halo_ready, NG)
            for b in range(2):
                h_low(0, 0, b)
            peeled(pool, HALF, lambda i: [body(2 * i + e, e) for e in range(2)])

        @block.vector
        def _(dve):
            def h_values(n):
                dve.wait_ge(x_turned, n + 1)
                if exists(n - 1, NB):
                    dve.wait_ge(h_lo, n)
                for c in range(KC):
                    last = dve.tensor_scalar(h32[:, c * P:(c + 1) * P], ps_x[:, c // 4, (c % 4) * P:(c % 4 + 1) * P],
                                             coef_a[:, c, DB:NC], coef_b[:, c, DB:NC], ALU.mult, ALU.add)
                last.then_inc(h_ready, 1)

            def pooled_values(s, g, done):
                dve.wait_ge(win_step, s * LEVELS + done)
                if exists(s - 1, NS):
                    dve.wait_ge(y_done, 4 * (s - 1) + g + 1)
                total = win[:, g % 2, g % 2, PREV:]
                first = isinstance(s, int) and s == 0
                if first:
                    dve.tensor_tensor(early[:], total[:, 0:16], count[:, g, :], ALU.mult).then_inc(early_step, 1)
                    dve.wait_ge(early_step, 2 * g + 1)
                    dve.tensor_tensor(pooled[:, g, 0:16], early[:], u_ext[:, g, PREV:PREV + 16],
                                      ALU.subtract).then_inc(early_step, 1)
                    dve.wait_ge(early_step, 2 * g + 2)
                z = 16 if first else 0
                dve.scalar_tensor_tensor(out=pooled[:, g, z:], in0=total[:, z:], scalar=1.0 / (2 << g),
                                         in1=u_ext[:, g, PREV + z:], op0=ALU.mult, op1=ALU.subtract).then_inc(pooled_ready, 1)
                dve.wait_ge(pooled_ready, 4 * s + g + 1)
                if exists(s + 1, NS):
                    dve.tensor_copy(u_ext[:, g, 0:PREV], u_ext[:, g, T:]).then_inc(halo_ready, 1)

            def mix(s, g):
                dve.wait_ge(y_done, 4 * s + g + 1)
                if exists(s - 1, NS):
                    dve.wait_ge(mixed_out[g], 16 * s)
                dve.tensor_scalar(mixed[:, g, :], ps_y[:, g % 2, 0:T], vec_t[:, 8 + g:9 + g], vec_t[:, 12 + g:13 + g],
                                  ALU.add, ALU.mult).then_inc(y_step, 1)
                dve.wait_ge(y_step, 4 * s + g + 1)
                dve.tensor_tensor(mixed[:, g, :], mixed[:, g, :], gate_p[:, g, :], ALU.mult).then_inc(mixed_ready, 1)

            def body(s, e):
                done = 0
                for b in range(2):
                    if exists(s + 1, NS):
                        h_values(2 * s + 2 + b)
                    for g in (2 * b, 2 * b + 1):
                        done += g + 1
                        pooled_values(s, g, done)
                for g in range(NG):
                    mix(s, g)
            dve.wait_ge(tab_in, 32)
            for b in range(2):
                h_values(b)
            peeled(dve, HALF, lambda i: [body(2 * i + e, e) for e in range(2)])
            for k in range(3):
                dve.wait_ge(zs_done, k + 1)
                dve.tensor_copy(zs_b[:, k * 512:(k + 1) * 512], ps_z[k % 2][0:DB, :]).then_inc(zs_ready, 1)
            dve.wait_ge(prev_done, 1)
            dve.tensor_copy(prev[:], ps_y[0:PREV, 0, :]).then_inc(prev_ready, 1)

        @block.tensor
        def _(pe):
            def turn_x(n, b):
                pe.wait_ge(x_scaled, n + 1)
                if exists(n - 1, NB):
                    pe.wait_ge(h_ready, n)
                for c in range(KC):
                    last = pe.transpose(ps_x[:, c // 4, (c % 4) * P:(c % 4 + 1) * P], xt[:, b, c * P:(c + 1) * P], ident[:])
                last.then_inc(x_turned, 1)

            def group(s, e, g):
                if g >= 2:
                    pe.wait_ge(u_kept, 4 * s + g - 1)
                elif exists(s - 1, NS):
                    pe.wait_ge(u_kept, 4 * (s - 1) + g + 3)
                for off, at in ((OFF_U, 0), (OFF_GP, T)):
                    cols = slice(off + g * P, off + (g + 1) * P)
                    for c in range(KC):
                        last = mm3(pe, ps_u[:, g % 2, at:at + T], [wb[0][:, c, cols], wb[1][:, c, cols]],
                                   [hb[0][:, e, c, :], hb[1][:, e, c, :]], c == 0, c == KC - 1)
                last.then_inc(u_done, 1)

            def body(s, e):
                pe.wait_ge(h_lo, 2 * s + 2)
                for b in range(2):
                    if exists(s + 1, NS):
                        turn_x(2 * s + 2 + b, b)
                    group(s, e, 2 * b)
                    group(s, e, 2 * b + 1)
                for b in range(2):
                    if exists(s - 1, NS):
                        pe.wait_ge(a_kept, 2 * (s - 1) + b + 1)
                    for c in range(KC):
                        cols = slice(b * P, (b + 1) * P)
                        last = mm3(pe, ps_a[:, b, :], [hb[0][:, e, c, cols], hb[1][:, e, c, cols]],
                                   [wb[0][:, c, 0:DATT], wb[1][:, c, 0:DATT]], c == 0, c == KC - 1)
                    last.then_inc(a_done, 1)
                for g in range(NG):
                    pe.wait_ge(pooled_ready, 4 * s + g + 1)
                    if g >= 2:
                        pe.wait_ge(y_step, 4 * s + g - 1)
                    elif exists(s - 1, NS):
                        pe.wait_ge(y_step, 4 * (s - 1) + g + 3)
                    pe.matmul(ps_y[:, g % 2, 0:T], w_pool[:, g, :], pooled[:, g, :], start=True, stop=True).then_inc(y_done, 1)
            for b in range(2):
                turn_x(b, b)
            peeled(pe, HALF, lambda i: [body(2 * i + e, e) for e in range(2)])
            pe.wait_ge(a_kept, NB)
            for k in range(3):
                if k == 2:
                    pe.wait_ge(zs_ready, 1)
                for c in range(KC):
                    cols = slice(k * 512, (k + 1) * 512)
                    last = mm3(pe, ps_z[k % 2], [hs[0][:, c, :], hs[1][:, c, :]],
                               [wb[0][:, c, cols], wb[1][:, c, cols]], c == 0, c == KC - 1)
                last.then_inc(zs_done, 1)
            pe.wait_ge(y_step, 4 * NS)
            for g in range(NG):
                last = pe.transpose(ps_y[0:PREV, 0, g * P:(g + 1) * P], u_ext[:, g, T:], ident[:])
            last.then_inc(prev_done, 1)

    VW = VD + 1
    tiles = [(I, j) for I in range(NGRP) for j in range(GRP * I + GRP)]
    chunks = [(I, r, c) for I in range(NGRP) for r in range(GRP) for c in range(I + 1)]
    NT, NCH = len(tiles), len(chunks)
    assert NT % 4 == 0 and NCH % 2 == 0

    def tile_cols(k):
        I, j = tiles[k]
        c0 = max(0, j - GRP * I) * P
        return c0, GRP * P - c0

    def side_work():
        side = [[] for _ in range(NT)]
        for k, c in ((1, 0), (3, 1), (5, 2), (8, 3)):
            side[k].append(("prepare", c))
        start = 6
        for n in range(NCH):
            k = start + n * (NT - start) // NCH
            if n:
                k = max(k, last_k)
            last_k = k
            side[k].append(("maxima", n))
            if n + 1 == NCH or chunks[n + 1][0] != chunks[n][0]:
                I = chunks[n][0]
                if I < NGRP - 1:
                    side[max(k + 2, 9)].append(("turn", I))
        return side
    side = side_work()
    LASTG = NGRP - 1

    with ExitStack() as ctx:
        sems = []
        ctx.callback(release, nc, sems)

        def psum(name, shape):
            return ctx.enter_context(nc.psum_tensor("att_" + name, shape, F32))

        def sem(name):
            return stage_semaphore(nc, sems, "att_" + name)

        lat_lo = nc.alloc_sbuf_tensor_at("lat_lo", [P, 3, S], F32R, offset=after_lat - 3 * S * 4)
        m = Map(nc, after_lat)
        lat_hi = m("lat_hi", [P, 3, S], F32R)
        v = m("v", [P, NB, H, VW], F32)
        q = [[m(f"q_hi{e}", [P, S], F32R), m(f"q_lo{e}", [P, S], F32R)] for e in range(2)]
        kk = [[m(f"k_hi{e}", [P, S], F32R), m(f"k_lo{e}", [P, S], F32R)] for e in range(2)]
        rope = m("rope", [P, S], F32)
        pt = m("pt", [P, 4, 512], F32)
        q32 = m("q32", [P, 2, 512], F32)
        rot = m("att_rot", [P, 512], F32)
        wq_raw = m("wq_raw", [P, QC, P], F32)
        wk_raw = m("wk_raw", [P, VD], F32)
        wq = [m("wq_hi", [P, QC, P], F32R), m("wq_lo", [P, QC, P], F32R)]
        wk = [m("wk_hi", [P, P], F32R), m("wk_lo", [P, P], F32R)]
        mx = m("mx", [P, 2, GRP, NGRP], F32)
        negm = m("negm", [P, 2, GRP], F32)
        rec = m("rec", [P, 2, GRP], F32)
        att = m("att", [P, 2, GRP, VD], F32)
        early_map = Map(nc, m.at)
        wv = [early_map("wv_hi", [P, DATT], F32R), early_map("wv_lo", [P, DATT], F32R)]
        wv_raw = early_map("wv_raw", [P, DATT], F32)
        kr = early_map("kr_rows", [P, NB, ROPE], F32)
        ps_s, ps_p, ps_o = psum("ps_s", [P, 2, 512]), psum("ps_p", [P, 2, 512]), psum("ps_o", [P, 2, 512])
        ps_q, ps_k = psum("ps_q", [P, 512]), psum("ps_k", [P, 512])

        kr_in, wv_in, rope_in, wq_in = sem("kr_in"), sem("wv_in"), sem("rope_in"), sem("wq_in")
        lat_hi_ready, lat_lo_ready, filled = sem("lat_hi_ready"), sem("lat_lo_ready"), sem("filled")
        wv_hi_ready, wv_ready, wq_hi_ready, wq_ready = sem("wv_hi_ready"), sem("wv_ready"), sem("wq_hi_ready"), sem("wq_ready")
        kr_turned, kr_hi_ready, kr_kept, v_done, v_kept = (
            sem("kr_turned"), sem("kr_hi_ready"), sem("kr_kept"), sem("v_done"), sem("v_kept"))
        q_done, k_done, q_read, q32_ready, q_hi_ready, q_lo_ready, k_hi_ready, k_kept = (
            sem("q_done"), sem("k_done"), sem("q_read"), sem("q32_ready"), sem("q_hi_ready"), sem("q_lo_ready"),
            sem("k_hi_ready"), sem("k_kept"))
        chunk_done, chunk_read, negm_ready, m_turned, m_kept = (
            sem("chunk_done"), sem("chunk_read"), sem("negm_ready"), sem("m_turned"), sem("m_kept"))
        scores_done, exp_done, pv_done, rec_ready, att_ready = (
            sem("scores_done"), sem("exp_done"), sem("pv_done"), sem("rec_ready"), sem("att_ready"))
        att_out = [sem("att_out0"), sem("att_out1")]
        wuq = t["w_uq"].rearrange("a (c p) h d -> p (a c) h d", p=P)
        wuk = t["w_uk"].rearrange("a k h d -> k (a h) d")
        att_groups = att_d.rearrange("(g r p) (h d) -> p g r h d", p=P, r=GRP, h=H)
        HP = H // 2
        block = ctx.enter_context(nc.Block())

        @block.sync
        def _(sp):
            def load_weights(g):
                one = ds(g, 1)
                sp.dma_start(wq_raw[:, :, 0:QK].unsqueeze(2), wuq[:, :, one, :]).then_inc(wq_in, 16)
                sp.dma_start(wq_raw[:, :, QK:QK + 16].unsqueeze(2), wuq[:, :, one, NOPE + 16:QK]).then_inc(wq_in, 16)
                sp.dma_start(wq_raw[:, :, QK + 16:P].unsqueeze(2), wuq[:, :, one, NOPE:NOPE + 16]).then_inc(wq_in, 16)
                sp.dma_start(wk_raw[:].unsqueeze(1), wuk[:, one, :]).then_inc(wq_in, 16)

            def store(h, I):
                sp.wait_ge(att_ready, NGRP * h + I + 1)
                sp.dma_start(att_groups[:, I, :, ds(h, 1), :].squeeze(2), att[:, I % 2]).then_inc(att_out[I % 2], 16)

            def body(h, e):
                if exists(h + 2, H):
                    sp.wait_ge(wq_ready, h + 2)
                    load_weights(h + 2)
                for I in range(NGRP):
                    store(h, I)
            load_weights(0)
            sp.dma_start(kr[:], kr_out).then_inc(kr_in, 16)
            sp.dma_start(wv_raw[:], t["w_uv"].rearrange("a k h d -> (a k) (h d)")).then_inc(wv_in, 16)
            sp.dma_start(rope[:], t["c_rope_cols"]).then_inc(rope_in, 16)
            sp.wait_ge(wq_ready, 1)
            load_weights(1)
            peeled(sp, HP, lambda i: [body(2 * i + e, e) for e in range(2)])
            for e in range(2):
                sp.wait_ge(att_out[e], 16 * H * NGRP // 2)

        @block.scalar
        def _(act):
            def prepare(g, slot, c):
                cols = slice(c * 512, (c + 1) * 512)
                act.wait_ge(k_done, NGRP * g + c + 1)
                act.activation(kk[slot][0][0:NOPE, cols], ps_k[0:NOPE, :], ACT.Copy).then_inc(k_hi_ready, 1)
                act.wait_ge(q32_ready, NGRP * g + c + 1)
                act.activation(q[slot][0][0:QK, cols], q32[0:QK, c % 2, :], ACT.Copy).then_inc(q_hi_ready, 1)

            def keep_max(g, slot, I):
                act.wait_ge(m_turned, NGRP * g + I + 1)
                act.activation(q[slot][0][QK:QK + 1, I * 512:(I + 1) * 512], ps_k[0:1, :], ACT.Copy).then_inc(m_kept, 1)

            def weights_high(g):
                act.wait_ge(wq_in, 64 * g + 64)
                if exists(g - 1, H):
                    act.wait_ge(k_done, NGRP * g)
                act.activation(wq[0][:], wq_raw[:], ACT.Copy)
                act.activation(wk[0][:, 0:NOPE], wk_raw[:], ACT.Copy).then_inc(wq_hi_ready, 1)

            def exponentials(h, k):
                c0, n = tile_cols(k)
                act.wait_ge(scores_done, NT * h + k + 1)
                if exists(NT * h + k - 4, NT * H):
                    act.wait_ge(pv_done, NT * h + k - 3)
                act.activation(pt[:, k % 4, 0:n], ps_s[:, k % 2, 0:n], ACT.Exp, scale=SCALE).then_inc(exp_done, 1)

            def body(h, e):
                for k in range(NT):
                    exponentials(h, k)
                    if k == 1:
                        keep_max(h, e, LASTG)
                    if exists(h + 1, H):
                        for what, n in side[k]:
                            if what == "prepare":
                                prepare(h + 1, 1 - e, n)
                            elif what == "turn":
                                keep_max(h + 1, 1 - e, n)
                    if k == NT // 2 and exists(h + 2, H):
                        weights_high(h + 2)
            weights_high(0)
            for c in range(NGRP):
                act.activation(lat_hi[:, :, c * 512:(c + 1) * 512], lat_t[:, :, c * 512:(c + 1) * 512],
                               ACT.Copy).then_inc(lat_hi_ready, 1)
                if c == 0:
                    act.wait_ge(wv_in, 16)
                    act.activation(wv[0][:], wv_raw[:], ACT.Copy).then_inc(wv_hi_ready, 1)
            for c in range(NGRP):
                act.wait_ge(kr_turned, c + 1)
                for e in range(2):
                    last = act.activation(kk[e][0][NOPE:QK, c * 512:(c + 1) * 512], (ps_s if c < 2 else ps_p)[0:ROPE, c % 2, :],
                                          ACT.Copy)
                last.then_inc(kr_hi_ready, 1)
            for n in range(NB):
                act.wait_ge(v_done, n + 1)
                act.activation(v[:, n, :, 0:VD], ps_o[:, n % 2, :].rearrange("p (h d) -> p h d", h=H),
                               ACT.Copy).then_inc(v_kept, 1)
            for c in range(NGRP):
                prepare(0, 0, c)
            weights_high(1)
            for I in range(LASTG):
                keep_max(0, 0, I)
            peeled(act, HP, lambda i: [body(2 * i + e, e) for e in range(2)])

        @block.gpsimd
        def _(pool):
            def weights_low(g):
                pool.wait_ge(wq_hi_ready, g + 1)
                pool.tensor_tensor(wq[1][:], wq_raw[:], wq[0][:].bitcast(F32), ALU.subtract)
                pool.tensor_tensor(wk[1][:, 0:NOPE], wk_raw[:], wk[0][:, 0:NOPE].bitcast(F32),
                                   ALU.subtract).then_inc(wq_ready, 1)

            def q_low(g, slot, c):
                cols = slice(c * 512, (c + 1) * 512)
                pool.wait_ge(q_hi_ready, NGRP * g + c + 1)
                pool.tensor_tensor(q[slot][1][0:QK, cols], q32[0:QK, c % 2, :], q[slot][0][0:QK, cols].bitcast(F32),
                                   ALU.subtract).then_inc(q_lo_ready, 1)

            def body(h, e):
                if exists(h + 1, H):
                    for c in range(NGRP):
                        q_low(h + 1, 1 - e, c)
                    if exists(h + 2, H):
                        weights_low(h + 2)
            for part in wk:
                pool.memset(part[:, NOPE:P].bitcast(F32), 0.0)
            pool.memset(v[:, :, :, VD:VW], 1.0).then_inc(filled, 1)
            weights_low(0)
            pool.wait_ge(wv_hi_ready, 1)
            pool.tensor_tensor(wv[1][:], wv_raw[:], wv[0][:].bitcast(F32), ALU.subtract).then_inc(wv_ready, 1)
            for c in range(NGRP):
                q_low(0, 0, c)
            weights_low(1)
            peeled(pool, HP, lambda i: [body(2 * i + e, e) for e in range(2)])

        @block.vector
        def _(dve):
            def prepare(g, slot, c):
                cols = slice(c * 512, (c + 1) * 512)
                dve.wait_ge(q_done, NGRP * g + c + 1)
                if exists(NGRP * g + c - 2, NGRP * H):
                    dve.wait_ge(q_lo_ready, NGRP * g + c - 1)
                if exists(NGRP * g + c - 1, NGRP * H):
                    dve.wait_ge(q32_ready, NGRP * g + c)
                dve.tensor_tensor(rot[NOPE:QK, :], ps_q[QK:P, :], rope[QK:P, cols], ALU.mult)
                dve.tensor_tensor(q32[0:QK, c % 2, :], ps_q[0:QK, :], rope[0:QK, cols], ALU.mult).then_inc(q_read, 1)
                dve.wait_ge(q_read, NGRP * g + c + 1)
                dve.tensor_tensor(q32[NOPE:QK, c % 2, :], q32[NOPE:QK, c % 2, :], rot[NOPE:QK, :], ALU.add).then_inc(q32_ready, 1)
                dve.wait_ge(k_hi_ready, NGRP * g + c + 1)
                dve.tensor_tensor(kk[slot][1][0:NOPE, cols], ps_k[0:NOPE, :], kk[slot][0][0:NOPE, cols].bitcast(F32),
                                  ALU.subtract).then_inc(k_kept, 1)

            def maxima(g, n):
                I, r, c = chunks[n]
                width = 512 if c < I else (r + 1) * P
                if r == 0 and c == 0 and exists(NGRP * g + I - 2, NGRP * H):
                    dve.wait_ge(negm_ready, NGRP * g + I - 1)
                dve.wait_ge(chunk_done, NCH * g + n + 1)
                dve.tensor_reduce(mx[:, I % 2, r, c:c + 1], ps_p[:, n % 2, 0:width], AX.X, ALU.max).then_inc(chunk_read, 1)
                if r == GRP - 1 and c == I:
                    dve.wait_ge(chunk_read, NCH * g + n + 1)
                    if exists(NGRP * g + I - 2, NGRP * H):
                        dve.wait_ge(m_turned, NGRP * g + I - 1)
                    dve.tensor_reduce(negm[:, I % 2, :], mx[:, I % 2, :, 0:I + 1], AX.X, ALU.max,
                                      negate=True).then_inc(negm_ready, 1)

            def finish(h, I, k):
                dve.wait_ge(pv_done, NT * h + k + 1)
                sums = ps_o[:, I % 2, 0:GRP * VW].rearrange("p (r c) -> p r c", r=GRP)
                dve.reciprocal(rec[:, I % 2, :].unsqueeze(2), sums[:, :, VD:VW]).then_inc(rec_ready, 1)
                dve.wait_ge(rec_ready, NGRP * h + I + 1)
                if exists(NGRP * h + I - 2, NGRP * H):
                    dve.wait_ge(att_out[I % 2], 16 * (2 * h + I // 2))
                dve.tensor_tensor(att[:, I % 2], sums[:, :, 0:VD], rec[:, I % 2, :].unsqueeze(2).broadcast_to([P, GRP, VD]),
                                  ALU.mult).then_inc(att_ready, 1)

            def body(h, e):
                for k in range(NT):
                    if exists(h + 1, H):
                        for what, n in side[k]:
                            if what == "prepare":
                                prepare(h + 1, 1 - e, n)
                            elif what == "maxima":
                                maxima(h + 1, n)
                    if k == 0 and exists(h - 1, H):
                        finish(h - 1, LASTG, NT - 1)
                    elif k and (k == NT or tiles[k][0] != tiles[k - 1][0]):
                        finish(h, tiles[k - 1][0], k - 1)
            for e in range(2):
                last = dve.memset(kk[e][0][QK:QK + 1, :].bitcast(F32), 1.0)
            last.then_inc(filled, 1)
            for c in range(NGRP):
                dve.wait_ge(lat_hi_ready, c + 1)
                dve.tensor_tensor(lat_lo[:, :, c * 512:(c + 1) * 512], lat_t[:, :, c * 512:(c + 1) * 512],
                                  lat_hi[:, :, c * 512:(c + 1) * 512].bitcast(F32), ALU.subtract).then_inc(lat_lo_ready, 1)
            for c in range(NGRP):
                dve.wait_ge(kr_hi_ready, c + 1)
                for e in range(2):
                    cols = slice(c * 512, (c + 1) * 512)
                    last = dve.tensor_tensor(kk[e][1][NOPE:QK, cols], (ps_s if c < 2 else ps_p)[0:ROPE, c % 2, :],
                                             kk[e][0][NOPE:QK, cols].bitcast(F32), ALU.subtract)
                last.then_inc(kr_kept, 1)
            dve.wait_ge(rope_in, 16)
            for c in range(NGRP):
                prepare(0, 0, c)
            for n in range(NCH):
                maxima(0, n)
            peeled(dve, HP, lambda i: [body(2 * i + e, e) for e in range(2)])
            finish(H - 1, LASTG, NT - 1)

        @block.tensor
        def _(pe):
            def prepare(g, slot, c):
                cols = slice(c * 512, (c + 1) * 512)
                pe.wait_ge(wq_ready, g + 1)
                if exists(NGRP * g + c - 1, NGRP * H):
                    pe.wait_ge(q_read, NGRP * g + c)
                for j in range(QC):
                    last = mm3(pe, ps_q[:], [wq[0][:, j, :], wq[1][:, j, :]], [lat_hi[:, j, cols], lat_lo[:, j, cols]],
                               j == 0, j == QC - 1)
                last.then_inc(q_done, 1)
                if exists(NGRP * g + c - 1, NGRP * H):
                    pe.wait_ge(k_kept, NGRP * g + c)
                if exists(g - 1, H):
                    pe.wait_ge(m_kept, NGRP * g)
                mm3(pe, ps_k[:], [wk[0][:], wk[1][:]], [lat_hi[:, QC, cols], lat_lo[:, QC, cols]],
                    True, True).then_inc(k_done, 1)

            def maxima(g, slot, n):
                I, r, c = chunks[n]
                width = 512 if c < I else (r + 1) * P
                at = (GRP * I + r) * P
                if r == 0 and c == 0:
                    pe.wait_ge(q_hi_ready, NGRP * g + I + 1)
                    pe.wait_ge(k_hi_ready, NGRP * g + I + 1)
                if exists(NCH * g + n - 2, NCH * H):
                    pe.wait_ge(chunk_read, NCH * g + n - 1)
                last = pe.matmul(ps_p[:, n % 2, 0:width], q[slot][0][0:QK, at:at + P],
                                 kk[slot][0][0:QK, c * 512:c * 512 + width], start=True, stop=(c < I))
                if c == I:
                    last = pe.matmul(ps_p[:, n % 2, width - P:width], identb[:], mask_q[:], start=False, stop=True)
                last.then_inc(chunk_done, 1)

            def turn(g, I):
                pe.wait_ge(negm_ready, NGRP * g + I + 1)
                pe.wait_ge(k_kept, NGRP * g + NGRP)
                if exists(NGRP * g + I - 1, NGRP * H):
                    pe.wait_ge(m_kept, NGRP * g + I)
                for r in range(GRP):
                    last = pe.transpose(ps_k[0:1, r * P:(r + 1) * P], negm[:, I % 2, r:r + 1], ident[:])
                last.then_inc(m_turned, 1)

            def scores(h, slot, k):
                I, j = tiles[k]
                c0, n = tile_cols(k)
                cols = slice(I * 512 + c0, (I + 1) * 512)
                keys = slice(j * P, (j + 1) * P)
                out = ps_s[:, k % 2, 0:n]
                if j == 0:
                    pe.wait_ge(m_kept, NGRP * h + I + 1)
                    if I == 0:
                        pe.wait_ge(q_lo_ready, NGRP * h + NGRP)
                if exists(NT * h + k - 2, NT * H):
                    pe.wait_ge(exp_done, NT * h + k - 1)
                pe.matmul(out, kk[slot][0][0:QK + 1, keys], q[slot][0][0:QK + 1, cols], start=True, stop=False)
                pe.matmul(out, kk[slot][0][0:QK, keys], q[slot][1][0:QK, cols], start=False, stop=False)
                last = pe.matmul(out, kk[slot][1][0:QK, keys], q[slot][0][0:QK, cols], start=False, stop=(j < GRP * I))
                if j >= GRP * I:
                    last = pe.matmul(ps_s[:, k % 2, 0:P], identb[:], mask_k[:], start=False, stop=True)
                last.then_inc(scores_done, 1)

            def values(h, k):
                I, j = tiles[k]
                c0, _ = tile_cols(k)
                pe.wait_ge(exp_done, NT * h + k + 1)
                if j == 0 and exists(NGRP * h + I - 2, NGRP * H):
                    pe.wait_ge(att_ready, NGRP * h + I - 1)
                for r in range(c0 // P, GRP):
                    last = pe.matmul(ps_o[:, I % 2, r * VW:(r + 1) * VW], pt[:, k % 4, r * P - c0:(r + 1) * P - c0],
                                     v[:, j, ds(h, 1), :].squeeze(1), start=(j == 0 and r == 0), stop=(j == GRP * I + r),
                                     skip_group_check=True)
                last.then_inc(pv_done, 1)

            def body(h, e):
                for k in range(NT):
                    scores(h, e, k)
                    if k == 1:
                        turn(h, LASTG)
                    if exists(h + 1, H):
                        for what, n in side[k]:
                            if what == "prepare":
                                prepare(h + 1, 1 - e, n)
                            elif what == "maxima":
                                maxima(h + 1, 1 - e, n)
                            else:
                                turn(h + 1, n)
                    if k:
                        values(h, k - 1)
                    elif exists(h - 1, H):
                        values(h - 1, NT - 1)
            pe.wait_ge(kr_in, 16)
            for n in range(NB):
                c = n // GRP
                last = pe.transpose((ps_s if c < 2 else ps_p)[0:ROPE, c % 2, (n % GRP) * P:(n % GRP + 1) * P], kr[:, n, :], ident[:])
                if n % GRP == GRP - 1:
                    last.then_inc(kr_turned, 1)
            pe.wait_ge(wv_ready, 1)
            pe.wait_ge(filled, 2)
            for n in range(NB):
                if n % GRP == 0:
                    pe.wait_ge(lat_lo_ready, n // GRP + 1)
                if n >= 2:
                    pe.wait_ge(v_kept, n - 1)
                cols = slice(n * P, (n + 1) * P)
                mm3(pe, ps_o[:, n % 2, :], [lat_hi[:, QC, cols], lat_lo[:, QC, cols]], [wv[0][:], wv[1][:]],
                    True, True).then_inc(v_done, 1)
            for c in range(NGRP):
                prepare(0, 0, c)
            pe.wait_ge(kr_kept, NGRP)
            for n in range(NCH):
                maxima(0, 0, n)
                if n + 1 < NCH and chunks[n + 1][0] != chunks[n][0]:
                    turn(0, chunks[n][0])
            pe.wait_ge(v_kept, NB)
            peeled(pe, HP, lambda i: [body(2 * i + e, e) for e in range(2)])
            values(H - 1, NT - 1)

    at_out = Map(nc, after_lat)
    wo = [at_out("wo_hi", [P, KC, D], F32R), at_out("wo_lo", [P, KC, D], F32R)]
    ms = [at_out("ms_hi", [P, KC, P], F32R), at_out("ms_lo", [P, KC, P], F32R)]
    with ExitStack() as ctx:
        sems = []
        ctx.callback(release, nc, sems)

        def psum(name, shape):
            return ctx.enter_context(nc.psum_tensor("smp_" + name, shape, F32))

        def sem(name):
            return stage_semaphore(nc, sems, "smp_" + name)

        QT = TPP // GRP
        m = Map(nc, at_out.at)
        ck = [m(f"ck{e}", [P, TPP, KVL], F32) for e in range(2)]
        cr = [m(f"cr{e}", [P, TPP, ROPE], F32) for e in range(2)]
        wo_raw = m("wo_raw", [P, D], F32)
        ckt = m("ckt", [P, 2, 512], F32)
        state = m("state", [DB, PREV, DPOOL], F32)
        m2 = Map(nc, after_lat - 3 * S * 4)
        z = m2("s_z", [DB, DIN], F32)
        junk = m2("s_junk", [DB, OFF_KR], F32)
        lat = m2("s_lat", [DB, LA], F32)
        rot = m2("s_rot", [DB, H, ROPE], F32)
        crt = m2("crt", [P, 512], F32)
        pr = [m2(f"pr{e}", [P, TPP + 1, H], F32) for e in range(2)]
        mixed = m2("s_mixed", [DB, D], F32)
        wsum = m2("s_wsum", [DB, DPOOL], F32)
        assert m2.at <= after_lat
        wuq_s = m("s_wuq", [P, QC, H * QK], F32)
        wuk_s = m("s_wuk", [P, H * NOPE], F32)
        wuv_s = m("s_wuv", [P, DATT], F32)
        wp_s = m("s_wpool", [P, NG, P], F32)
        rows = m("s_rows", [DB, 2, DPOOL], F32)
        qn_w = m("s_qn_w", [DB, QL + KVL], F32)
        tab = m("s_tab", [DB, 2, ROPE], F32)
        stat = m("s_stat", [DB, 2], F32)
        lat_c = m("s_lat_c", [P, 3, DB], F32)
        krt = m("s_krt", [ROPE, DB], F32)
        qrow = m("s_q", [DB, H, QK], F32)
        qn_c = m("s_qn_c", [NOPE, H, DB], F32)
        wuk_t = m("s_wuk_t", [NOPE, H, P], F32)
        qabs = m("s_qabs", [P, DB, H], F32)
        qr = m("s_qr", [P, DB, GRP, H], F32)
        new_row = m("s_new_row", [1, DB, H], F32)
        new_col = m("s_new_col", [H, DB], F32)
        crow = m("s_crow", [1, 2, KVL], F32)
        page_i = m("s_page_i", [DB, NPG], I32)
        page_f = m("s_page_f", [DB, NPG], F32)
        page_c = m("s_page_c", [NPG, DB], F32)
        spread = m("s_spread", [NPG, P], F32)
        page_x = m("s_page_x", [P, DB], U32)
        quarter = m("s_quarter", [P, 1], F32)
        mx8 = m("s_mx8", [P, 2, H], F32)
        negm = m("s_negm", [H, 2], F32)
        diag = m("s_diag", [H, 2, H], F32)
        negb = m("s_negb", [P, 2, H], F32)
        dsum = m("s_dsum", [P, 2, H], F32)
        rec = m("s_rec", [P, 2, H], F32)
        olat = m("s_olat", [P, H, DB], F32)
        pool_c = m("s_pool_c", [P, NG, DB], F32)
        ps_t = psum("ps_t", [P, 2, 512])
        ps_r = psum("ps_r", [P, 512])
        ps_s = psum("ps_s", [P, 2, 512])
        ps_m = psum("ps_m", [P, 512])
        ps_o = psum("ps_o", [P, 512])
        ps_a = psum("ps_a", [P, 512])

        z_in, tab_in, w_in2, state_in, page_in, wo_in, crow_in = (
            sem("z_in"), sem("tab_in"), sem("w_in"), sem("state_in"), sem("page_in"), sem("wo_in"), [sem("crow0"), sem("crow1")])
        page_turned = sem("page_turned")
        cache_in = [sem("cache_in0"), sem("cache_in1")]
        page_step, page_ready, ss_ready, var_ready, sd_ready, rot_step, lat_ready, kr_ready, silu_ready = (
            sem("page_step"), sem("page_ready"), sem("ss_ready"), sem("var_ready"), sem("sd_ready"), sem("rot_step"),
            sem("lat_ready"), sem("kr_ready"), sem("silu_ready"))
        setup_pe, setup_dve, out_done, zeroed = sem("setup_pe"), sem("setup_dve"), sem("out_done"), sem("zeroed")
        wo_hi_ready, wo_lo_ready = sem("wo_hi_ready"), sem("wo_lo_ready")
        t_kept = [sem("t_kept0"), sem("t_kept1")]
        t_turned, r_turned, r_kept, s_done, mx_ready, mx_turned, negm_ready, diag_ready, negb_done, negb_ready = (
            sem("t_turned"), sem("r_turned"), sem("r_kept"), sem("s_done"), sem("mx_ready"), sem("mx_turned"),
            sem("negm_ready"), sem("diag_ready"), sem("negb_done"), sem("negb_ready"))
        shifted, exp_ready, dsum_ready, pv_done, rec_ready, olat_ready = (
            sem("shifted"), sem("exp_ready"), sem("dsum_ready"), sem("pv_done"), sem("rec_ready"), sem("olat_ready"))
        fin_pe, fin_dve = sem("fin_pe"), sem("fin_dve")
        HP = DB // 2
        ckv_q = t["cache_ckv"].rearrange("a n (c s) k -> (a n c) (s k)", c=QTR)
        kr_q = t["cache_krope"].rearrange("a n (c s) k -> (a n c) (s k)", c=QTR)
        ckv_new = o[5].rearrange("a b s k -> (a s) b k")
        w_out = t["w_out"].rearrange("a (c p) n -> p (a c) n", p=P)
        NQ = t["cache_ckv"].shape[1] * QTR
        block = ctx.enter_context(nc.Block())

        @block.sync
        def _(sp):
            sp.dma_start(z[:], zs_d).then_inc(z_in, 16)
            sp.dma_start(page_i[:], t["page_table"]).then_inc(page_in, 16)
            sp.dma_start(spread[:], t["c_spread"]).then_inc(page_in, 16)
            sp.dma_start(quarter[:], t["c_quarter"]).then_inc(page_in, 16)
            sp.dma_start(qn_w[:, 0:QL], t["q_norm_w"].rearrange("a n -> (a n)").partition_broadcast(DB)).then_inc(tab_in, 16)
            sp.dma_start(qn_w[:, QL:], t["kv_norm_w"].rearrange("a n -> (a n)").partition_broadcast(DB)).then_inc(tab_in, 16)
            sp.dma_start(tab[:], t["c_rope_sample"].rearrange("t b r -> b t r")).then_inc(tab_in, 16)
            sp.dma_start(rows[:, 0, :], t["b_pool"].rearrange("a g c -> (a g c)").partition_broadcast(DB)).then_inc(tab_in, 16)
            sp.dma_start(rows[:, 1, :], t["pool_scale"].rearrange("a c -> (a c)").partition_broadcast(DB)).then_inc(tab_in, 16)
            sp.dma_start(wuq_s[:], t["w_uq"].rearrange("a (c p) h d -> p (a c) (h d)", p=P)).then_inc(w_in2, 16)
            sp.dma_start(wuk_s[:], t["w_uk"].rearrange("a k h d -> (a k) (h d)")).then_inc(w_in2, 16)
            sp.dma_start(wuv_s[:], t["w_uv"].rearrange("a k h d -> (a k) (h d)")).then_inc(w_in2, 16)
            sp.dma_start(wp_s[:], t["w_pool"].rearrange("a g c d -> c (a g) d")).then_inc(w_in2, 16)
            sp.dma_start(state[:], t["state_pool"].rearrange("a b s c -> (a b) s c")).then_inc(state_in, 16)
            sp.wait_ge(lat_ready, 1)
            sp.dma_start(o[5].rearrange("a b s k -> (a b s) k"), lat[:, OFF_KV:OFF_KR]).then_inc(out_done, 16)
            sp.dma_start(o[6].rearrange("a b s k -> (a b s) k"), lat[:, OFF_KR:LA]).then_inc(out_done, 16)
            sp.wait_ge(out_done, 32)
            sp.wait_ge(state_in, 16)
            sp.dma_start(o[7].rearrange("a b s c -> (a b) s c")[:, 0:PREV - 1, :], state[:, 1:, :]).then_inc(out_done, 16)
            sp.dma_start(o[7].rearrange("a b s c -> (a b) s c")[:, PREV - 1:, :],
                         z[:, LA + OFF_U:LA + OFF_GP].unsqueeze(1)).then_inc(out_done, 16)

            def body(n, e):
                if exists(n - 1, DB):
                    sp.wait_ge(wo_lo_ready, n)
                sp.dma_start(wo_raw[:].unsqueeze(1), w_out[:, ds(n, 1), :]).then_inc(wo_in, 16)
                if exists(n - 2, DB):
                    sp.wait_ge(pv_done, n - 1)
                sp.dma_start(crow[:, e, :].unsqueeze(1), ckv_new[:, ds(n, 1), :]).then_inc(crow_in[e], 16)
            peeled(sp, HP, lambda i: [body(2 * i + e, e) for e in range(2)])
            sp.wait_ge(out_done, 64)

        @block.gpsimd
        def _(pool):
            def gather(n, e):
                pool.indirect_dma_start(ck[e][:].rearrange("p s k -> p (s k)"), None, ckv_q,
                                        bass.IndirectOffsetOnAxis(ap=page_x[:, n:n + 1], axis=0),
                                        bounds_check=NQ - 1, oob_is_err=True).then_inc(cache_in[e], 16)
                pool.indirect_dma_start(cr[e][:].rearrange("p s k -> p (s k)"), None, kr_q,
                                        bass.IndirectOffsetOnAxis(ap=page_x[:, n:n + 1], axis=0),
                                        bounds_check=NQ - 1, oob_is_err=True).then_inc(cache_in[e], 16)

            pool.wait_ge(page_ready, 1)
            gather(0, 0)
            gather(1, 1)
            pool.memset(qr[:], 0.0)
            for part in ms:
                last = pool.memset(part[:].bitcast(F32), 0.0)
            last.then_inc(zeroed, 1)
            for n in range(DB):
                pool.wait_ge(wo_hi_ready, n + 1)
                pool.tensor_tensor(wo[1][:, n, :], wo_raw[:], wo[0][:, n, :].bitcast(F32), ALU.subtract).then_inc(wo_lo_ready, 1)
                if n + 2 < DB:
                    pool.wait_ge(cache_in[n % 2], 16 * (n - n % 2) + 32)
                    pool.wait_ge(pv_done, n + 1)
                    gather(n + 2, n % 2)

        @block.scalar
        def _(act):
            act.wait_ge(z_in, 16)
            act.activation(junk[:, 0:QL], z[:, 0:QL], ACT.Square, accum_out=stat[:, 0:1])
            act.activation(junk[:, OFF_KV:OFF_KR], z[:, OFF_KV:OFF_KR], ACT.Square, accum_out=stat[:, 1:2]).then_inc(ss_ready, 1)
            act.wait_ge(var_ready, 1)
            act.activation(stat[:], stat[:], ACT.Sqrt).then_inc(sd_ready, 1)
            act.activation(z[:, LA:LA + DATT], z[:, LA:LA + DATT], ACT.Silu)
            act.activation(z[:, LA + OFF_GP:DIN], z[:, LA + OFF_GP:DIN], ACT.Silu).then_inc(silu_ready, 1)

            def body(n, e):
                act.wait_ge(wo_in, 16 * n + 16)
                act.activation(wo[0][:, ds(n, 1), :], wo_raw[:].unsqueeze(1), ACT.Copy).then_inc(wo_hi_ready, 1)
                for half in range(2):
                    act.wait_ge(r_turned, 2 * n + half + 1)
                    act.activation(crt[:], ps_r[:], ACT.Copy).then_inc(r_kept, 1)
                    for k in range(QT // 2):
                        if k % 2:
                            act.wait_ge(t_turned, QT * n + half * QT // 2 + k + 1)
                            act.activation(ckt[:, 1, :], ps_t[:, 1, :], ACT.Copy).then_inc(t_kept[1], 1)
                act.wait_ge(shifted, n + 1)
                act.activation(pr[e][:, 0:TPP, :], pr[e][:, 0:TPP, :], ACT.Exp, scale=SCALE)
                act.activation(pr[e][0:1, TPP, :], pr[e][0:1, TPP, :], ACT.Exp, scale=SCALE).then_inc(exp_ready, 1)
            peeled(act, HP, lambda i: [body(2 * i + e, e) for e in range(2)])

        @block.vector
        def _(dve):
            step = [0]

            def kept(ins):
                step[0] += 1
                ins.then_inc(setup_dve, 1)
                return step[0]

            dve.wait_ge(page_in, 48)
            dve.tensor_copy(page_f[:], page_i[:]).then_inc(page_step, 1)
            dve.wait_ge(page_turned, 1)
            dve.tensor_copy(page_c[:], ps_o[0:NPG, 0:DB]).then_inc(page_step, 1)
            dve.wait_ge(page_turned, 2)
            dve.tensor_scalar(page_x[:], ps_o[:, DB:2 * DB], quarter[:], None, ALU.add).then_inc(page_ready, 1)
            dve.wait_ge(ss_ready, 1)
            dve.tensor_scalar(stat[:, 0:1], stat[:, 0:1], 1.0 / QL, EPS, ALU.mult, ALU.add)
            dve.tensor_scalar(stat[:, 1:2], stat[:, 1:2], 1.0 / KVL, EPS, ALU.mult, ALU.add).then_inc(var_ready, 1)
            dve.wait_ge(tab_in, 80)
            dve.tensor_tensor(lat[:, OFF_KR:LA], z[:, OFF_KR:LA], tab[:, 0, :], ALU.mult)
            dve.tensor_tensor(rot[:, 0, 0:16], z[:, OFF_KR + 16:LA], tab[:, 1, 0:16], ALU.mult)
            dve.tensor_tensor(rot[:, 0, 16:32], z[:, OFF_KR:OFF_KR + 16], tab[:, 1, 16:32], ALU.mult).then_inc(rot_step, 1)
            dve.wait_ge(rot_step, 1)
            dve.tensor_tensor(lat[:, OFF_KR:LA], lat[:, OFF_KR:LA], rot[:, 0, :], ALU.add).then_inc(rot_step, 1)
            dve.wait_ge(sd_ready, 1)
            dve.reciprocal(stat[:], stat[:]).then_inc(kr_ready, 1)
            dve.wait_ge(kr_ready, 1)
            dve.scalar_tensor_tensor(out=lat[:, 0:QL], in0=z[:, 0:QL], scalar=stat[:, 0:1], in1=qn_w[:, 0:QL],
                                     op0=ALU.mult, op1=ALU.mult)
            dve.scalar_tensor_tensor(out=lat[:, OFF_KV:OFF_KR], in0=z[:, OFF_KV:OFF_KR], scalar=stat[:, 1:2], in1=qn_w[:, QL:],
                                     op0=ALU.mult, op1=ALU.mult).then_inc(lat_ready, 1)
            dve.wait_ge(setup_pe, 1)
            dve.tensor_copy(lat_c[:], ps_m[:, 0:3 * DB].rearrange("p (c b) -> p c b", c=3))
            kept(dve.tensor_copy(krt[:], ps_m[0:ROPE, 3 * DB:4 * DB]))
            dve.wait_ge(setup_pe, 2)
            kept(dve.tensor_copy(qrow[:].rearrange("b h d -> b (h d)").rearrange("b (k n) -> b k n", k=2),
                                 ps_s[0:DB, :, 0:H * QK // 2]))
            dve.wait_ge(setup_dve, 2)
            dve.tensor_tensor(rot[:, :, 0:16], qrow[:, :, NOPE + 16:QK],
                              tab[:, 1, 0:16].unsqueeze(1).broadcast_to([DB, H, 16]), ALU.mult)
            kept(dve.tensor_tensor(rot[:, :, 16:32], qrow[:, :, NOPE:NOPE + 16],
                                   tab[:, 1, 16:32].unsqueeze(1).broadcast_to([DB, H, 16]), ALU.mult))
            dve.wait_ge(setup_dve, 3)
            kept(dve.tensor_tensor(qrow[:, :, NOPE:QK], qrow[:, :, NOPE:QK],
                                   tab[:, 0, :].unsqueeze(1).broadcast_to([DB, H, ROPE]), ALU.mult))
            dve.wait_ge(setup_dve, 4)
            kept(dve.tensor_tensor(qrow[:, :, NOPE:QK], qrow[:, :, NOPE:QK], rot[:], ALU.add))
            dve.wait_ge(setup_pe, 3)
            kept(dve.tensor_copy(wuk_t[:].rearrange("p h k -> p (h k)").rearrange("p (a n) -> p a n", a=2), ps_t[0:NOPE]))
            dve.wait_ge(setup_pe, 4)
            dve.tensor_copy(qn_c[:], ps_o[0:NOPE, 0:H * DB].rearrange("p (h b) -> p h b", h=H))
            dve.wait_ge(zeroed, 1)
            for g in range(GRP):
                last = dve.tensor_copy(qr[g * ROPE:(g + 1) * ROPE, :, g, :],
                                       ps_o[0:ROPE, H * DB:2 * H * DB].rearrange("p (h b) -> p b h", h=H))
            kept(last)
            dve.wait_ge(setup_pe, 5)
            kept(dve.tensor_copy(qabs[:], ps_m[:, 0:H * DB].rearrange("p (h b) -> p b h", h=H)))
            dve.wait_ge(setup_pe, 6)
            dve.tensor_copy(new_row[:], ps_a[0:1, 0:DB * H].rearrange("p (b h) -> p b h", b=DB))
            kept(dve.tensor_copy(new_col[:], ps_r[0:H, 0:DB]))

            def normalised(n, e):
                dve.wait_ge(pv_done, n + 1)
                dve.reciprocal(rec[:, e, :], ps_o[:, H:2 * H]).then_inc(rec_ready, 1)
                dve.wait_ge(rec_ready, n + 1)
                dve.tensor_tensor(olat[:, :, ds(n, 1)], ps_o[:, 0:H].unsqueeze(2), rec[:, e, :].unsqueeze(2),
                                  ALU.mult).then_inc(olat_ready, 1)

            def body(n, e):
                for half in range(2):
                    for k in range(0, QT // 2, 2):
                        dve.wait_ge(t_turned, QT * n + half * QT // 2 + k + 1)
                        dve.tensor_copy(ckt[:, 0, :], ps_t[:, 0, :]).then_inc(t_kept[0], 1)
                dve.wait_ge(s_done, n + 1)
                dve.tensor_reduce(mx8[:, e, :], ps_s[:, e, 0:TPP * H].rearrange("p (t h) -> p h t", h=H),
                                  AX.X, ALU.max).then_inc(mx_ready, 1)
                dve.wait_ge(mx_turned, n + 1)
                dve.tensor_reduce(negm[:, e:e + 1], ps_m[0:H, 0:P], AX.X, ALU.max).then_inc(negm_ready, 1)
                dve.wait_ge(negm_ready, 2 * n + 1)
                dve.tensor_tensor(negm[:, e:e + 1], negm[:, e:e + 1], new_col[:, ds(n, 1)], ALU.max).then_inc(negm_ready, 1)
                dve.wait_ge(negm_ready, 2 * n + 2)
                dve.tensor_scalar(diag[:, e, :], ident[0:H, 0:H], negm[:, e:e + 1], -1.0, ALU.mult, ALU.mult).then_inc(diag_ready, 1)
                if exists(n - 1, DB):
                    normalised(n - 1, 1 - e)
                dve.wait_ge(negb_done, n + 1)
                dve.tensor_copy(negb[:, e, :], ps_m[:, P:P + H]).then_inc(negb_ready, 1)
                dve.wait_ge(negb_ready, n + 1)
                if exists(n - 2, DB):
                    dve.wait_ge(pv_done, n - 1)
                dve.tensor_tensor(pr[e][:, 0:TPP, :], ps_s[:, e, 0:TPP * H].rearrange("p (t h) -> p t h", h=H),
                                  negb[:, e, :].unsqueeze(1).broadcast_to([P, TPP, H]), ALU.add)
                dve.tensor_tensor(pr[e][0:1, TPP:TPP + 1, :], new_row[:, ds(n, 1), :], negb[0:1, e, :].unsqueeze(1),
                                  ALU.add).then_inc(shifted, 1)
                dve.wait_ge(exp_ready, n + 1)
                dve.tensor_reduce(dsum[:, e, :], pr[e][:, 0:TPP, :].rearrange("p t h -> p h t"), AX.X, ALU.add).then_inc(dsum_ready, 1)
            dve.wait_ge(state_in, 16)
            u = z[:, LA + OFF_U:LA + OFF_GP]
            for g in range(NG):
                w = 2 << g
                cols = slice(g * P, (g + 1) * P)
                last = dve.tensor_reduce(wsum[:, cols], state[:, PREV + 1 - w:, cols].rearrange("b s c -> b c s"), AX.X, ALU.add)
            kept(last)
            dve.wait_ge(setup_dve, 10)
            kept(dve.tensor_tensor(wsum[:], wsum[:], u, ALU.add))
            dve.wait_ge(setup_dve, 11)
            for g in range(NG):
                cols = slice(g * P, (g + 1) * P)
                last = dve.scalar_tensor_tensor(out=wsum[:, cols], in0=wsum[:, cols], scalar=1.0 / (2 << g), in1=u[:, cols],
                                                op0=ALU.mult, op1=ALU.subtract)
            kept(last)
            dve.wait_ge(setup_pe, 7)
            kept(dve.tensor_copy(pool_c[:], ps_a[:, 0:NG * DB].rearrange("p (g b) -> p g b", g=NG)))
            dve.wait_ge(setup_pe, 8)
            kept(dve.tensor_tensor(mixed[:, DATT:], ps_a[0:DB, :], rows[:, 0, :], ALU.add))
            dve.wait_ge(setup_dve, 14)
            kept(dve.tensor_tensor(mixed[:, DATT:], mixed[:, DATT:], rows[:, 1, :], ALU.mult))
            dve.wait_ge(setup_dve, 15)
            dve.wait_ge(silu_ready, 1)
            kept(dve.tensor_tensor(mixed[:, DATT:], mixed[:, DATT:], z[:, LA + OFF_GP:DIN], ALU.mult))
            peeled(dve, HP, lambda i: [body(2 * i + e, e) for e in range(2)])
            normalised(DB - 1, 1)
            dve.wait_ge(fin_pe, 1)
            dve.tensor_tensor(mixed[:, 0:DATT], ps_a[0:DB, :], z[:, LA:LA + DATT], ALU.mult).then_inc(fin_dve, 1)
            dve.wait_ge(fin_pe, 2)
            turned = ps_m[:, 0:KC * DB].rearrange("p (c b) -> p c b", c=KC)
            dve.tensor_copy(ms[0][:, :, 0:DB], turned).then_inc(fin_dve, 1)
            dve.wait_ge(fin_dve, 2)
            dve.tensor_tensor(ms[1][:, :, 0:DB], turned, ms[0][:, :, 0:DB].bitcast(F32), ALU.subtract).then_inc(fin_dve, 1)

        @block.tensor
        def _(pe):
            pe.wait_ge(page_step, 1)
            pe.transpose(ps_o[0:NPG, 0:DB], page_f[:], ident[0:DB, 0:DB]).then_inc(page_turned, 1)
            pe.wait_ge(page_step, 2)
            pe.matmul(ps_o[:, DB:2 * DB], spread[:], page_c[:], start=True, stop=True).then_inc(page_turned, 1)
            pe.wait_ge(lat_ready, 1)
            for c in range(3):
                pe.transpose(ps_m[:, c * DB:(c + 1) * DB], lat[:, c * P:(c + 1) * P], ident[0:DB, 0:DB])
            pe.transpose(ps_m[0:ROPE, 3 * DB:4 * DB], lat[:, OFF_KR:LA], ident[0:DB, 0:DB]).then_inc(setup_pe, 1)
            pe.wait_ge(w_in2, 64)
            pe.wait_ge(setup_dve, 1)
            for k in range(2):
                for c in range(QC):
                    last = pe.matmul(ps_s[0:DB, k, 0:H * QK // 2], lat_c[:, c, :],
                                     wuq_s[:, c, k * H * QK // 2:(k + 1) * H * QK // 2], start=(c == 0), stop=(c == QC - 1))
            last.then_inc(setup_pe, 1)
            for h in range(H):
                last = pe.transpose(ps_t[0:NOPE, h // 4, (h % 4) * P:(h % 4 + 1) * P], wuk_s[:, h * NOPE:(h + 1) * NOPE], ident[:])
            last.then_inc(setup_pe, 1)
            pe.wait_ge(setup_dve, 5)
            for h in range(H):
                pe.transpose(ps_o[0:NOPE, h * DB:(h + 1) * DB], qrow[:, h, 0:NOPE], ident[0:DB, 0:DB])
                last = pe.transpose(ps_o[0:ROPE, (H + h) * DB:(H + h + 1) * DB], qrow[:, h, NOPE:QK], ident[0:DB, 0:DB])
            last.then_inc(setup_pe, 1)
            pe.wait_ge(setup_dve, 7)
            for h in range(H):
                last = pe.matmul(ps_m[:, h * DB:(h + 1) * DB], wuk_t[:, h, :], qn_c[:, h, :], start=True, stop=True)
            last.then_inc(setup_pe, 1)
            pe.wait_ge(setup_dve, 8)
            for n in range(DB):
                pe.matmul(ps_a[0:1, n * H:(n + 1) * H], lat_c[:, QC, n:n + 1], qabs[:, n, :], start=True, stop=False)
                pe.matmul(ps_a[0:1, n * H:(n + 1) * H], krt[:, n:n + 1], qr[0:ROPE, n, 0, :], start=False, stop=True)
                pe.matmul(ps_r[0:H, n:n + 1], qabs[:, n, :], lat_c[:, QC, n:n + 1], start=True, stop=False)
                last = pe.matmul(ps_r[0:H, n:n + 1], qr[0:ROPE, n, 0, :], krt[:, n:n + 1], start=False, stop=True)
            last.then_inc(setup_pe, 1)
            pe.wait_ge(setup_dve, 12)
            for g in range(NG):
                last = pe.transpose(ps_a[:, g * DB:(g + 1) * DB], wsum[:, g * P:(g + 1) * P], ident[0:DB, 0:DB])
            last.then_inc(setup_pe, 1)
            pe.wait_ge(setup_dve, 13)
            for g in range(NG):
                last = pe.matmul(ps_a[0:DB, g * P:(g + 1) * P], pool_c[:, g, :], wp_s[:, g, :], start=True, stop=True)
            last.then_inc(setup_pe, 1)

            def product(n, e):
                pe.wait_ge(dsum_ready, n + 1)
                if exists(n - 1, DB):
                    pe.wait_ge(olat_ready, n)
                pe.wait_ge(crow_in[e], 8 * (n - e) + 16)
                for k in range(TPP):
                    pe.matmul(ps_o[:, 0:H], ck[e][:, k, :], pr[e][:, k, :], start=(k == 0), stop=False)
                pe.matmul(ps_o[:, 0:H], crow[:, e, :], pr[e][0:1, TPP, :], start=False, stop=True)
                pe.matmul(ps_o[:, H:2 * H], ones[:], dsum[:, e, :], start=True, stop=False)
                pe.matmul(ps_o[:, H:2 * H], ones[0:1, :], pr[e][0:1, TPP, :], start=False, stop=True).then_inc(pv_done, 1)

            def body(n, e):
                pe.wait_ge(cache_in[e], 16 * (n - e) + 32)
                for half in range(2):
                    G0 = half * QT // 2

                    def turn(k):
                        if k >= 2 or half or exists(n - 1, DB):
                            pe.wait_ge(t_kept[k % 2], (QT // 2) * n + (G0 + k) // 2)
                        for g in range(GRP):
                            last = pe.transpose(ps_t[:, k % 2, g * P:(g + 1) * P], ck[e][:, (G0 + k) * GRP + g, :], ident[:])
                        last.then_inc(t_turned, 1)
                    if half or exists(n - 1, DB):
                        pe.wait_ge(r_kept, 2 * n + half)
                    for k in range(QT // 2):
                        last = pe.transpose(ps_r[:, k * P:(k + 1) * P],
                                            cr[e][:, (G0 + k) * GRP:(G0 + k + 1) * GRP, :].rearrange("p g r -> p (g r)"), ident[:])
                    last.then_inc(r_turned, 1)
                    turn(0)
                    pe.wait_ge(r_kept, 2 * n + half + 1)
                    for k in range(QT // 2):
                        if k + 1 < QT // 2:
                            turn(k + 1)
                        at = (G0 + k) * GRP * H
                        pe.matmul(ps_s[:, e, at:at + GRP * H], crt[:, k * P:(k + 1) * P], qr[:, ds(n, 1), :, :].squeeze(1),
                                  start=True, stop=False, skip_group_check=True)
                        pe.wait_ge(t_kept[k % 2], (QT // 2) * n + (G0 + k) // 2 + 1)
                        for g in range(GRP):
                            last = pe.matmul(ps_s[:, e, at + g * H:at + (g + 1) * H], ckt[:, k % 2, g * P:(g + 1) * P],
                                             qabs[:, ds(n, 1), :].squeeze(1), start=False, stop=(g == GRP - 1),
                                             skip_group_check=True)
                last.then_inc(s_done, 1)
                if exists(n - 1, DB):
                    pe.wait_ge(negb_ready, n)
                pe.wait_ge(mx_ready, n + 1)
                pe.transpose(ps_m[0:H, 0:P], mx8[:, e, :], ident[:]).then_inc(mx_turned, 1)
                if exists(n - 1, DB):
                    product(n - 1, 1 - e)
                pe.wait_ge(diag_ready, n + 1)
                pe.matmul(ps_m[:, P:P + H], ones[0:H, :], diag[:, e, :], start=True, stop=True).then_inc(negb_done, 1)
            pe.wait_ge(setup_dve, 14)
            peeled(pe, HP, lambda i: [body(2 * i + e, e) for e in range(2)])
            product(DB - 1, 1)
            pe.wait_ge(olat_ready, DB)
            for h in range(H):
                last = pe.matmul(ps_a[0:DB, h * VD:(h + 1) * VD], olat[:, h, :], wuv_s[:, h * VD:(h + 1) * VD], start=True, stop=True)
            last.then_inc(fin_pe, 1)
            pe.wait_ge(fin_dve, 1)
            pe.wait_ge(setup_dve, 16)
            for c in range(KC):
                last = pe.transpose(ps_m[:, c * DB:(c + 1) * DB], mixed[:, c * P:(c + 1) * P], ident[0:DB, 0:DB])
            last.then_inc(fin_pe, 1)

    with ExitStack() as ctx:
        sems = []
        ctx.callback(release, nc, sems)

        def psum(name, shape):
            return ctx.enter_context(nc.psum_tensor("out_" + name, shape, F32))

        def sem(name):
            return stage_semaphore(nc, sems, "out_" + name)

        m = Map(nc, at_out.at)
        gate = m("gate", [P, D], F32)
        fn_w = m("fn_w", [P, D], F32)
        ar = [m(f"att_rows{b}", [P, DATT], F32) for b in range(2)]
        ga = [m(f"gate_rows{b}", [P, DATT], F32) for b in range(2)]
        pc = [m(f"pool_cols{b}", [P, NG, P], F32) for b in range(2)]
        xr = [m(f"x_rows{b}", [P, D], F32) for b in range(2)]
        mh = [m(f"mixed_hi{b}", [P, KC, P], F32R) for b in range(2)]
        ml = [m(f"mixed_lo{b}", [P, KC, P], F32R) for b in range(2)]
        y = [m(f"y{b}", [P, D], F32) for b in range(2)]
        junk = m("out_junk", [P, 2, D], F32)
        stat = m("out_stat", [P, 2], F32)
        xs = m("out_xs", [DB, D], F32)
        gs = m("out_gate_s", [DB, D], F32)
        ps_t = psum("ps_t", [P, 512])
        ps_y = [psum(f"ps_y{b}", [P, 2, 512]) for b in range(2)]
        tab_in, s_in = sem("tab_in"), sem("s_in")
        r_in = [sem("rows_in0"), sem("rows_in1")]
        x_in = [sem("x_in0"), sem("x_in1")]
        gated, turned, hi_ready, lo_att, lo_pool = sem("gated"), sem("turned"), sem("hi_ready"), sem("lo_att"), sem("lo_pool")
        y_done, y_read, y_sum, ss_ready, var_ready, sd_ready, r_ready, y_ready = (
            sem("y_done"), sem("y_read"), sem("y_sum"), sem("ss_ready"), sem("var_ready"), sem("sd_ready"), sem("r_ready"),
            sem("y_ready"))
        y_out = [sem("y_out0"), sem("y_out1")]
        att_blocks = att_d.rearrange("(n p) e -> p n e", p=P)
        pool_cols = pool_d.rearrange("g p s -> p g s")
        y_blocks = o[0].rearrange("a (n p) d -> p (a n) d", p=P)
        HB = NB // 2
        block = ctx.enter_context(nc.Block())

        @block.sync
        def _(sp):
            def load(n, b):
                sp.dma_start(ar[b][:].unsqueeze(1), att_blocks[:, ds(n, 1), :]).then_inc(r_in[b], 16)
                sp.dma_start(ga[b][:].unsqueeze(1), gate_att_blocks[:, ds(n, 1), :]).then_inc(r_in[b], 16)
                sp.dma_start(pc[b][:], pool_cols[:, :, ds(n * P, P)]).then_inc(r_in[b], 16)

            def load_x(n, b):
                sp.dma_start(xr[b][:].unsqueeze(1), x_blocks[:, ds(n, 1), :]).then_inc(x_in[b], 16)

            def body(i):
                for b in range(2):
                    n = 2 * i + b
                    if exists(n + 2, NB):
                        sp.wait_ge(lo_pool, n + 1)
                        sp.wait_ge(turned, n + 1)
                        load(n + 2, b)
                        sp.wait_ge(y_sum, 2 * n + 2)
                        load_x(n + 2, b)
            for b in range(2):
                load(b, b)
            sp.dma_start(gate[:], mod_d[DB, 2 * D:].partition_broadcast(P)).then_inc(tab_in, 16)
            sp.dma_start(fn_w[:], t["final_norm_w"].partition_broadcast(P)).then_inc(tab_in, 16)
            for b in range(2):
                load_x(b, b)
            sp.dma_start(xs[:], t["x_sample"].rearrange("b s d -> (b s) d")).then_inc(s_in, 16)
            sp.dma_start(gs[:], mod_d[0:DB, 2 * D:]).then_inc(s_in, 16)
            peeled(sp, HB, body)
            sp.wait_ge(y_ready, NB + 1)
            sp.dma_start(o[1].rearrange("b s d -> (b s) d"), y[0][0:DB, :]).then_inc(y_out[0], 16)
            sp.wait_ge(y_out[0], 16 * (HB + 1))
            sp.wait_ge(y_out[1], 16 * HB)

        @block.scalar
        def _(act):
            def high(n, b):
                act.wait_ge(turned, n + 1)
                if exists(n - 2, NB):
                    act.wait_ge(y_done, n - 1)
                act.activation(mh[b][:, 0:GRP, :], ps_t[:].rearrange("p (c s) -> p c s", c=GRP), ACT.Copy)
                act.activation(mh[b][:, GRP:, :], pc[b][:], ACT.Copy).then_inc(hi_ready, 1)

            def statistics(n, b, rows):
                act.wait_ge(y_sum, 2 * n + 2)
                act.activation(junk[0:rows, b, :], y[b][0:rows, :], ACT.Square, accum_out=stat[0:rows, b:b + 1]).then_inc(ss_ready, 1)
                act.wait_ge(var_ready, n + 1)
                act.activation(stat[0:rows, b:b + 1], stat[0:rows, b:b + 1], ACT.Sqrt).then_inc(sd_ready, 1)

            def store(n, b):
                act.wait_ge(y_ready, n + 1)
                act.dma_start(y_blocks[:, ds(n, 1), :], y[b][:].unsqueeze(1)).then_inc(y_out[b], 16)

            def body(i):
                for b in range(2):
                    n = 2 * i + b
                    if exists(n + 1, NB):
                        high(n + 1, 1 - b)
                    if exists(n - 1, NB):
                        store(n - 1, 1 - b)
                    statistics(n, b, P)
            high(0, 0)
            peeled(act, HB, body)
            store(NB - 1, 1)
            statistics(NB, 0, DB)

        @block.gpsimd
        def _(pool):
            def gated_rows(n, b):
                pool.wait_ge(r_in[b], 24 * (n - b) + 48)
                pool.tensor_tensor(ar[b][:], ar[b][:], ga[b][:], ALU.mult).then_inc(gated, 1)

            def low(n, b):
                pool.wait_ge(hi_ready, n + 1)
                pool.tensor_tensor(ml[b][:, GRP:, :], pc[b][:], mh[b][:, GRP:, :].bitcast(F32), ALU.subtract).then_inc(lo_pool, 1)

            def body(i):
                for b in range(2):
                    n = 2 * i + b
                    low(n, b)
                    if exists(n + 2, NB):
                        gated_rows(n + 2, b)
            for b in range(2):
                gated_rows(b, b)
            peeled(pool, HB, body)

        @block.vector
        def _(dve):
            def low(n, b):
                dve.wait_ge(hi_ready, n + 1)
                dve.tensor_tensor(ml[b][:, 0:GRP, :], ps_t[:].rearrange("p (c s) -> p c s", c=GRP),
                                  mh[b][:, 0:GRP, :].bitcast(F32), ALU.subtract).then_inc(lo_att, 1)

            def residual(n, b, rows, g_rows, x_rows):
                dve.wait_ge(y_done, n + 1)
                if exists(n - 2, NB):
                    dve.wait_ge(y_out[b], 8 * (n - b))
                dve.tensor_tensor(y[b][0:rows, :].rearrange("p (k c) -> p k c", k=2), ps_y[b][0:rows],
                                  g_rows.rearrange("p (k c) -> p k c", k=2), ALU.mult).then_inc(y_sum, 1)
                dve.wait_ge(y_sum, 2 * n + 1)
                dve.tensor_tensor(y[b][0:rows, :], y[b][0:rows, :], x_rows, ALU.add).then_inc(y_sum, 1)
                dve.wait_ge(ss_ready, n + 1)
                dve.tensor_scalar(stat[0:rows, b:b + 1], stat[0:rows, b:b + 1], 1.0 / D, EPS, ALU.mult, ALU.add).then_inc(var_ready, 1)
                dve.wait_ge(sd_ready, n + 1)
                dve.reciprocal(stat[0:rows, b:b + 1], stat[0:rows, b:b + 1]).then_inc(r_ready, 1)
                dve.wait_ge(r_ready, n + 1)
                dve.scalar_tensor_tensor(out=y[b][0:rows, :], in0=y[b][0:rows, :], scalar=stat[0:rows, b:b + 1], in1=fn_w[0:rows, :],
                                         op0=ALU.mult, op1=ALU.mult).then_inc(y_ready, 1)

            def body(i):
                for b in range(2):
                    n = 2 * i + b
                    if exists(n + 1, NB):
                        low(n + 1, 1 - b)
                    dve.wait_ge(x_in[b], 16 * i + 16)
                    residual(n, b, P, gate[:], xr[b][:])
            low(0, 0)
            dve.wait_ge(tab_in, 32)
            dve.wait_ge(s_in, 32)
            peeled(dve, HB, body)
            dve.wait_ge(y_out[0], 16 * HB)
            residual(NB, 0, DB, gs[:], xs[:])

        @block.tensor
        def _(pe):
            def turn(n, b):
                pe.wait_ge(gated, n + 1)
                if exists(n - 1, NB):
                    pe.wait_ge(lo_att, n)
                for c in range(GRP):
                    last = pe.transpose(ps_t[:, c * P:(c + 1) * P], ar[b][:, c * P:(c + 1) * P], ident[:])
                last.then_inc(turned, 1)

            def product(b, part):
                for c in range(KC):
                    for k in range(2):
                        cols = slice(k * 512, (k + 1) * 512)
                        last = mm3(pe, ps_y[b][:, k, :], [part[0][:, c, :], part[1][:, c, :]],
                                   [wo[0][:, c, cols], wo[1][:, c, cols]], c == 0, c == KC - 1)
                last.then_inc(y_done, 1)

            def body(i):
                for b in range(2):
                    n = 2 * i + b
                    if exists(n + 1, NB):
                        turn(n + 1, 1 - b)
                    pe.wait_ge(lo_att, n + 1)
                    pe.wait_ge(lo_pool, n + 1)
                    if exists(n - 2, NB):
                        pe.wait_ge(y_sum, 2 * n - 3)
                    product(b, [mh[b], ml[b]])
            turn(0, 0)
            peeled(pe, HB, body)
            pe.wait_ge(y_sum, 2 * NB - 3)
            product(0, ms)


_INS = ["x_prompt", "x_sample", "c_prompt", "c_sample", "cache_ckv", "cache_krope", "state_pool", "page_table",
        "ada_w", "ada_b", "norm_w", "w_in", "q_norm_w", "w_uq", "kv_norm_w", "w_uk", "w_uv",
        "w_pool", "b_pool", "pool_scale", "w_out", "final_norm_w"]
_OUTS = [(1, S, D), (DB, 1, D), (1, 1, S, KVL), (1, 1, S, ROPE), (1, 1, PREV, DPOOL),
         (1, DB, 1, KVL), (1, DB, 1, ROPE), (1, DB, PREV, DPOOL)]


def _constants():
    f32 = np.float32
    inv = (f32(10000.0) ** (-np.arange(0, ROPE, 2, dtype=f32) / f32(ROPE))).astype(f32)

    def tables(pos):
        ang = (pos.astype(f32)[:, None] * inv[None, :]).astype(f32).astype(np.float64)
        cos, sin = np.cos(ang).astype(f32), np.sin(ang).astype(f32)
        return np.concatenate([cos, cos], 1), np.concatenate([-sin, sin], 1)

    cos, sin = tables(np.arange(S))
    cos_s, sin_s = tables(np.full(DB, NPG * PG))
    tok = np.arange(P)
    late = np.where(tok[None, :] <= tok[:, None], 0.0, MASKED)
    windows = 2 ** (np.arange(NG) + 1)
    return {
        "c_ident": np.eye(P, dtype=f32),
        "c_mask_q": late.astype(f32),
        "c_mask_k": np.ascontiguousarray(late.T).astype(f32),
        "c_rope_rows": np.ascontiguousarray(np.stack([cos, sin]).reshape(2, NB, P, ROPE).transpose(0, 2, 1, 3)),
        "c_rope_cols": np.ascontiguousarray(np.concatenate([np.ones((NOPE, S), f32), cos.T, sin.T])),
        "c_rope_sample": np.stack([cos_s, sin_s]),
        "c_count": (1.0 / np.minimum(tok[None, :16] + 1.0, windows[:, None])).astype(f32),
        "c_spread": np.where(tok[None, :] // QTR == np.arange(NPG)[:, None], float(QTR), 0.0).astype(f32),
        "c_quarter": (tok % QTR).astype(f32)[:, None],
    }


def kernel(**inputs):
    import numpy as _np
    import concourse.bacc as _bacc
    from concourse import mybir as _mybir
    from concourse.bass_utils import run_bass_kernel_spmd as _run

    nc = _bacc.Bacc("TRN2", target_bir_lowering=False, num_devices=1)
    arrays, tensors = {}, {}
    data = {name: _np.ascontiguousarray(inputs[name]) for name in _INS}
    data.update(_constants())
    for name, a in data.items():
        arrays[f"in_{name}_dram"] = a
        tensors[name] = nc.dram_tensor(f"in_{name}_dram", a.shape, _mybir.dt.from_np(a.dtype), kind="ExternalInput").ap()
    outs = [nc.dram_tensor(f"out_{i}_dram", shape, _mybir.dt.float32, kind="ExternalOutput").ap()
            for i, shape in enumerate(_OUTS)]
    build(nc, tensors, outs)
    r = _run(nc, [arrays], core_ids=[0])
    return tuple(r.results[0][f"out_{i}_dram"] for i in range(len(_OUTS)))
```

```python
from contextlib import ExitStack

import numpy as np

import concourse.bass as bass
from concourse import mybir

F32 = mybir.dt.float32
F32R = mybir.dt.float32r
BF16 = mybir.dt.bfloat16
I32 = mybir.dt.int32
U32 = mybir.dt.uint32
ALU = mybir.AluOpType
ACT = mybir.ActivationFunctionType
AX = mybir.AxisListType

P = 128
D = 1024
KC = D // P
S = 2048
NB = S // P
DB = 8
NC = DB + 1
H = 8
NOPE, ROPE, VD = 64, 32, 64
QK = NOPE + ROPE
QL, KVL = 256, 128
QC = QL // P
DATT = H * VD
DPOOL = 512
NG = 4
PREV = 15
OFF_KV, OFF_KR, OFF_GA = QL, QL + KVL, QL + KVL + ROPE
DIN = OFF_GA + DATT + 2 * DPOOL
LA = OFF_GA
LB = DIN - OFF_GA
OFF_U, OFF_GP = DATT, DATT + DPOOL
EPS = 1e-6
SCALE = QK ** -0.5
NPG, PG = 32, 128
QTR = 4
TPP = PG // QTR
MASKED = -1e30
BASE = 16896
GRP = 4
NGRP = NB // GRP


class Map:

    def __init__(self, nc, start):
        self.nc, self.at = nc, start

    def __call__(self, name, shape, dt):
        size = {F32: 4, F32R: 4, BF16: 2, I32: 4, U32: 4}[dt]
        n = int(np.prod(shape[1:])) * size
        t = self.nc.alloc_sbuf_tensor_at(name, list(shape), dt, offset=self.at)
        self.at += (n + 31) // 32 * 32
        assert self.at <= 229344, (name, self.at)
        return t


def exists(n, count):
    return not isinstance(n, int) or 0 <= n < count


def stage_semaphore(nc, sems, name):
    sems.append(nc.alloc_semaphore(name))
    return sems[-1]


def release(nc, sems):
    nc.clear_and_free_semaphores(sems)
    nc.all_engine_barrier()


def peeled(eng, count, body, tail=1):
    body(0)
    with eng.Fori(1, count - tail) as i:
        body(i)
    for i in range(count - tail, count):
        body(i)


def mm3(pe, out, lhs, rhs, first, last):
    pe.matmul(out, lhs[0], rhs[0], start=first, stop=False)
    pe.matmul(out, lhs[0], rhs[1], start=False, stop=False)
    return pe.matmul(out, lhs[1], rhs[0], start=False, stop=last)


def build(nc, t, o):
    x_blocks = t["x_prompt"].rearrange("a (n p) d -> p (a n) d", p=P)
    ckv_out = o[2].rearrange("a b (n p) k -> p (a b n) k", p=P)
    kr_out = o[3].rearrange("a b (n p) k -> p (a b n) k", p=P)
    w_in = t["w_in"].rearrange("a (c p) n -> p (a c) n", p=P)

    mod_d = nc.dram_tensor("mod_scratch", (NC, 3 * D), F32, kind="Internal").ap()
    zs_d = nc.dram_tensor("sample_z_scratch", (DB, DIN), F32, kind="Internal").ap()
    gate_att_d = nc.dram_tensor("gate_att_scratch", (S, DATT), F32, kind="Internal").ap()
    pool_d = nc.dram_tensor("pool_scratch", (NG, P, S), F32, kind="Internal").ap()
    att_d = nc.dram_tensor("att_scratch", (S, DATT), F32, kind="Internal").ap()
    gate_att_blocks = gate_att_d.rearrange("(n p) e -> p n e", p=P)

    keep = Map(nc, BASE)
    ident = keep("ident", [P, P], F32)
    identb = keep("identb", [P, P], BF16)
    mask_q = keep("mask_q", [P, P], BF16)
    mask_k = keep("mask_k", [P, P], BF16)
    ones = keep("ones", [P, P], F32)
    rstd = keep("rstd", [P, NB + 1], F32)
    coef_a = keep("coef_a", [P, KC, NC], F32)
    coef_b = keep("coef_b", [P, KC, NC], F32)
    vec_t = keep("vec_t", [P, 16], F32)
    lat_t = keep("lat_t", [P, 3, S], F32)
    after_lat = keep.at
    hs = [keep("hs_hi", [P, KC, P], F32R), keep("hs_lo", [P, KC, P], F32R)]
    after_hs = keep.at

    m = Map(nc, after_hs)
    wa = [m("wa_hi", [P, KC, LA], F32R), m("wa_lo", [P, KC, LA], F32R)]
    after_wa = m.at
    with ExitStack() as ctx:
        sems = []
        ctx.callback(release, nc, sems)

        def psum(name, shape):
            return ctx.enter_context(nc.psum_tensor("mod_" + name, shape, F32))

        def sem(name):
            return stage_semaphore(nc, sems, "mod_" + name)

        NX = 3
        xt = m("mod_x", [P, NX, D], F32)
        xs = m("mod_xs", [DB, D], F32)
        wa_raw = m("wa_raw", [P, KC, LA], F32)
        c_sb = m("c_sb", [NC, D], F32)
        c_act = m("c_act", [P, KC, NC], F32)
        vecs = m("vecs", [16, P], F32)
        bias = m("ada_b_rows", [NC, 3 * D], F32)
        mod = m("mod_rows", [NC, 3 * D], F32)
        NA = 5
        ada = m("ada", [P, NA, 3 * D], F32)
        ss = m("x_ss", [P, NB + 1], F32)
        masks = m("masks_f32", [P, 2, P], F32)
        junk_s = m("junk_s", [DB, D], F32)
        hs32 = m("hs32", [P, KC, DB], F32)
        ps_mod = psum("ps_mod", [P, 6, 512])
        ps_c = psum("ps_c", [P, 512])
        ps_t = psum("ps_t", [P, 512])

        const_in, masks_in, c_in, small_in, xs_in = sem("const_in"), sem("masks_in"), sem("c_in"), sem("small_in"), sem("xs_in")
        ada_in = [sem(f"ada_in{k}") for k in range(NA)]
        x_in = [sem(f"x_in{k}") for k in range(NX)]
        wa_in = sem("wa_in")
        c_turned, c_ready, vec_turned, vec_ready = sem("c_turned"), sem("c_ready"), sem("vec_turned"), sem("vec_ready")
        ada_used, mod_summed, mod_ready, mod_turned = sem("ada_used"), sem("mod_summed"), sem("mod_ready"), sem("mod_turned")
        x_squared, ss_ready, ss_zero, var_ready, sd_ready, rstd_ready = (
            sem("x_squared"), sem("ss_ready"), sem("ss_zero"), sem("var_ready"), sem("sd_ready"), sem("rstd_ready"))
        wa_hi_ready, wa_lo_ready = sem("wa_hi_ready"), sem("wa_lo_ready")
        hs_zero, xs_scaled, xs_turned, hs_done, coef_ready, mod_out = (
            sem("hs_zero"), sem("xs_scaled"), sem("xs_turned"), sem("hs_done"), sem("coef_ready"), sem("mod_out"))

        ada_rows = t["ada_w"].rearrange("a (c p) n -> p (a c) n", p=P)
        block = ctx.enter_context(nc.Block())

        @block.sync
        def _(sp):
            sp.dma_start(ident[:], t["c_ident"]).then_inc(const_in, 16)
            sp.dma_start(c_sb[0:DB, :], t["c_sample"]).then_inc(c_in, 16)
            sp.dma_start(c_sb[DB:NC, :], t["c_prompt"]).then_inc(c_in, 16)
            for k in range(KC):
                if k >= NA:
                    sp.wait_ge(ada_used, k - NA + 1)
                sp.dma_start(ada[:, k % NA, :], ada_rows[:, k, :]).then_inc(ada_in[k % NA], 16)
                if k == 0:
                    sp.dma_start(vecs[0:8, :], t["norm_w"].rearrange("a (c p) -> (a c) p", p=P)).then_inc(small_in, 16)
                    sp.dma_start(vecs[8:12, :], t["b_pool"][0]).then_inc(small_in, 16)
                    sp.dma_start(vecs[12:16, :], t["pool_scale"].rearrange("a (c p) -> (a c) p", p=P)).then_inc(small_in, 16)
                    sp.dma_start(bias[:], t["ada_b"].rearrange("a n -> (a n)").partition_broadcast(NC)).then_inc(small_in, 16)
                    sp.dma_start(masks[:, 0, :], t["c_mask_q"]).then_inc(masks_in, 16)
                    sp.dma_start(masks[:, 1, :], t["c_mask_k"]).then_inc(masks_in, 16)
            sp.wait_ge(mod_ready, 6)
            sp.dma_start(mod_d, mod[:]).then_inc(mod_out, 16)
            sp.wait_ge(mod_out, 16)

        @block.scalar
        def _(act):
            act.dma_start(xs[:], t["x_sample"].rearrange("b s d -> (b s) d")).then_inc(xs_in, 16)
            for n in range(NX):
                act.dma_start(xt[:, n, :], x_blocks[:, n, :]).then_inc(x_in[n], 16)
            act.dma_start(wa_raw[:], w_in[:, :, 0:LA]).then_inc(wa_in, 16)
            act.wait_ge(c_turned, 1)
            act.activation(c_act[:].rearrange("p c n -> p (c n)"), ps_c[:, 0:KC * NC], ACT.Silu).then_inc(c_ready, 1)
            act.wait_ge(ss_zero, 1)
            act.wait_ge(xs_in, 16)
            act.activation(junk_s[:], xs[:], ACT.Square, accum_out=ss[0:DB, NB:NB + 1]).then_inc(x_squared, 1)
            for n in range(NB):
                act.wait_ge(x_in[n % NX], 16 * (n // NX + 1))
                act.activation(xt[:, n % NX, :], xt[:, n % NX, :], ACT.Square,
                               accum_out=ss[:, n:n + 1]).then_inc(x_squared, 1)
                if n >= 1 and n - 1 + NX < NB:
                    act.wait_ge(x_squared, n + 1)
                    act.dma_start(xt[:, (n - 1) % NX, :], x_blocks[:, n - 1 + NX, :]).then_inc(x_in[(n - 1) % NX], 16)
            act.wait_ge(var_ready, 1)
            act.activation(ss[:], ss[:], ACT.Sqrt).then_inc(sd_ready, 1)
            act.wait_ge(wa_in, 16)
            act.activation(wa[0][:], wa_raw[:], ACT.Copy).then_inc(wa_hi_ready, 1)

        @block.gpsimd
        def _(pool):
            pool.memset(ones[:], 1.0)
            for part in hs:
                last = pool.memset(part[:].bitcast(F32), 0.0)
            last.then_inc(hs_zero, 1)
            pool.wait_ge(const_in, 16)
            pool.tensor_copy(identb[:], ident[:])
            pool.wait_ge(masks_in, 32)
            pool.tensor_copy(mask_q[:], masks[:, 0, :])
            pool.tensor_copy(mask_k[:], masks[:, 1, :])
            pool.wait_ge(wa_hi_ready, 1)
            pool.tensor_tensor(wa[1][:], wa_raw[:], wa[0][:].bitcast(F32), ALU.subtract).then_inc(wa_lo_ready, 1)

        @block.vector
        def _(dve):
            dve.memset(ss[:], 0.0).then_inc(ss_zero, 1)
            dve.wait_ge(vec_turned, 1)
            dve.tensor_copy(vec_t[:], ps_t[:, 0:16]).then_inc(vec_ready, 1)
            dve.wait_ge(small_in, 64)
            dve.wait_ge(x_squared, NB + 1)
            dve.tensor_scalar(ss[:], ss[:], 1.0 / D, EPS, ALU.mult, ALU.add).then_inc(var_ready, 1)
            dve.wait_ge(sd_ready, 1)
            dve.reciprocal(rstd[:], ss[:]).then_inc(rstd_ready, 1)
            dve.wait_ge(rstd_ready, 1)
            dve.tensor_scalar(xs[:], xs[:], rstd[0:DB, NB:NB + 1], None, ALU.mult).then_inc(xs_scaled, 1)
            dve.wait_ge(mod_summed, 1)
            for g in range(6):
                dve.tensor_tensor(mod[:, g * 512:(g + 1) * 512], ps_mod[0:NC, g, :], bias[:, g * 512:(g + 1) * 512],
                                  ALU.add).then_inc(mod_ready, 1)
            dve.wait_ge(vec_ready, 1)
            dve.wait_ge(mod_turned, 1)
            turned = ps_c[:, 0:2 * KC * NC].rearrange("p (k c n) -> p k c n", k=2, c=KC)
            dve.tensor_copy(coef_b[:], turned[:, 0])
            dve.scalar_tensor_tensor(out=coef_a[:], in0=turned[:, 1], scalar=1.0,
                                     in1=vec_t[:, 0:KC].unsqueeze(2).broadcast_to([P, KC, NC]),
                                     op0=ALU.add, op1=ALU.mult).then_inc(coef_ready, 1)
            dve.wait_ge(coef_ready, 1)
            dve.wait_ge(xs_turned, 1)
            xs_t = ps_t[:, 64:64 + KC * DB].rearrange("p (c b) -> p c b", c=KC)
            dve.tensor_tensor(hs32[:], xs_t, coef_a[:, :, 0:DB], ALU.mult).then_inc(hs_done, 1)
            dve.wait_ge(hs_done, 1)
            dve.tensor_tensor(hs32[:], hs32[:], coef_b[:, :, 0:DB], ALU.add).then_inc(hs_done, 1)
            dve.wait_ge(hs_done, 2)
            dve.wait_ge(hs_zero, 1)
            dve.tensor_copy(hs[0][:, :, 0:DB], hs32[:]).then_inc(hs_done, 1)
            dve.wait_ge(hs_done, 3)
            dve.tensor_tensor(hs[1][:, :, 0:DB], hs32[:], hs[0][:, :, 0:DB].bitcast(F32), ALU.subtract).then_inc(hs_done, 1)

        @block.tensor
        def _(pe):
            pe.wait_ge(const_in, 16)
            pe.wait_ge(c_in, 32)
            for k in range(KC):
                last = pe.transpose(ps_c[:, k * NC:(k + 1) * NC], c_sb[:, k * P:(k + 1) * P], ident[0:NC, 0:NC])
            last.then_inc(c_turned, 1)
            pe.wait_ge(small_in, 64)
            pe.transpose(ps_t[:, 0:16], vecs[:], ident[0:16, 0:16]).then_inc(vec_turned, 1)
            pe.wait_ge(c_ready, 1)
            for k in range(KC):
                pe.wait_ge(ada_in[k % NA], 16 * (k // NA + 1))
                for g in range(6):
                    last = pe.matmul(ps_mod[0:NC, g, :], c_act[:, k, :], ada[:, k % NA, g * 512:(g + 1) * 512],
                                     start=(k == 0), stop=(k == KC - 1))
                last.then_inc(mod_summed if k == KC - 1 else ada_used, 1)
            pe.wait_ge(xs_scaled, 1)
            pe.wait_ge(vec_ready, 1)
            for k in range(KC):
                last = pe.transpose(ps_t[:, 64 + k * DB:64 + (k + 1) * DB], xs[:, k * P:(k + 1) * P], ident[0:DB, 0:DB])
            last.then_inc(xs_turned, 1)
            pe.wait_ge(mod_ready, 4)
            for k in range(2 * KC):
                last = pe.transpose(ps_c[:, k * NC:(k + 1) * NC], mod[:, k * P:(k + 1) * P], ident[0:NC, 0:NC])
            last.then_inc(mod_turned, 1)

    wb_at = Map(nc, after_wa)
    wb = [wb_at("wb_hi", [P, KC, LB], F32R), wb_at("wb_lo", [P, KC, LB], F32R)]
    ds = bass.ds
    with ExitStack() as ctx:
        sems = []
        ctx.callback(release, nc, sems)

        def psum(name, shape):
            return ctx.enter_context(nc.psum_tensor("lat_" + name, shape, F32))

        def sem(name):
            return stage_semaphore(nc, sems, "lat_" + name)

        m = Map(nc, wb_at.at)
        xt = m("lat_x", [P, 2, D], F32)
        h32 = m("lat_h32", [P, D], F32)
        hb = [m("lat_h_hi", [P, 2, D], F32R), m("lat_h_lo", [P, 2, D], F32R)]
        wraw = m("lat_wraw", [P, LB], F32)
        lat = m("lat_rows", [P, 2, LA], F32)
        junk = m("lat_junk", [P, 2, OFF_KR], F32)
        stat = m("lat_stat", [P, 2, 2], F32)
        rot = m("lat_rot", [P, 2, ROPE], F32)
        qn_w = m("qn_w", [P, QL], F32)
        kn_w = m("kn_w", [P, KVL], F32)
        cosk = m("cosk", [P, NB, ROPE], F32)
        sink = m("sink", [P, NB, ROPE], F32)
        zs = m("zs_a", [DB, LA], F32)
        ps_x = psum("ps_x", [P, 2, 512])
        ps_z = psum("ps_z", [P, 2, 512])
        ps_l = psum("ps_l", [P, 512])
        ps_s = psum("ps_s", [P, 512])
        x_in = [sem("x_in0"), sem("x_in1")]
        tab_in, wb_in = sem("tab_in"), sem("wb_in")
        x_scaled, x_turned, h_ready, h_hi, h_lo = (
            sem("x_scaled"), sem("x_turned"), sem("h_ready"), sem("h_hi"), sem("h_lo"))
        z_done, ss_ready, var_ready, sd_ready, step_done = (
            sem("z_done"), sem("ss_ready"), sem("var_ready"), sem("sd_ready"), sem("step_done"))
        lat_ready, lat_turned, lat_kept = sem("lat_ready"), sem("lat_turned"), sem("lat_kept")
        lat_out = [sem("lat_out0"), sem("lat_out1")]
        wb_hi, wb_lo = sem("wb_hi_ready"), sem("wb_lo_ready")
        zs_done, zs_ready, zs_out = sem("zs_done"), sem("zs_ready"), sem("zs_out")
        NP2 = NB // 2
        block = ctx.enter_context(nc.Block())

        @block.sync
        def _(sp):
            for b in range(2):
                sp.dma_start(xt[:, b, :], x_blocks[:, b, :]).then_inc(x_in[b], 16)
            sp.dma_start(qn_w[:], t["q_norm_w"].rearrange("a n -> (a n)").partition_broadcast(P)).then_inc(tab_in, 16)
            sp.dma_start(kn_w[:], t["kv_norm_w"].rearrange("a n -> (a n)").partition_broadcast(P)).then_inc(tab_in, 16)
            sp.dma_start(cosk[:], t["c_rope_rows"][0]).then_inc(tab_in, 16)
            sp.dma_start(sink[:], t["c_rope_rows"][1]).then_inc(tab_in, 16)

            def body(i):
                for b in range(2):
                    n = 2 * i + b
                    if exists(n + 2, NB):
                        sp.wait_ge(x_turned, n + 1)
                        sp.dma_start(xt[:, b, :], x_blocks[:, ds(n + 2, 1), :]).then_inc(x_in[b], 16)
                if exists(i - 1, KC):
                    sp.wait_ge(wb_lo, i)
                sp.dma_start(wraw[:].unsqueeze(1), w_in[:, ds(i, 1), LA:DIN]).then_inc(wb_in, 16)
            peeled(sp, NP2, body)
            sp.wait_ge(zs_ready, 1)
            sp.dma_start(zs_d[:, 0:LA], zs[:]).then_inc(zs_out, 16)
            sp.wait_ge(zs_out, 16)

        @block.scalar
        def _(act):
            def scale_x(n, b):
                act.wait_ge(x_in[b], 16 * (n // 2 + 1) if isinstance(n, int) else 8 * (n - b) + 16)
                act.activation(xt[:, b, :], xt[:, b, :], ACT.Copy, scale=rstd[:, ds(n, 1)]).then_inc(x_scaled, 1)

            def h_high(n, b):
                act.wait_ge(h_ready, n + 1)
                if exists(n - 2, NB):
                    act.wait_ge(z_done, n - 1)
                act.activation(hb[0][:, b, :], h32[:], ACT.Copy).then_inc(h_hi, 1)

            def keep_lat(n, b):
                act.wait_ge(lat_turned, n + 1)
                act.activation(lat_t[:, :, ds(n * P, P)], ps_l[:, 0:3 * P].rearrange("p (c s) -> p c s", c=3),
                               ACT.Copy).then_inc(lat_kept, 1)
                act.dma_start(ckv_out[:, ds(n, 1), :], lat[:, b, OFF_KV:OFF_KR].unsqueeze(1)).then_inc(lat_out[b], 16)
                act.dma_start(kr_out[:, ds(n, 1), :], lat[:, b, OFF_KR:LA].unsqueeze(1)).then_inc(lat_out[b], 16)

            def body(i):
                for b in range(2):
                    n = 2 * i + b
                    if exists(n + 2, NB):
                        h_high(n + 2, b)
                    if exists(n + 3, NB):
                        scale_x(n + 3, 1 - b)
                    act.wait_ge(z_done, n + 1)
                    if exists(n - 2, NB):
                        act.wait_ge(var_ready, n - 1)
                    act.activation(junk[:, b, 0:QL], ps_z[:, b, 0:QL], ACT.Square, accum_out=stat[:, b, 0:1])
                    act.activation(junk[:, b, OFF_KV:OFF_KR], ps_z[:, b, OFF_KV:OFF_KR], ACT.Square,
                                   accum_out=stat[:, b, 1:2]).then_inc(ss_ready, 1)
                    if exists(n - 1, NB):
                        keep_lat(n - 1, 1 - b)
                    act.wait_ge(var_ready, n + 1)
                    act.activation(stat[:, b, :], stat[:, b, :], ACT.Sqrt).then_inc(sd_ready, 1)
                act.wait_ge(wb_in, 16 * i + 16)
                act.activation(wb[0][:, ds(i, 1), :], wraw[:].unsqueeze(1), ACT.Copy).then_inc(wb_hi, 1)
            scale_x(0, 0)
            scale_x(1, 1)
            h_high(0, 0)
            h_high(1, 1)
            scale_x(2, 0)
            peeled(act, NP2, body, tail=2)
            keep_lat(NB - 1, 1)
            for b in range(2):
                act.wait_ge(lat_out[b], 16 * NB)

        @block.gpsimd
        def _(pool):
            def h_low(n, b):
                pool.wait_ge(h_hi, n + 1)
                pool.tensor_tensor(hb[1][:, b, :], h32[:], hb[0][:, b, :].bitcast(F32), ALU.subtract).then_inc(h_lo, 1)

            def body(i):
                for b in range(2):
                    if exists(2 * i + b + 2, NB):
                        h_low(2 * i + b + 2, b)
                pool.wait_ge(wb_hi, i + 1)
                pool.tensor_tensor(wb[1][:, ds(i, 1), :], wraw[:].unsqueeze(1), wb[0][:, ds(i, 1), :].bitcast(F32),
                                   ALU.subtract).then_inc(wb_lo, 1)
            h_low(0, 0)
            h_low(1, 1)
            peeled(pool, NP2, body)

        @block.vector
        def _(dve):
            def h_values(n):
                dve.wait_ge(x_turned, n + 1)
                if exists(n - 1, NB):
                    dve.wait_ge(h_lo, n)
                for c in range(KC):
                    last = dve.tensor_scalar(h32[:, c * P:(c + 1) * P], ps_x[:, c // 4, (c % 4) * P:(c % 4 + 1) * P],
                                             coef_a[:, c, DB:NC], coef_b[:, c, DB:NC], ALU.mult, ALU.add)
                last.then_inc(h_ready, 1)

            def body(i):
                for b in range(2):
                    n = 2 * i + b
                    if exists(n + 2, NB):
                        h_values(n + 2)
                    dve.wait_ge(ss_ready, n + 1)
                    dve.tensor_scalar(stat[:, b, 0:1], stat[:, b, 0:1], 1.0 / QL, EPS, ALU.mult, ALU.add)
                    dve.tensor_scalar(stat[:, b, 1:2], stat[:, b, 1:2], 1.0 / KVL, EPS, ALU.mult, ALU.add).then_inc(var_ready, 1)
                    if exists(n - 2, NB):
                        dve.wait_ge(lat_turned, n - 1)
                        dve.wait_ge(lat_out[b], 32 * i if b == 0 else 32 * i)
                    z = ps_z[:, b, :]
                    dve.tensor_tensor(lat[:, b, OFF_KR:LA], z[:, OFF_KR:LA], cosk[:, ds(n, 1), :].squeeze(1), ALU.mult)
                    dve.tensor_tensor(rot[:, b, 0:16], z[:, OFF_KR + 16:LA], sink[:, ds(n, 1), 0:16].squeeze(1), ALU.mult)
                    dve.tensor_tensor(rot[:, b, 16:32], z[:, OFF_KR:OFF_KR + 16], sink[:, ds(n, 1), 16:32].squeeze(1),
                                      ALU.mult).then_inc(step_done, 1)
                    dve.wait_ge(step_done, 2 * n + 1)
                    dve.tensor_tensor(lat[:, b, OFF_KR:LA], lat[:, b, OFF_KR:LA], rot[:, b, :], ALU.add)
                    dve.wait_ge(sd_ready, n + 1)
                    dve.reciprocal(stat[:, b, :], stat[:, b, :]).then_inc(step_done, 1)
                    dve.wait_ge(step_done, 2 * n + 2)
                    dve.scalar_tensor_tensor(out=lat[:, b, 0:QL], in0=z[:, 0:QL], scalar=stat[:, b, 0:1], in1=qn_w[:],
                                             op0=ALU.mult, op1=ALU.mult)
                    dve.scalar_tensor_tensor(out=lat[:, b, OFF_KV:OFF_KR], in0=z[:, OFF_KV:OFF_KR], scalar=stat[:, b, 1:2],
                                             in1=kn_w[:], op0=ALU.mult, op1=ALU.mult).then_inc(lat_ready, 1)
            dve.wait_ge(tab_in, 64)
            h_values(0)
            h_values(1)
            peeled(dve, NP2, body)
            dve.wait_ge(zs_done, 1)
            dve.tensor_copy(zs[:], ps_s[0:DB, 0:LA]).then_inc(zs_ready, 1)

        @block.tensor
        def _(pe):
            def turn_x(n, b):
                pe.wait_ge(x_scaled, n + 1)
                if exists(n - 1, NB):
                    pe.wait_ge(h_ready, n)
                for c in range(KC):
                    last = pe.transpose(ps_x[:, c // 4, (c % 4) * P:(c % 4 + 1) * P], xt[:, b, c * P:(c + 1) * P], ident[:])
                last.then_inc(x_turned, 1)

            def turn_lat(n, b):
                pe.wait_ge(lat_ready, n + 1)
                if exists(n - 1, NB):
                    pe.wait_ge(lat_kept, n)
                for c in range(3):
                    last = pe.transpose(ps_l[:, c * P:(c + 1) * P], lat[:, b, c * P:(c + 1) * P], ident[:])
                last.then_inc(lat_turned, 1)

            def body(i):
                for b in range(2):
                    n = 2 * i + b
                    if exists(n + 2, NB):
                        turn_x(n + 2, b)
                    pe.wait_ge(h_lo, n + 1)
                    if exists(n - 2, NB):
                        pe.wait_ge(lat_ready, n - 1)
                    for c in range(KC):
                        cols = slice(c * P, (c + 1) * P)
                        last = mm3(pe, ps_z[:, b, 0:LA], [hb[0][:, b, cols], hb[1][:, b, cols]],
                                   [wa[0][:, c, :], wa[1][:, c, :]], c == 0, c == KC - 1)
                    last.then_inc(z_done, 1)
                    if exists(n - 1, NB):
                        turn_lat(n - 1, 1 - b)
            turn_x(0, 0)
            turn_x(1, 1)
            peeled(pe, NP2, body)
            turn_lat(NB - 1, 1)
            for c in range(KC):
                last = mm3(pe, ps_s[:, 0:LA], [hs[0][:, c, :], hs[1][:, c, :]],
                           [wa[0][:, c, :], wa[1][:, c, :]], c == 0, c == KC - 1)
            last.then_inc(zs_done, 1)

    T = 2 * P
    NS = S // T
    with ExitStack() as ctx:
        sems = []
        ctx.callback(release, nc, sems)

        def psum(name, shape):
            return ctx.enter_context(nc.psum_tensor("mix_" + name, shape, F32))

        def sem(name):
            return stage_semaphore(nc, sems, "mix_" + name)

        m = Map(nc, after_hs)
        u_ext = m("u_ext", [P, NG, PREV + T], F32)
        win = m("win", [P, 2, 2, PREV + T], F32)
        pooled = m("pooled", [P, NG, T], F32)
        gate_p = m("gate_p", [P, NG, T], F32)
        mixed = m("mixed", [P, NG, T], F32)
        gate_a = m("gate_a", [P, 2, DATT], F32)
        assert m.at <= after_wa
        m = Map(nc, wb_at.at)
        hb = [m("mix_h_hi", [P, 2, KC, T], F32R), m("mix_h_lo", [P, 2, KC, T], F32R)]
        xt = m("mix_x", [P, 2, D], F32)
        h32 = m("mix_h32", [P, D], F32)
        w_pool = m("w_pool", [P, NG, P], F32)
        count = m("count", [P, NG, 16], F32)
        early = m("early", [P, 16], F32)
        prev = m("prev", [PREV, DPOOL], F32)
        zs_b = xt[0:DB].rearrange("p b d -> p (b d)")[:, 0:LB]
        ps_x = psum("ps_x", [P, 2, 512])
        ps_u = psum("ps_u", [P, 2, 512])
        ps_a = psum("ps_a", [P, 2, 512])
        ps_y = psum("ps_y", [P, 2, 512])
        ps_z = [ps_a[:, 0, :], ps_a[:, 1, :]]
        x_in = [sem("x_in0"), sem("x_in1")]
        tab_in = sem("tab_in")
        x_scaled, x_turned, h_ready, h_hi, h_lo = (
            sem("x_scaled"), sem("x_turned"), sem("h_ready"), sem("h_hi"), sem("h_lo"))
        u_done, u_kept, win_step, win_ready, pooled_ready, halo_ready = (
            sem("u_done"), sem("u_kept"), sem("win_step"), sem("win_ready"), sem("pooled_ready"), sem("halo_ready"))
        a_done, a_kept, y_done, y_step, mixed_ready = (
            sem("a_done"), sem("a_kept"), sem("y_done"), sem("y_step"), sem("mixed_ready"))
        early_step = sem("early_step")
        mixed_out = [sem(f"mixed_out{g}") for g in range(NG)]
        a_out = [sem("a_out0"), sem("a_out1")]
        zs_done, zs_ready, zs_out, prev_done, prev_ready = (
            sem("zs_done"), sem("zs_ready"), sem("zs_out"), sem("prev_done"), sem("prev_ready"))
        HALF = NS // 2
        LEVELS = sum(g + 1 for g in range(NG))
        block = ctx.enter_context(nc.Block())

        @block.sync
        def _(sp):
            for b in range(2):
                sp.dma_start(xt[:, b, :], x_blocks[:, b, :]).then_inc(x_in[b], 16)
            sp.dma_start(w_pool[:], t["w_pool"].rearrange("a g c d -> c (a g) d")).then_inc(tab_in, 16)
            sp.dma_start(count[:].rearrange("p g s -> p (g s)"),
                         t["c_count"].rearrange("g s -> (g s)").partition_broadcast(P)).then_inc(tab_in, 16)

            def load_x(n, b):
                sp.wait_ge(x_turned, n - 1)
                sp.dma_start(xt[:, b, :], x_blocks[:, ds(n, 1), :]).then_inc(x_in[b], 16)

            def body(s, e):
                for b in range(2):
                    if exists(s + 2, NS):
                        load_x(2 * s + 4 + b, b)
                for b in range(2):
                    sp.wait_ge(a_kept, 2 * s + b + 1)
                    sp.dma_start(gate_att_blocks[:, ds(2 * s + b, 1), :], gate_a[:, b, :].unsqueeze(1)).then_inc(a_out[b], 16)
                for g in range(NG):
                    sp.wait_ge(mixed_ready, 4 * s + g + 1)
                    sp.dma_start(pool_d[g][:, ds(s * T, T)], mixed[:, g, :]).then_inc(mixed_out[g], 16)
            for b in range(2):
                load_x(2 + b, b)
            peeled(sp, HALF, lambda i: [body(2 * i + e, e) for e in range(2)])
            sp.wait_ge(zs_ready, 3)
            sp.dma_start(zs_d[:, LA:DIN], zs_b).then_inc(zs_out, 16)
            sp.wait_ge(prev_ready, 1)
            sp.dma_start(o[4].rearrange("a b r c -> (a b r) c"), prev[:]).then_inc(zs_out, 16)
            sp.wait_ge(zs_out, 32)
            for b in range(2):
                sp.wait_ge(a_out[b], 16 * NS)
            for g in range(NG):
                sp.wait_ge(mixed_out[g], 16 * NS)

        @block.scalar
        def _(act):
            def scale_x(n, b):
                act.wait_ge(x_in[b], 8 * (n - b) + 16)
                act.activation(xt[:, b, :], xt[:, b, :], ACT.Copy, scale=rstd[:, ds(n, 1)]).then_inc(x_scaled, 1)

            def h_high(s, e, b):
                act.wait_ge(h_ready, 2 * s + b + 1)
                if exists(s - 2, NS):
                    act.wait_ge(a_done, 2 * (s - 1))
                act.activation(hb[0][:, e, :, b * P:(b + 1) * P], h32[:].rearrange("p (c s) -> p c s", c=KC),
                               ACT.Copy).then_inc(h_hi, 1)

            def keep_u(s, g):
                act.wait_ge(u_done, 4 * s + g + 1)
                act.wait_ge(halo_ready, 4 * s + g + 1)
                act.activation(u_ext[:, g, PREV:], ps_u[:, g % 2, 0:T], ACT.Copy)
                if exists(s - 1, NS):
                    act.wait_ge(mixed_ready, 4 * (s - 1) + g + 1)
                act.activation(gate_p[:, g, :], ps_u[:, g % 2, T:2 * T], ACT.Silu).then_inc(u_kept, 1)

            def body(s, e):
                for b in range(2):
                    if exists(s + 1, NS):
                        h_high(s + 1, 1 - e, b)
                    keep_u(s, 2 * b)
                    keep_u(s, 2 * b + 1)
                for b in range(2):
                    if exists(s + 2, NS):
                        scale_x(2 * s + 4 + b, b)
                for b in range(2):
                    act.wait_ge(a_done, 2 * s + b + 1)
                    if exists(s - 1, NS):
                        act.wait_ge(a_out[b], 16 * s)
                    act.activation(gate_a[:, b, :], ps_a[:, b, :], ACT.Silu).then_inc(a_kept, 1)
            for b in range(2):
                scale_x(b, b)
            for b in range(2):
                h_high(0, 0, b)
            for b in range(2):
                scale_x(2 + b, b)
            peeled(act, HALF, lambda i: [body(2 * i + e, e) for e in range(2)])

        @block.gpsimd
        def _(pool):
            steps = [0]

            def h_low(s, e, b):
                pool.wait_ge(h_hi, 2 * s + b + 1)
                pool.tensor_tensor(hb[1][:, e, :, b * P:(b + 1) * P], h32[:].rearrange("p (c s) -> p c s", c=KC),
                                   hb[0][:, e, :, b * P:(b + 1) * P].bitcast(F32), ALU.subtract).then_inc(h_lo, 1)

            def window(s, g, done):
                pool.wait_ge(u_kept, 4 * s + g + 1)
                if g >= 2:
                    pool.wait_ge(pooled_ready, 4 * s + g - 1)
                elif exists(s - 1, NS):
                    pool.wait_ge(pooled_ready, 4 * (s - 1) + g + 3)
                src = u_ext[:, g, :]
                for level in range(g + 1):
                    shift = 1 << level
                    width = T + (1 << (g + 1)) - 2 * shift
                    if level:
                        pool.wait_ge(win_step, s * LEVELS + done + level)
                    dst = win[:, g % 2, level % 2, PREV + T - width:]
                    last = pool.tensor_tensor(dst, src[:, PREV + T - width:PREV + T],
                                              src[:, PREV + T - width - shift:PREV + T - shift], ALU.add)
                    last.then_inc(win_step, 1)
                    src = win[:, g % 2, level % 2, :]

            def body(s, e):
                done = 0
                for b in range(2):
                    if exists(s + 1, NS):
                        h_low(s + 1, 1 - e, b)
                    for g in (2 * b, 2 * b + 1):
                        window(s, g, done)
                        done += g + 1
            pool.memset(u_ext[:], 0.0).then_inc(halo_ready, NG)
            for b in range(2):
                h_low(0, 0, b)
            peeled(pool, HALF, lambda i: [body(2 * i + e, e) for e in range(2)])

        @block.vector
        def _(dve):
            def h_values(n):
                dve.wait_ge(x_turned, n + 1)
                if exists(n - 1, NB):
                    dve.wait_ge(h_lo, n)
                for c in range(KC):
                    last = dve.tensor_scalar(h32[:, c * P:(c + 1) * P], ps_x[:, c // 4, (c % 4) * P:(c % 4 + 1) * P],
                                             coef_a[:, c, DB:NC], coef_b[:, c, DB:NC], ALU.mult, ALU.add)
                last.then_inc(h_ready, 1)

            def pooled_values(s, g, done):
                dve.wait_ge(win_step, s * LEVELS + done)
                if exists(s - 1, NS):
                    dve.wait_ge(y_done, 4 * (s - 1) + g + 1)
                total = win[:, g % 2, g % 2, PREV:]
                first = isinstance(s, int) and s == 0
                if first:
                    dve.tensor_tensor(early[:], total[:, 0:16], count[:, g, :], ALU.mult).then_inc(early_step, 1)
                    dve.wait_ge(early_step, 2 * g + 1)
                    dve.tensor_tensor(pooled[:, g, 0:16], early[:], u_ext[:, g, PREV:PREV + 16],
                                      ALU.subtract).then_inc(early_step, 1)
                    dve.wait_ge(early_step, 2 * g + 2)
                z = 16 if first else 0
                dve.scalar_tensor_tensor(out=pooled[:, g, z:], in0=total[:, z:], scalar=1.0 / (2 << g),
                                         in1=u_ext[:, g, PREV + z:], op0=ALU.mult, op1=ALU.subtract).then_inc(pooled_ready, 1)
                dve.wait_ge(pooled_ready, 4 * s + g + 1)
                if exists(s + 1, NS):
                    dve.tensor_copy(u_ext[:, g, 0:PREV], u_ext[:, g, T:]).then_inc(halo_ready, 1)

            def mix(s, g):
                dve.wait_ge(y_done, 4 * s + g + 1)
                if exists(s - 1, NS):
                    dve.wait_ge(mixed_out[g], 16 * s)
                dve.tensor_scalar(mixed[:, g, :], ps_y[:, g % 2, 0:T], vec_t[:, 8 + g:9 + g], vec_t[:, 12 + g:13 + g],
                                  ALU.add, ALU.mult).then_inc(y_step, 1)
                dve.wait_ge(y_step, 4 * s + g + 1)
                dve.tensor_tensor(mixed[:, g, :], mixed[:, g, :], gate_p[:, g, :], ALU.mult).then_inc(mixed_ready, 1)

            def body(s, e):
                done = 0
                for b in range(2):
                    if exists(s + 1, NS):
                        h_values(2 * s + 2 + b)
                    for g in (2 * b, 2 * b + 1):
                        done += g + 1
                        pooled_values(s, g, done)
                for g in range(NG):
                    mix(s, g)
            dve.wait_ge(tab_in, 32)
            for b in range(2):
                h_values(b)
            peeled(dve, HALF, lambda i: [body(2 * i + e, e) for e in range(2)])
            for k in range(3):
                dve.wait_ge(zs_done, k + 1)
                dve.tensor_copy(zs_b[:, k * 512:(k + 1) * 512], ps_z[k % 2][0:DB, :]).then_inc(zs_ready, 1)
            dve.wait_ge(prev_done, 1)
            dve.tensor_copy(prev[:], ps_y[0:PREV, 0, :]).then_inc(prev_ready, 1)

        @block.tensor
        def _(pe):
            def turn_x(n, b):
                pe.wait_ge(x_scaled, n + 1)
                if exists(n - 1, NB):
                    pe.wait_ge(h_ready, n)
                for c in range(KC):
                    last = pe.transpose(ps_x[:, c // 4, (c % 4) * P:(c % 4 + 1) * P], xt[:, b, c * P:(c + 1) * P], ident[:])
                last.then_inc(x_turned, 1)

            def group(s, e, g):
                if g >= 2:
                    pe.wait_ge(u_kept, 4 * s + g - 1)
                elif exists(s - 1, NS):
                    pe.wait_ge(u_kept, 4 * (s - 1) + g + 3)
                for off, at in ((OFF_U, 0), (OFF_GP, T)):
                    cols = slice(off + g * P, off + (g + 1) * P)
                    for c in range(KC):
                        last = mm3(pe, ps_u[:, g % 2, at:at + T], [wb[0][:, c, cols], wb[1][:, c, cols]],
                                   [hb[0][:, e, c, :], hb[1][:, e, c, :]], c == 0, c == KC - 1)
                last.then_inc(u_done, 1)

            def body(s, e):
                pe.wait_ge(h_lo, 2 * s + 2)
                for b in range(2):
                    if exists(s + 1, NS):
                        turn_x(2 * s + 2 + b, b)
                    group(s, e, 2 * b)
                    group(s, e, 2 * b + 1)
                for b in range(2):
                    if exists(s - 1, NS):
                        pe.wait_ge(a_kept, 2 * (s - 1) + b + 1)
                    for c in range(KC):
                        cols = slice(b * P, (b + 1) * P)
                        last = mm3(pe, ps_a[:, b, :], [hb[0][:, e, c, cols], hb[1][:, e, c, cols]],
                                   [wb[0][:, c, 0:DATT], wb[1][:, c, 0:DATT]], c == 0, c == KC - 1)
                    last.then_inc(a_done, 1)
                for g in range(NG):
                    pe.wait_ge(pooled_ready, 4 * s + g + 1)
                    if g >= 2:
                        pe.wait_ge(y_step, 4 * s + g - 1)
                    elif exists(s - 1, NS):
                        pe.wait_ge(y_step, 4 * (s - 1) + g + 3)
                    pe.matmul(ps_y[:, g % 2, 0:T], w_pool[:, g, :], pooled[:, g, :], start=True, stop=True).then_inc(y_done, 1)
            for b in range(2):
                turn_x(b, b)
            peeled(pe, HALF, lambda i: [body(2 * i + e, e) for e in range(2)])
            pe.wait_ge(a_kept, NB)
            for k in range(3):
                if k == 2:
                    pe.wait_ge(zs_ready, 1)
                for c in range(KC):
                    cols = slice(k * 512, (k + 1) * 512)
                    last = mm3(pe, ps_z[k % 2], [hs[0][:, c, :], hs[1][:, c, :]],
                               [wb[0][:, c, cols], wb[1][:, c, cols]], c == 0, c == KC - 1)
                last.then_inc(zs_done, 1)
            pe.wait_ge(y_step, 4 * NS)
            for g in range(NG):
                last = pe.transpose(ps_y[0:PREV, 0, g * P:(g + 1) * P], u_ext[:, g, T:], ident[:])
            last.then_inc(prev_done, 1)

    VW = VD + 1
    tiles = [(I, j) for I in range(NGRP) for j in range(GRP * I + GRP)]
    chunks = [(I, r, c) for I in range(NGRP) for r in range(GRP) for c in range(I + 1)]
    NT, NCH = len(tiles), len(chunks)
    assert NT % 4 == 0 and NCH % 2 == 0

    def tile_cols(k):
        I, j = tiles[k]
        c0 = max(0, j - GRP * I) * P
        return c0, GRP * P - c0

    def side_work():
        side = [[] for _ in range(NT)]
        for k, c in ((1, 0), (3, 1), (5, 2), (8, 3)):
            side[k].append(("prepare", c))
        start = 6
        for n in range(NCH):
            k = start + n * (NT - start) // NCH
            if n:
                k = max(k, last_k)
            last_k = k
            side[k].append(("maxima", n))
            if n + 1 == NCH or chunks[n + 1][0] != chunks[n][0]:
                I = chunks[n][0]
                if I < NGRP - 1:
                    side[max(k + 2, 9)].append(("turn", I))
        return side
    side = side_work()
    LASTG = NGRP - 1

    with ExitStack() as ctx:
        sems = []
        ctx.callback(release, nc, sems)

        def psum(name, shape):
            return ctx.enter_context(nc.psum_tensor("att_" + name, shape, F32))

        def sem(name):
            return stage_semaphore(nc, sems, "att_" + name)

        lat_lo = nc.alloc_sbuf_tensor_at("lat_lo", [P, 3, S], F32R, offset=after_lat - 3 * S * 4)
        m = Map(nc, after_lat)
        lat_hi = m("lat_hi", [P, 3, S], F32R)
        v = m("v", [P, NB, H, VW], F32)
        q = [[m(f"q_hi{e}", [P, S], F32R), m(f"q_lo{e}", [P, S], F32R)] for e in range(2)]
        kk = [[m(f"k_hi{e}", [P, S], F32R), m(f"k_lo{e}", [P, S], F32R)] for e in range(2)]
        rope = m("rope", [P, S], F32)
        pt = m("pt", [P, 4, 512], F32)
        q32 = m("q32", [P, 2, 512], F32)
        rot = m("att_rot", [P, 512], F32)
        wq_raw = m("wq_raw", [P, QC, P], F32)
        wk_raw = m("wk_raw", [P, VD], F32)
        wq = [m("wq_hi", [P, QC, P], F32R), m("wq_lo", [P, QC, P], F32R)]
        wk = [m("wk_hi", [P, P], F32R), m("wk_lo", [P, P], F32R)]
        mx = m("mx", [P, 2, GRP, NGRP], F32)
        negm = m("negm", [P, 2, GRP], F32)
        rec = m("rec", [P, 2, GRP], F32)
        att = m("att", [P, 2, GRP, VD], F32)
        early_map = Map(nc, m.at)
        wv = [early_map("wv_hi", [P, DATT], F32R), early_map("wv_lo", [P, DATT], F32R)]
        wv_raw = early_map("wv_raw", [P, DATT], F32)
        kr = early_map("kr_rows", [P, NB, ROPE], F32)
        ps_s, ps_p, ps_o = psum("ps_s", [P, 2, 512]), psum("ps_p", [P, 2, 512]), psum("ps_o", [P, 2, 512])
        ps_q, ps_k = psum("ps_q", [P, 512]), psum("ps_k", [P, 512])

        kr_in, wv_in, rope_in, wq_in = sem("kr_in"), sem("wv_in"), sem("rope_in"), sem("wq_in")
        lat_hi_ready, lat_lo_ready, filled = sem("lat_hi_ready"), sem("lat_lo_ready"), sem("filled")
        wv_hi_ready, wv_ready, wq_hi_ready, wq_ready = sem("wv_hi_ready"), sem("wv_ready"), sem("wq_hi_ready"), sem("wq_ready")
        kr_turned, kr_hi_ready, kr_kept, v_done, v_kept = (
            sem("kr_turned"), sem("kr_hi_ready"), sem("kr_kept"), sem("v_done"), sem("v_kept"))
        q_done, k_done, q_read, q32_ready, q_hi_ready, q_lo_ready, k_hi_ready, k_kept = (
            sem("q_done"), sem("k_done"), sem("q_read"), sem("q32_ready"), sem("q_hi_ready"), sem("q_lo_ready"),
            sem("k_hi_ready"), sem("k_kept"))
        chunk_done, chunk_read, negm_ready, m_turned, m_kept = (
            sem("chunk_done"), sem("chunk_read"), sem("negm_ready"), sem("m_turned"), sem("m_kept"))
        scores_done, exp_done, pv_done, rec_ready, att_ready = (
            sem("scores_done"), sem("exp_done"), sem("pv_done"), sem("rec_ready"), sem("att_ready"))
        att_out = [sem("att_out0"), sem("att_out1")]
        wuq = t["w_uq"].rearrange("a (c p) h d -> p (a c) h d", p=P)
        wuk = t["w_uk"].rearrange("a k h d -> k (a h) d")
        att_groups = att_d.rearrange("(g r p) (h d) -> p g r h d", p=P, r=GRP, h=H)
        HP = H // 2
        block = ctx.enter_context(nc.Block())

        @block.sync
        def _(sp):
            def load_weights(g):
                one = ds(g, 1)
                sp.dma_start(wq_raw[:, :, 0:QK].unsqueeze(2), wuq[:, :, one, :]).then_inc(wq_in, 16)
                sp.dma_start(wq_raw[:, :, QK:QK + 16].unsqueeze(2), wuq[:, :, one, NOPE + 16:QK]).then_inc(wq_in, 16)
                sp.dma_start(wq_raw[:, :, QK + 16:P].unsqueeze(2), wuq[:, :, one, NOPE:NOPE + 16]).then_inc(wq_in, 16)
                sp.dma_start(wk_raw[:].unsqueeze(1), wuk[:, one, :]).then_inc(wq_in, 16)

            def store(h, I):
                sp.wait_ge(att_ready, NGRP * h + I + 1)
                sp.dma_start(att_groups[:, I, :, ds(h, 1), :].squeeze(2), att[:, I % 2]).then_inc(att_out[I % 2], 16)

            def body(h, e):
                if exists(h + 2, H):
                    sp.wait_ge(wq_ready, h + 2)
                    load_weights(h + 2)
                for I in range(NGRP):
                    store(h, I)
            load_weights(0)
            sp.dma_start(kr[:], kr_out).then_inc(kr_in, 16)
            sp.dma_start(wv_raw[:], t["w_uv"].rearrange("a k h d -> (a k) (h d)")).then_inc(wv_in, 16)
            sp.dma_start(rope[:], t["c_rope_cols"]).then_inc(rope_in, 16)
            sp.wait_ge(wq_ready, 1)
            load_weights(1)
            peeled(sp, HP, lambda i: [body(2 * i + e, e) for e in range(2)])
            for e in range(2):
                sp.wait_ge(att_out[e], 16 * H * NGRP // 2)

        @block.scalar
        def _(act):
            def prepare(g, slot, c):
                cols = slice(c * 512, (c + 1) * 512)
                act.wait_ge(k_done, NGRP * g + c + 1)
                act.activation(kk[slot][0][0:NOPE, cols], ps_k[0:NOPE, :], ACT.Copy).then_inc(k_hi_ready, 1)
                act.wait_ge(q32_ready, NGRP * g + c + 1)
                act.activation(q[slot][0][0:QK, cols], q32[0:QK, c % 2, :], ACT.Copy).then_inc(q_hi_ready, 1)

            def keep_max(g, slot, I):
                act.wait_ge(m_turned, NGRP * g + I + 1)
                act.activation(q[slot][0][QK:QK + 1, I * 512:(I + 1) * 512], ps_k[0:1, :], ACT.Copy).then_inc(m_kept, 1)

            def weights_high(g):
                act.wait_ge(wq_in, 64 * g + 64)
                if exists(g - 1, H):
                    act.wait_ge(k_done, NGRP * g)
                act.activation(wq[0][:], wq_raw[:], ACT.Copy)
                act.activation(wk[0][:, 0:NOPE], wk_raw[:], ACT.Copy).then_inc(wq_hi_ready, 1)

            def exponentials(h, k):
                c0, n = tile_cols(k)
                act.wait_ge(scores_done, NT * h + k + 1)
                if exists(NT * h + k - 4, NT * H):
                    act.wait_ge(pv_done, NT * h + k - 3)
                act.activation(pt[:, k % 4, 0:n], ps_s[:, k % 2, 0:n], ACT.Exp, scale=SCALE).then_inc(exp_done, 1)

            def body(h, e):
                for k in range(NT):
                    exponentials(h, k)
                    if k == 1:
                        keep_max(h, e, LASTG)
                    if exists(h + 1, H):
                        for what, n in side[k]:
                            if what == "prepare":
                                prepare(h + 1, 1 - e, n)
                            elif what == "turn":
                                keep_max(h + 1, 1 - e, n)
                    if k == NT // 2 and exists(h + 2, H):
                        weights_high(h + 2)
            weights_high(0)
            for c in range(NGRP):
                act.activation(lat_hi[:, :, c * 512:(c + 1) * 512], lat_t[:, :, c * 512:(c + 1) * 512],
                               ACT.Copy).then_inc(lat_hi_ready, 1)
                if c == 0:
                    act.wait_ge(wv_in, 16)
                    act.activation(wv[0][:], wv_raw[:], ACT.Copy).then_inc(wv_hi_ready, 1)
            for c in range(NGRP):
                act.wait_ge(kr_turned, c + 1)
                for e in range(2):
                    last = act.activation(kk[e][0][NOPE:QK, c * 512:(c + 1) * 512], (ps_s if c < 2 else ps_p)[0:ROPE, c % 2, :],
                                          ACT.Copy)
                last.then_inc(kr_hi_ready, 1)
            for n in range(NB):
                act.wait_ge(v_done, n + 1)
                act.activation(v[:, n, :, 0:VD], ps_o[:, n % 2, :].rearrange("p (h d) -> p h d", h=H),
                               ACT.Copy).then_inc(v_kept, 1)
            for c in range(NGRP):
                prepare(0, 0, c)
            weights_high(1)
            for I in range(LASTG):
                keep_max(0, 0, I)
            peeled(act, HP, lambda i: [body(2 * i + e, e) for e in range(2)])

        @block.gpsimd
        def _(pool):
            def weights_low(g):
                pool.wait_ge(wq_hi_ready, g + 1)
                pool.tensor_tensor(wq[1][:], wq_raw[:], wq[0][:].bitcast(F32), ALU.subtract)
                pool.tensor_tensor(wk[1][:, 0:NOPE], wk_raw[:], wk[0][:, 0:NOPE].bitcast(F32),
                                   ALU.subtract).then_inc(wq_ready, 1)

            def q_low(g, slot, c):
                cols = slice(c * 512, (c + 1) * 512)
                pool.wait_ge(q_hi_ready, NGRP * g + c + 1)
                pool.tensor_tensor(q[slot][1][0:QK, cols], q32[0:QK, c % 2, :], q[slot][0][0:QK, cols].bitcast(F32),
                                   ALU.subtract).then_inc(q_lo_ready, 1)

            def body(h, e):
                if exists(h + 1, H):
                    for c in range(NGRP):
                        q_low(h + 1, 1 - e, c)
                    if exists(h + 2, H):
                        weights_low(h + 2)
            for part in wk:
                pool.memset(part[:, NOPE:P].bitcast(F32), 0.0)
            pool.memset(v[:, :, :, VD:VW], 1.0).then_inc(filled, 1)
            weights_low(0)
            pool.wait_ge(wv_hi_ready, 1)
            pool.tensor_tensor(wv[1][:], wv_raw[:], wv[0][:].bitcast(F32), ALU.subtract).then_inc(wv_ready, 1)
            for c in range(NGRP):
                q_low(0, 0, c)
            weights_low(1)
            peeled(pool, HP, lambda i: [body(2 * i + e, e) for e in range(2)])

        @block.vector
        def _(dve):
            def prepare(g, slot, c):
                cols = slice(c * 512, (c + 1) * 512)
                dve.wait_ge(q_done, NGRP * g + c + 1)
                if exists(NGRP * g + c - 2, NGRP * H):
                    dve.wait_ge(q_lo_ready, NGRP * g + c - 1)
                if exists(NGRP * g + c - 1, NGRP * H):
                    dve.wait_ge(q32_ready, NGRP * g + c)
                dve.tensor_tensor(rot[NOPE:QK, :], ps_q[QK:P, :], rope[QK:P, cols], ALU.mult)
                dve.tensor_tensor(q32[0:QK, c % 2, :], ps_q[0:QK, :], rope[0:QK, cols], ALU.mult).then_inc(q_read, 1)
                dve.wait_ge(q_read, NGRP * g + c + 1)
                dve.tensor_tensor(q32[NOPE:QK, c % 2, :], q32[NOPE:QK, c % 2, :], rot[NOPE:QK, :], ALU.add).then_inc(q32_ready, 1)
                dve.wait_ge(k_hi_ready, NGRP * g + c + 1)
                dve.tensor_tensor(kk[slot][1][0:NOPE, cols], ps_k[0:NOPE, :], kk[slot][0][0:NOPE, cols].bitcast(F32),
                                  ALU.subtract).then_inc(k_kept, 1)

            def maxima(g, n):
                I, r, c = chunks[n]
                width = 512 if c < I else (r + 1) * P
                if r == 0 and c == 0 and exists(NGRP * g + I - 2, NGRP * H):
                    dve.wait_ge(negm_ready, NGRP * g + I - 1)
                dve.wait_ge(chunk_done, NCH * g + n + 1)
                dve.tensor_reduce(mx[:, I % 2, r, c:c + 1], ps_p[:, n % 2, 0:width], AX.X, ALU.max).then_inc(chunk_read, 1)
                if r == GRP - 1 and c == I:
                    dve.wait_ge(chunk_read, NCH * g + n + 1)
                    if exists(NGRP * g + I - 2, NGRP * H):
                        dve.wait_ge(m_turned, NGRP * g + I - 1)
                    dve.tensor_reduce(negm[:, I % 2, :], mx[:, I % 2, :, 0:I + 1], AX.X, ALU.max,
                                      negate=True).then_inc(negm_ready, 1)

            def finish(h, I, k):
                dve.wait_ge(pv_done, NT * h + k + 1)
                sums = ps_o[:, I % 2, 0:GRP * VW].rearrange("p (r c) -> p r c", r=GRP)
                dve.reciprocal(rec[:, I % 2, :].unsqueeze(2), sums[:, :, VD:VW]).then_inc(rec_ready, 1)
                dve.wait_ge(rec_ready, NGRP * h + I + 1)
                if exists(NGRP * h + I - 2, NGRP * H):
                    dve.wait_ge(att_out[I % 2], 16 * (2 * h + I // 2))
                dve.tensor_tensor(att[:, I % 2], sums[:, :, 0:VD], rec[:, I % 2, :].unsqueeze(2).broadcast_to([P, GRP, VD]),
                                  ALU.mult).then_inc(att_ready, 1)

            def body(h, e):
                for k in range(NT):
                    if exists(h + 1, H):
                        for what, n in side[k]:
                            if what == "prepare":
                                prepare(h + 1, 1 - e, n)
                            elif what == "maxima":
                                maxima(h + 1, n)
                    if k == 0 and exists(h - 1, H):
                        finish(h - 1, LASTG, NT - 1)
                    elif k and (k == NT or tiles[k][0] != tiles[k - 1][0]):
                        finish(h, tiles[k - 1][0], k - 1)
            for e in range(2):
                last = dve.memset(kk[e][0][QK:QK + 1, :].bitcast(F32), 1.0)
            last.then_inc(filled, 1)
            for c in range(NGRP):
                dve.wait_ge(lat_hi_ready, c + 1)
                dve.tensor_tensor(lat_lo[:, :, c * 512:(c + 1) * 512], lat_t[:, :, c * 512:(c + 1) * 512],
                                  lat_hi[:, :, c * 512:(c + 1) * 512].bitcast(F32), ALU.subtract).then_inc(lat_lo_ready, 1)
            for c in range(NGRP):
                dve.wait_ge(kr_hi_ready, c + 1)
                for e in range(2):
                    cols = slice(c * 512, (c + 1) * 512)
                    last = dve.tensor_tensor(kk[e][1][NOPE:QK, cols], (ps_s if c < 2 else ps_p)[0:ROPE, c % 2, :],
                                             kk[e][0][NOPE:QK, cols].bitcast(F32), ALU.subtract)
                last.then_inc(kr_kept, 1)
            dve.wait_ge(rope_in, 16)
            for c in range(NGRP):
                prepare(0, 0, c)
            for n in range(NCH):
                maxima(0, n)
            peeled(dve, HP, lambda i: [body(2 * i + e, e) for e in range(2)])
            finish(H - 1, LASTG, NT - 1)

        @block.tensor
        def _(pe):
            def prepare(g, slot, c):
                cols = slice(c * 512, (c + 1) * 512)
                pe.wait_ge(wq_ready, g + 1)
                if exists(NGRP * g + c - 1, NGRP * H):
                    pe.wait_ge(q_read, NGRP * g + c)
                for j in range(QC):
                    last = mm3(pe, ps_q[:], [wq[0][:, j, :], wq[1][:, j, :]], [lat_hi[:, j, cols], lat_lo[:, j, cols]],
                               j == 0, j == QC - 1)
                last.then_inc(q_done, 1)
                if exists(NGRP * g + c - 1, NGRP * H):
                    pe.wait_ge(k_kept, NGRP * g + c)
                if exists(g - 1, H):
                    pe.wait_ge(m_kept, NGRP * g)
                mm3(pe, ps_k[:], [wk[0][:], wk[1][:]], [lat_hi[:, QC, cols], lat_lo[:, QC, cols]],
                    True, True).then_inc(k_done, 1)

            def maxima(g, slot, n):
                I, r, c = chunks[n]
                width = 512 if c < I else (r + 1) * P
                at = (GRP * I + r) * P
                if r == 0 and c == 0:
                    pe.wait_ge(q_hi_ready, NGRP * g + I + 1)
                    pe.wait_ge(k_hi_ready, NGRP * g + I + 1)
                if exists(NCH * g + n - 2, NCH * H):
                    pe.wait_ge(chunk_read, NCH * g + n - 1)
                last = pe.matmul(ps_p[:, n % 2, 0:width], q[slot][0][0:QK, at:at + P],
                                 kk[slot][0][0:QK, c * 512:c * 512 + width], start=True, stop=(c < I))
                if c == I:
                    last = pe.matmul(ps_p[:, n % 2, width - P:width], identb[:], mask_q[:], start=False, stop=True)
                last.then_inc(chunk_done, 1)

            def turn(g, I):
                pe.wait_ge(negm_ready, NGRP * g + I + 1)
                pe.wait_ge(k_kept, NGRP * g + NGRP)
                if exists(NGRP * g + I - 1, NGRP * H):
                    pe.wait_ge(m_kept, NGRP * g + I)
                for r in range(GRP):
                    last = pe.transpose(ps_k[0:1, r * P:(r + 1) * P], negm[:, I % 2, r:r + 1], ident[:])
                last.then_inc(m_turned, 1)

            def scores(h, slot, k):
                I, j = tiles[k]
                c0, n = tile_cols(k)
                cols = slice(I * 512 + c0, (I + 1) * 512)
                keys = slice(j * P, (j + 1) * P)
                out = ps_s[:, k % 2, 0:n]
                if j == 0:
                    pe.wait_ge(m_kept, NGRP * h + I + 1)
                    if I == 0:
                        pe.wait_ge(q_lo_ready, NGRP * h + NGRP)
                if exists(NT * h + k - 2, NT * H):
                    pe.wait_ge(exp_done, NT * h + k - 1)
                pe.matmul(out, kk[slot][0][0:QK + 1, keys], q[slot][0][0:QK + 1, cols], start=True, stop=False)
                pe.matmul(out, kk[slot][0][0:QK, keys], q[slot][1][0:QK, cols], start=False, stop=False)
                last = pe.matmul(out, kk[slot][1][0:QK, keys], q[slot][0][0:QK, cols], start=False, stop=(j < GRP * I))
                if j >= GRP * I:
                    last = pe.matmul(ps_s[:, k % 2, 0:P], identb[:], mask_k[:], start=False, stop=True)
                last.then_inc(scores_done, 1)

            def values(h, k):
                I, j = tiles[k]
                c0, _ = tile_cols(k)
                pe.wait_ge(exp_done, NT * h + k + 1)
                if j == 0 and exists(NGRP * h + I - 2, NGRP * H):
                    pe.wait_ge(att_ready, NGRP * h + I - 1)
                for r in range(c0 // P, GRP):
                    last = pe.matmul(ps_o[:, I % 2, r * VW:(r + 1) * VW], pt[:, k % 4, r * P - c0:(r + 1) * P - c0],
                                     v[:, j, ds(h, 1), :].squeeze(1), start=(j == 0 and r == 0), stop=(j == GRP * I + r),
                                     skip_group_check=True)
                last.then_inc(pv_done, 1)

            def body(h, e):
                for k in range(NT):
                    scores(h, e, k)
                    if k == 1:
                        turn(h, LASTG)
                    if exists(h + 1, H):
                        for what, n in side[k]:
                            if what == "prepare":
                                prepare(h + 1, 1 - e, n)
                            elif what == "maxima":
                                maxima(h + 1, 1 - e, n)
                            else:
                                turn(h + 1, n)
                    if k:
                        values(h, k - 1)
                    elif exists(h - 1, H):
                        values(h - 1, NT - 1)
            pe.wait_ge(kr_in, 16)
            for n in range(NB):
                c = n // GRP
                last = pe.transpose((ps_s if c < 2 else ps_p)[0:ROPE, c % 2, (n % GRP) * P:(n % GRP + 1) * P], kr[:, n, :], ident[:])
                if n % GRP == GRP - 1:
                    last.then_inc(kr_turned, 1)
            pe.wait_ge(wv_ready, 1)
            pe.wait_ge(filled, 2)
            for n in range(NB):
                if n % GRP == 0:
                    pe.wait_ge(lat_lo_ready, n // GRP + 1)
                if n >= 2:
                    pe.wait_ge(v_kept, n - 1)
                cols = slice(n * P, (n + 1) * P)
                mm3(pe, ps_o[:, n % 2, :], [lat_hi[:, QC, cols], lat_lo[:, QC, cols]], [wv[0][:], wv[1][:]],
                    True, True).then_inc(v_done, 1)
            for c in range(NGRP):
                prepare(0, 0, c)
            pe.wait_ge(kr_kept, NGRP)
            for n in range(NCH):
                maxima(0, 0, n)
                if n + 1 < NCH and chunks[n + 1][0] != chunks[n][0]:
                    turn(0, chunks[n][0])
            pe.wait_ge(v_kept, NB)
            peeled(pe, HP, lambda i: [body(2 * i + e, e) for e in range(2)])
            values(H - 1, NT - 1)

    stay = Map(nc, after_lat)
    wo = [stay("wo_hi", [P, KC, D], F32R), stay("wo_lo", [P, KC, D], F32R)]
    ms = [stay("ms_hi", [P, KC, P], F32R), stay("ms_lo", [P, KC, P], F32R)]
    ck = [stay(f"ck{e}", [P, TPP, KVL], F32) for e in range(2)]
    cr = [stay(f"cr{e}", [P, TPP, ROPE], F32) for e in range(2)]
    wuv_s = stay("s_wuv", [P, DATT], F32)
    crow = stay("s_crow", [1, DB, KVL], F32)
    qabs = stay("s_qabs", [P, DB, H], F32)
    qr = stay("s_qr", [P, DB, GRP, H], F32)
    new_row = stay("s_new_row", [1, DB, H], F32)
    new_col = stay("s_new_col", [H, DB], F32)
    page_x = stay("s_page_x", [P, DB], U32)
    m2 = Map(nc, after_lat - 3 * S * 4)
    z = m2("s_z", [DB, DIN], F32)
    mixed = m2("s_mixed", [DB, D], F32)
    cache_in = [nc.alloc_semaphore("cache_in0"), nc.alloc_semaphore("cache_in1")]
    QT = TPP // GRP
    ckv_q = t["cache_ckv"].rearrange("a n (c s) k -> (a n c) (s k)", c=QTR)
    kr_q = t["cache_krope"].rearrange("a n (c s) k -> (a n c) (s k)", c=QTR)
    NQ = t["cache_ckv"].shape[1] * QTR

    def gather(pool, n, e):
        for tile, rows in ((ck[e], ckv_q), (cr[e], kr_q)):
            pool.indirect_dma_start(tile[:].rearrange("p s k -> p (s k)"), None, rows,
                                    bass.IndirectOffsetOnAxis(ap=page_x[:, n:n + 1], axis=0),
                                    bounds_check=NQ - 1, oob_is_err=True).then_inc(cache_in[e], 16)

    with ExitStack() as ctx:
        sems = []
        ctx.callback(release, nc, sems)

        def psum(name, shape):
            return ctx.enter_context(nc.psum_tensor("smp_" + name, shape, F32))

        def sem(name):
            return stage_semaphore(nc, sems, "smp_" + name)

        m = Map(nc, stay.at)
        wo_raw = m("wo_raw", [P, 2, D], F32)
        state = m("state", [DB, sum((2 << g) - 1 for g in range(NG)), P], F32)
        ms2 = Map(nc, m2.at)
        junk = ms2("s_junk", [DB, OFF_KR], F32)
        lat = ms2("s_lat", [DB, LA], F32)
        rot = ms2("s_rot", [DB, H, ROPE], F32)
        wsum = ms2("s_wsum", [DB, DPOOL], F32)
        assert ms2.at <= after_lat
        wuq_s = m("s_wuq", [P, QC, H * QK], F32)
        wuk_s = m("s_wuk", [P, H * NOPE], F32)
        wp_s = m("s_wpool", [P, NG, P], F32)
        rows = m("s_rows", [DB, 2, DPOOL], F32)
        qn_w = m("s_qn_w", [DB, QL + KVL], F32)
        tab = m("s_tab", [DB, 2, ROPE], F32)
        stat = m("s_stat", [DB, 2], F32)
        lat_c = m("s_lat_c", [P, 3, DB], F32)
        krt = m("s_krt", [ROPE, DB], F32)
        qrow = m("s_q", [DB, H, QK], F32)
        qn_c = m("s_qn_c", [NOPE, H, DB], F32)
        wuk_t = m("s_wuk_t", [NOPE, H, P], F32)
        page_i = m("s_page_i", [DB, NPG], I32)
        page_f = m("s_page_f", [DB, NPG], F32)
        page_c = m("s_page_c", [NPG, DB], F32)
        spread = m("s_spread", [NPG, P], F32)
        quarter = m("s_quarter", [P, 1], F32)
        pool_c = m("s_pool_c", [P, NG, DB], F32)
        ps_t = psum("ps_t", [P, 2, 512])
        ps_r = psum("ps_r", [P, 512])
        ps_s = psum("ps_s", [P, 2, 512])
        ps_m = psum("ps_m", [P, 512])
        ps_o = psum("ps_o", [P, 512])
        ps_a = psum("ps_a", [P, 512])

        z_in, tab_in, w_in2, state_in, page_in, crow_in = (
            sem("z_in"), sem("tab_in"), sem("w_in"), sem("state_in"), sem("page_in"), sem("crow_in"))
        wo_in = [sem("wo_in0"), sem("wo_in1")]
        page_turned = sem("page_turned")
        page_step, page_ready, ss_ready, var_ready, sd_ready, rot_step, lat_ready, kr_ready, silu_ready = (
            sem("page_step"), sem("page_ready"), sem("ss_ready"), sem("var_ready"), sem("sd_ready"), sem("rot_step"),
            sem("lat_ready"), sem("kr_ready"), sem("silu_ready"))
        setup_pe, setup_dve, out_done, zeroed = sem("setup_pe"), sem("setup_dve"), sem("out_done"), sem("zeroed")
        wo_hi_ready = sem("wo_hi_ready")
        wo_lo_ready = [sem("wo_lo_ready0"), sem("wo_lo_ready1")]
        w_out = t["w_out"].rearrange("a (c p) n -> p (a c) n", p=P)
        prev = t["state_pool"].rearrange("a b s c -> (a b) s c")
        u_col = LA + OFF_U
        block = ctx.enter_context(nc.Block())

        @block.sync
        def _(sp):
            sp.dma_start(page_i[:], t["page_table"]).then_inc(page_in, 16)
            sp.dma_start(spread[:], t["c_spread"]).then_inc(page_in, 16)
            sp.dma_start(quarter[:], t["c_quarter"]).then_inc(page_in, 16)
            sp.dma_start(z[:], zs_d).then_inc(z_in, 16)
            sp.dma_start(qn_w[:, 0:QL], t["q_norm_w"].rearrange("a n -> (a n)").partition_broadcast(DB)).then_inc(tab_in, 16)
            sp.dma_start(qn_w[:, QL:], t["kv_norm_w"].rearrange("a n -> (a n)").partition_broadcast(DB)).then_inc(tab_in, 16)
            sp.dma_start(tab[:], t["c_rope_sample"].rearrange("t b r -> b t r")).then_inc(tab_in, 16)
            sp.dma_start(rows[:, 0, :], t["b_pool"].rearrange("a g c -> (a g c)").partition_broadcast(DB)).then_inc(tab_in, 16)
            sp.dma_start(rows[:, 1, :], t["pool_scale"].rearrange("a c -> (a c)").partition_broadcast(DB)).then_inc(tab_in, 16)
            at = 0
            for g in range(NG):
                w = 2 << g
                sp.dma_start(state[:, at:at + w - 1, :], prev[:, PREV + 1 - w:, g * P:(g + 1) * P]).then_inc(state_in, 16)
                at += w - 1
            sp.dma_start(o[7].rearrange("a b s c -> (a b) s c")[:, 0:PREV - 1, :], prev[:, 1:, :]).then_inc(out_done, 16)
            sp.dma_start(o[7].rearrange("a b s c -> (a b) s c")[:, PREV - 1:, :],
                         zs_d[:, u_col:u_col + DPOOL].unsqueeze(1)).then_inc(out_done, 16)
            sp.wait_ge(lat_ready, 1)
            sp.dma_start(o[5].rearrange("a b s k -> (a b s) k"), lat[:, OFF_KV:OFF_KR]).then_inc(out_done, 16)
            sp.dma_start(o[6].rearrange("a b s k -> (a b s) k"), lat[:, OFF_KR:LA]).then_inc(out_done, 16)
            sp.wait_ge(out_done, 64)
            sp.dma_start(crow[:], o[5].rearrange("a b s k -> (a s) b k")).then_inc(crow_in, 16)
            sp.wait_ge(crow_in, 16)

        @block.gpsimd
        def _(pool):
            pool.wait_ge(page_ready, 1)
            gather(pool, 0, 0)
            gather(pool, 1, 1)
            pool.memset(qr[:], 0.0)
            for part in ms:
                last = pool.memset(part[:].bitcast(F32), 0.0)
            last.then_inc(zeroed, 1)
            for n in range(0, KC, 2):
                pool.wait_ge(wo_hi_ready, n + 1)
                pool.tensor_tensor(wo[1][:, n, :], wo_raw[:, n % 2, :], wo[0][:, n, :].bitcast(F32),
                                   ALU.subtract).then_inc(wo_lo_ready[0], 1)

        @block.scalar
        def _(act):
            def load(n):
                act.dma_start(wo_raw[:, n % 2, :], w_out[:, n, :]).then_inc(wo_in[n % 2], 16)
            act.dma_start(wuq_s[:], t["w_uq"].rearrange("a (c p) h d -> p (a c) (h d)", p=P)).then_inc(w_in2, 16)
            act.dma_start(wuk_s[:], t["w_uk"].rearrange("a k h d -> (a k) (h d)")).then_inc(w_in2, 16)
            act.dma_start(wuv_s[:], t["w_uv"].rearrange("a k h d -> (a k) (h d)")).then_inc(w_in2, 16)
            act.dma_start(wp_s[:], t["w_pool"].rearrange("a g c d -> c (a g) d")).then_inc(w_in2, 16)
            load(0)
            load(1)
            act.wait_ge(z_in, 16)
            act.activation(junk[:, 0:QL], z[:, 0:QL], ACT.Square, accum_out=stat[:, 0:1])
            act.activation(junk[:, OFF_KV:OFF_KR], z[:, OFF_KV:OFF_KR], ACT.Square, accum_out=stat[:, 1:2]).then_inc(ss_ready, 1)
            act.wait_ge(var_ready, 1)
            act.activation(stat[:], stat[:], ACT.Sqrt).then_inc(sd_ready, 1)
            act.activation(z[:, LA:LA + DATT], z[:, LA:LA + DATT], ACT.Silu)
            act.activation(z[:, LA + OFF_GP:DIN], z[:, LA + OFF_GP:DIN], ACT.Silu).then_inc(silu_ready, 1)
            for n in range(KC):
                act.wait_ge(wo_in[n % 2], 16 * (n // 2 + 1))
                act.activation(wo[0][:, n, :], wo_raw[:, n % 2, :], ACT.Copy).then_inc(wo_hi_ready, 1)
                if 1 <= n < KC - 1:
                    act.wait_ge(wo_lo_ready[(n - 1) % 2], (n - 1) // 2 + 1)
                    load(n + 1)

        @block.vector
        def _(dve):
            step = [0]

            def kept(ins):
                step[0] += 1
                ins.then_inc(setup_dve, 1)
                return step[0]

            def split(n):
                dve.wait_ge(wo_hi_ready, n + 1)
                dve.tensor_tensor(wo[1][:, n, :], wo_raw[:, n % 2, :], wo[0][:, n, :].bitcast(F32),
                                  ALU.subtract).then_inc(wo_lo_ready[1], 1)

            dve.wait_ge(page_in, 48)
            dve.tensor_copy(page_f[:], page_i[:]).then_inc(page_step, 1)
            dve.wait_ge(page_turned, 1)
            dve.tensor_copy(page_c[:], ps_o[0:NPG, 0:DB]).then_inc(page_step, 1)
            dve.wait_ge(page_turned, 2)
            dve.tensor_scalar(page_x[:], ps_o[:, DB:2 * DB], quarter[:], None, ALU.add).then_inc(page_ready, 1)
            dve.wait_ge(ss_ready, 1)
            dve.tensor_scalar(stat[:, 0:1], stat[:, 0:1], 1.0 / QL, EPS, ALU.mult, ALU.add)
            dve.tensor_scalar(stat[:, 1:2], stat[:, 1:2], 1.0 / KVL, EPS, ALU.mult, ALU.add).then_inc(var_ready, 1)
            dve.wait_ge(tab_in, 80)
            dve.tensor_tensor(lat[:, OFF_KR:LA], z[:, OFF_KR:LA], tab[:, 0, :], ALU.mult)
            dve.tensor_tensor(rot[:, 0, 0:16], z[:, OFF_KR + 16:LA], tab[:, 1, 0:16], ALU.mult)
            dve.tensor_tensor(rot[:, 0, 16:32], z[:, OFF_KR:OFF_KR + 16], tab[:, 1, 16:32], ALU.mult).then_inc(rot_step, 1)
            dve.wait_ge(rot_step, 1)
            dve.tensor_tensor(lat[:, OFF_KR:LA], lat[:, OFF_KR:LA], rot[:, 0, :], ALU.add).then_inc(rot_step, 1)
            dve.wait_ge(sd_ready, 1)
            dve.reciprocal(stat[:], stat[:]).then_inc(kr_ready, 1)
            dve.wait_ge(kr_ready, 1)
            dve.scalar_tensor_tensor(out=lat[:, 0:QL], in0=z[:, 0:QL], scalar=stat[:, 0:1], in1=qn_w[:, 0:QL],
                                     op0=ALU.mult, op1=ALU.mult)
            dve.scalar_tensor_tensor(out=lat[:, OFF_KV:OFF_KR], in0=z[:, OFF_KV:OFF_KR], scalar=stat[:, 1:2], in1=qn_w[:, QL:],
                                     op0=ALU.mult, op1=ALU.mult).then_inc(lat_ready, 1)
            dve.wait_ge(setup_pe, 1)
            dve.tensor_copy(lat_c[:], ps_m[:, 0:3 * DB].rearrange("p (c b) -> p c b", c=3))
            kept(dve.tensor_copy(krt[:], ps_m[0:ROPE, 3 * DB:4 * DB]))
            dve.wait_ge(setup_pe, 2)
            kept(dve.tensor_copy(qrow[:].rearrange("b h d -> b (h d)").rearrange("b (k n) -> b k n", k=2),
                                 ps_s[0:DB, :, 0:H * QK // 2]))
            dve.wait_ge(setup_dve, 2)
            dve.tensor_tensor(rot[:, :, 0:16], qrow[:, :, NOPE + 16:QK],
                              tab[:, 1, 0:16].unsqueeze(1).broadcast_to([DB, H, 16]), ALU.mult)
            kept(dve.tensor_tensor(rot[:, :, 16:32], qrow[:, :, NOPE:NOPE + 16],
                                   tab[:, 1, 16:32].unsqueeze(1).broadcast_to([DB, H, 16]), ALU.mult))
            dve.wait_ge(setup_dve, 3)
            kept(dve.tensor_tensor(qrow[:, :, NOPE:QK], qrow[:, :, NOPE:QK],
                                   tab[:, 0, :].unsqueeze(1).broadcast_to([DB, H, ROPE]), ALU.mult))
            dve.wait_ge(setup_dve, 4)
            kept(dve.tensor_tensor(qrow[:, :, NOPE:QK], qrow[:, :, NOPE:QK], rot[:], ALU.add))
            dve.wait_ge(setup_pe, 3)
            kept(dve.tensor_copy(wuk_t[:].rearrange("p h k -> p (h k)").rearrange("p (a n) -> p a n", a=2), ps_t[0:NOPE]))
            dve.wait_ge(setup_pe, 4)
            dve.tensor_copy(qn_c[:], ps_o[0:NOPE, 0:H * DB].rearrange("p (h b) -> p h b", h=H))
            dve.wait_ge(zeroed, 1)
            for g in range(GRP):
                last = dve.tensor_copy(qr[g * ROPE:(g + 1) * ROPE, :, g, :],
                                       ps_o[0:ROPE, H * DB:2 * H * DB].rearrange("p (h b) -> p b h", h=H))
            kept(last)
            dve.wait_ge(setup_pe, 5)
            kept(dve.tensor_copy(qabs[:], ps_m[:, 0:H * DB].rearrange("p (h b) -> p b h", h=H)))
            dve.wait_ge(setup_pe, 6)
            dve.tensor_copy(new_row[:], ps_a[0:1, 0:DB * H].rearrange("p (b h) -> p b h", b=DB))
            kept(dve.tensor_copy(new_col[:], ps_r[0:H, 0:DB]))

            split(1)
            dve.wait_ge(state_in, 16 * NG)
            u = z[:, u_col:u_col + DPOOL]
            at = 0
            for g in range(NG):
                w = 2 << g
                cols = slice(g * P, (g + 1) * P)
                last = dve.tensor_reduce(wsum[:, cols], state[:, at:at + w - 1, :].rearrange("b s c -> b c s"), AX.X, ALU.add)
                at += w - 1
            kept(last)
            dve.wait_ge(setup_dve, 10)
            kept(dve.tensor_tensor(wsum[:], wsum[:], u, ALU.add))
            dve.wait_ge(setup_dve, 11)
            for g in range(NG):
                cols = slice(g * P, (g + 1) * P)
                last = dve.scalar_tensor_tensor(out=wsum[:, cols], in0=wsum[:, cols], scalar=1.0 / (2 << g), in1=u[:, cols],
                                                op0=ALU.mult, op1=ALU.subtract)
            kept(last)
            split(3)
            dve.wait_ge(setup_pe, 7)
            kept(dve.tensor_copy(pool_c[:], ps_a[:, 0:NG * DB].rearrange("p (g b) -> p g b", g=NG)))
            dve.wait_ge(setup_pe, 8)
            kept(dve.tensor_tensor(mixed[:, DATT:], ps_a[0:DB, :], rows[:, 0, :], ALU.add))
            dve.wait_ge(setup_dve, 14)
            kept(dve.tensor_tensor(mixed[:, DATT:], mixed[:, DATT:], rows[:, 1, :], ALU.mult))
            dve.wait_ge(setup_dve, 15)
            dve.wait_ge(silu_ready, 1)
            kept(dve.tensor_tensor(mixed[:, DATT:], mixed[:, DATT:], z[:, LA + OFF_GP:DIN], ALU.mult))
            split(5)
            split(7)

        @block.tensor
        def _(pe):
            pe.wait_ge(page_step, 1)
            pe.transpose(ps_o[0:NPG, 0:DB], page_f[:], ident[0:DB, 0:DB]).then_inc(page_turned, 1)
            pe.wait_ge(page_step, 2)
            pe.matmul(ps_o[:, DB:2 * DB], spread[:], page_c[:], start=True, stop=True).then_inc(page_turned, 1)
            pe.wait_ge(lat_ready, 1)
            for c in range(3):
                pe.transpose(ps_m[:, c * DB:(c + 1) * DB], lat[:, c * P:(c + 1) * P], ident[0:DB, 0:DB])
            pe.transpose(ps_m[0:ROPE, 3 * DB:4 * DB], lat[:, OFF_KR:LA], ident[0:DB, 0:DB]).then_inc(setup_pe, 1)
            pe.wait_ge(w_in2, 64)
            pe.wait_ge(setup_dve, 1)
            for k in range(2):
                for c in range(QC):
                    last = pe.matmul(ps_s[0:DB, k, 0:H * QK // 2], lat_c[:, c, :],
                                     wuq_s[:, c, k * H * QK // 2:(k + 1) * H * QK // 2], start=(c == 0), stop=(c == QC - 1))
            last.then_inc(setup_pe, 1)
            for h in range(H):
                last = pe.transpose(ps_t[0:NOPE, h // 4, (h % 4) * P:(h % 4 + 1) * P], wuk_s[:, h * NOPE:(h + 1) * NOPE], ident[:])
            last.then_inc(setup_pe, 1)
            pe.wait_ge(setup_dve, 5)
            for h in range(H):
                pe.transpose(ps_o[0:NOPE, h * DB:(h + 1) * DB], qrow[:, h, 0:NOPE], ident[0:DB, 0:DB])
                last = pe.transpose(ps_o[0:ROPE, (H + h) * DB:(H + h + 1) * DB], qrow[:, h, NOPE:QK], ident[0:DB, 0:DB])
            last.then_inc(setup_pe, 1)
            pe.wait_ge(setup_dve, 7)
            for h in range(H):
                last = pe.matmul(ps_m[:, h * DB:(h + 1) * DB], wuk_t[:, h, :], qn_c[:, h, :], start=True, stop=True)
            last.then_inc(setup_pe, 1)
            pe.wait_ge(setup_dve, 8)
            for n in range(DB):
                pe.matmul(ps_a[0:1, n * H:(n + 1) * H], lat_c[:, QC, n:n + 1], qabs[:, n, :], start=True, stop=False)
                pe.matmul(ps_a[0:1, n * H:(n + 1) * H], krt[:, n:n + 1], qr[0:ROPE, n, 0, :], start=False, stop=True)
                pe.matmul(ps_r[0:H, n:n + 1], qabs[:, n, :], lat_c[:, QC, n:n + 1], start=True, stop=False)
                last = pe.matmul(ps_r[0:H, n:n + 1], qr[0:ROPE, n, 0, :], krt[:, n:n + 1], start=False, stop=True)
            last.then_inc(setup_pe, 1)
            pe.wait_ge(setup_dve, 12)
            for g in range(NG):
                last = pe.transpose(ps_a[:, g * DB:(g + 1) * DB], wsum[:, g * P:(g + 1) * P], ident[0:DB, 0:DB])
            last.then_inc(setup_pe, 1)
            pe.wait_ge(setup_dve, 13)
            for g in range(NG):
                last = pe.matmul(ps_a[0:DB, g * P:(g + 1) * P], pool_c[:, g, :], wp_s[:, g, :], start=True, stop=True)
            last.then_inc(setup_pe, 1)


    ITEMS = [("r", 0), ("t", 0), ("t", 1), ("t", 2), ("t", 3), ("r", 1), ("t", 4), ("t", 5), ("t", 6), ("t", 7)]
    NI = len(ITEMS)
    assert QT == 8 and NI % 2 == 0 and NB == 2 * DB
    item_of = {n: j for j, (what, n) in enumerate(ITEMS) if what == "t"}

    def scored_before(j):
        what, n = ITEMS[j]
        if what == "r":
            return QT // 2 * n
        return max([g + 1 for g, i in item_of.items() if i < j and i % 2 == j % 2] +
                   [g + 1 - QT for g, i in item_of.items() if i > j and i % 2 == j % 2])

    UNITS = 4 * KC
    HU = UNITS // 2
    with ExitStack() as ctx:
        sems = []
        ctx.callback(release, nc, sems)

        def psum(name, shape):
            return ctx.enter_context(nc.psum_tensor("out_" + name, shape, F32))

        def sem(name):
            return stage_semaphore(nc, sems, "out_" + name)

        mo2 = Map(nc, m2.at)
        gs = mo2("out_gate_s", [DB, D], F32)
        crt = mo2("crt", [P, 512], F32)
        pr = [mo2(f"pr{e}", [P, TPP + 1, H], F32) for e in range(2)]
        mx8 = mo2("s_mx8", [P, 2, H], F32)
        negm = mo2("s_negm", [H, 2], F32)
        diag = mo2("s_diag", [H, 2, H], F32)
        crow_s = mo2("s_crow_s", [1, 2, KVL], F32)
        negb = mo2("s_negb", [P, 2, H], F32)
        dsum = mo2("s_dsum", [P, 2, H], F32)
        rec = mo2("s_rec", [P, 2, H], F32)
        olat = mo2("s_olat", [P, H, DB], F32)
        assert mo2.at <= after_lat
        m = Map(nc, stay.at)
        ckt = m("ckt", [P, 2, 512], F32)
        gate = m("gate", [P, D], F32)
        fn_w = m("fn_w", [P, D], F32)
        ar = [m(f"att_rows{b}", [P, DATT], F32) for b in range(2)]
        ga = [m(f"gate_rows{b}", [P, DATT], F32) for b in range(2)]
        pc = [m(f"pool_cols{b}", [P, NG, P], F32) for b in range(2)]
        xr = [m(f"x_rows{b}", [P, D], F32) for b in range(2)]
        mh = [m(f"mixed_hi{b}", [P, KC, P], F32R) for b in range(2)]
        ml = [m(f"mixed_lo{b}", [P, KC, P], F32R) for b in range(2)]
        y = [m(f"y{b}", [P, D], F32) for b in range(2)]
        junk = m("out_junk", [P, 2, D], BF16)
        stat = m("out_stat", [P, 2], F32)
        ps_t = psum("ps_t", [P, 512])
        ps_y = psum("ps_y", [P, 2, 512])
        ps_c = psum("ps_c", [P, 2, 512])
        ps_s = psum("ps_s", [P, 512])
        ps_m = psum("ps_m", [P, 512])
        ps_o = psum("ps_o", [P, 512])
        tab_in, gs_in = sem("tab_in"), sem("gs_in")
        r_in = [sem("rows_in0"), sem("rows_in1")]
        x_in = [sem("x_in0"), sem("x_in1")]
        gated, turned, hi_ready, lo_att, lo_pool = sem("gated"), sem("turned"), sem("hi_ready"), sem("lo_att"), sem("lo_pool")
        half_done, y_sum, ss_ready, var_ready, sd_ready, r_ready, y_ready = (
            sem("half_done"), sem("y_sum"), sem("ss_ready"), sem("var_ready"), sem("sd_ready"), sem("r_ready"), sem("y_ready"))
        y_out = [sem("y_out0"), sem("y_out1")]
        piece_turned, piece_kept, scored = sem("piece_turned"), [sem("piece_kept0"), sem("piece_kept1")], sem("scored")
        mx_ready, mx_turned, negm_ready, diag_ready, negb_done, negb_ready = (
            sem("mx_ready"), sem("mx_turned"), sem("negm_ready"), sem("diag_ready"), sem("negb_done"), sem("negb_ready"))
        shifted, exp_ready, dsum_ready, pv_done, rec_ready, olat_ready = (
            sem("shifted"), sem("exp_ready"), sem("dsum_ready"), sem("pv_done"), sem("rec_ready"), sem("olat_ready"))
        fin_pe, fin_dve = sem("fin_pe"), sem("fin_dve")
        att_blocks = att_d.rearrange("(n p) e -> p n e", p=P)
        pool_cols = pool_d.rearrange("g p s -> p g s")
        y_blocks = o[0].rearrange("a (n p) d -> p (a n) d", p=P)
        block = ctx.enter_context(nc.Block())

        @block.sync
        def _(sp):
            def load(n, b):
                sp.dma_start(ar[b][:].unsqueeze(1), att_blocks[:, ds(n, 1), :]).then_inc(r_in[b], 16)
                sp.dma_start(ga[b][:].unsqueeze(1), gate_att_blocks[:, ds(n, 1), :]).then_inc(r_in[b], 16)
                sp.dma_start(pc[b][:], pool_cols[:, :, ds(n * P, P)]).then_inc(r_in[b], 16)

            def load_x(n, b):
                sp.dma_start(xr[b][:].unsqueeze(1), x_blocks[:, ds(n, 1), :]).then_inc(x_in[b], 16)

            def body(i):
                for b in range(2):
                    n = 2 * i + b
                    if exists(n + 2, NB):
                        sp.wait_ge(lo_pool, n + 1)
                        sp.wait_ge(turned, n + 1)
                        load(n + 2, b)
                        sp.wait_ge(y_sum, 3 * n + 3)
                        load_x(n + 2, b)
            for b in range(2):
                load(b, b)
            sp.dma_start(gate[:], mod_d[DB, 2 * D:].partition_broadcast(P)).then_inc(tab_in, 16)
            sp.dma_start(fn_w[:], t["final_norm_w"].partition_broadcast(P)).then_inc(tab_in, 16)
            for b in range(2):
                load_x(b, b)
            sp.dma_start(gs[:], mod_d[0:DB, 2 * D:]).then_inc(gs_in, 16)
            peeled(sp, DB, body)
            sp.wait_ge(y_sum, 3 * NB - 3)
            sp.dma_start(xr[0][0:DB, :], t["x_sample"].rearrange("b s d -> (b s) d")).then_inc(x_in[0], 16)
            sp.wait_ge(y_ready, NB + 1)
            sp.dma_start(o[1].rearrange("b s d -> (b s) d"), y[0][0:DB, :]).then_inc(y_out[0], 16)
            sp.wait_ge(y_out[0], 16 * (DB + 1))
            sp.wait_ge(y_out[1], 16 * DB)

        @block.scalar
        def _(act):
            def high(n, b):
                act.wait_ge(turned, n + 1)
                if exists(n - 2, NB):
                    act.wait_ge(half_done, 2 * n - 2)
                act.activation(mh[b][:, 0:GRP, :], ps_t[:].rearrange("p (c s) -> p c s", c=GRP), ACT.Copy)
                act.activation(mh[b][:, GRP:, :], pc[b][:], ACT.Copy).then_inc(hi_ready, 1)

            def squares(n, b, rows):
                act.wait_ge(y_sum, 3 * n + 3)
                act.activation(junk[0:rows, b, :], y[b][0:rows, :], ACT.Square, accum_out=stat[0:rows, b:b + 1]).then_inc(ss_ready, 1)

            def root(n, b, rows):
                act.wait_ge(var_ready, n + 1)
                act.activation(stat[0:rows, b:b + 1], stat[0:rows, b:b + 1], ACT.Sqrt).then_inc(sd_ready, 1)

            def store(n, b):
                act.wait_ge(y_ready, n + 1)
                act.dma_start(y_blocks[:, ds(n, 1), :], y[b][:].unsqueeze(1)).then_inc(y_out[b], 16)

            def keep(s, j):
                act.wait_ge(piece_turned, NI * s + j + 1)
                if scored_before(j) > 0 or exists(s - 1, DB):
                    act.wait_ge(scored, QT * s + scored_before(j))
                act.activation(crt[:] if ITEMS[j][0] == "r" else ckt[:, 0, :], ps_c[:, 0, :], ACT.Copy).then_inc(piece_kept[0], 1)

            def body(i, e):
                for u in range(UNITS):
                    b, v = divmod(u, HU)
                    n = 2 * i + b
                    if v == 2 and exists(n - 1, NB):
                        squares(n - 1, 1 - b, P)
                    if v == 3 and exists(n - 1, NB):
                        root(n - 1, 1 - b, P)
                    if v == 6 and exists(n - 1, NB):
                        store(n - 1, 1 - b)
                    if v == 8 and exists(n + 1, NB):
                        high(n + 1, 1 - b)
                    if u % 4 == 1 and u // 2 < NI:
                        keep(i, u // 2)
                    if u == 27:
                        act.wait_ge(shifted, i + 1)
                        act.activation(crow_s[:, e, :], crow[:, ds(i, 1), :].squeeze(1), ACT.Copy)
                        act.activation(pr[e][:, 0:TPP, :], pr[e][:, 0:TPP, :], ACT.Exp, scale=SCALE)
                        act.activation(pr[e][0:1, TPP, :], pr[e][0:1, TPP, :], ACT.Exp, scale=SCALE).then_inc(exp_ready, 1)
            high(0, 0)
            peeled(act, DB // 2, lambda i: [body(2 * i + e, e) for e in range(2)])
            squares(NB - 1, 1, P)
            root(NB - 1, 1, P)
            store(NB - 1, 1)
            squares(NB, 0, DB)
            root(NB, 0, DB)

        @block.gpsimd
        def _(pool):
            def gated_rows(n, b):
                pool.wait_ge(r_in[b], 24 * (n - b) + 48)
                pool.tensor_tensor(ar[b][:], ar[b][:], ga[b][:], ALU.mult).then_inc(gated, 1)

            def low(n, b):
                pool.wait_ge(hi_ready, n + 1)
                pool.tensor_tensor(ml[b][:, GRP:, :], pc[b][:], mh[b][:, GRP:, :].bitcast(F32), ALU.subtract).then_inc(lo_pool, 1)

            for b in range(2):
                gated_rows(b, b)
            low(0, 0)
            for n in range(NB):
                s = n // 2
                if n % 2 == 0 and 1 <= s < DB - 1:
                    pool.wait_ge(cache_in[(s + 1) % 2], 16 * (s - 1 - (s - 1) % 2) + 32)
                    pool.wait_ge(pv_done, s)
                    gather(pool, s + 1, (s + 1) % 2)
                if n + 1 < NB:
                    low(n + 1, (n + 1) % 2)
                if n + 2 < NB:
                    gated_rows(n + 2, n % 2)

        @block.vector
        def _(dve):
            def low(n, b):
                dve.wait_ge(hi_ready, n + 1)
                dve.tensor_tensor(ml[b][:, 0:GRP, :], ps_t[:].rearrange("p (c s) -> p c s", c=GRP),
                                  mh[b][:, 0:GRP, :].bitcast(F32), ALU.subtract).then_inc(lo_att, 1)

            def gate_half(n, b, k, rows, g_rows):
                dve.wait_ge(half_done, 2 * n + k + 1)
                if k == 0 and exists(n - 2, NB):
                    dve.wait_ge(y_out[b], 8 * (n - b))
                cols = slice(k * 512, (k + 1) * 512)
                dve.tensor_tensor(y[b][0:rows, cols], ps_y[0:rows, k, :], g_rows[:, cols], ALU.mult).then_inc(y_sum, 1)

            def add_x(n, b, rows):
                dve.wait_ge(x_in[b], 8 * (n - b) + 16)
                dve.wait_ge(y_sum, 3 * n + 2)
                dve.tensor_tensor(y[b][0:rows, :], y[b][0:rows, :], xr[b][0:rows, :], ALU.add).then_inc(y_sum, 1)

            def variance(n, b, rows):
                dve.wait_ge(ss_ready, n + 1)
                dve.tensor_scalar(stat[0:rows, b:b + 1], stat[0:rows, b:b + 1], 1.0 / D, EPS, ALU.mult, ALU.add).then_inc(var_ready, 1)

            def normalise(n, b, rows):
                dve.wait_ge(sd_ready, n + 1)
                dve.reciprocal(stat[0:rows, b:b + 1], stat[0:rows, b:b + 1]).then_inc(r_ready, 1)
                dve.wait_ge(r_ready, n + 1)
                dve.scalar_tensor_tensor(out=y[b][0:rows, :], in0=y[b][0:rows, :], scalar=stat[0:rows, b:b + 1], in1=fn_w[0:rows, :],
                                         op0=ALU.mult, op1=ALU.mult).then_inc(y_ready, 1)

            def keep(s, j):
                dve.wait_ge(piece_turned, NI * s + j + 1)
                if scored_before(j) > 0 or exists(s - 1, DB):
                    dve.wait_ge(scored, QT * s + scored_before(j))
                dve.tensor_copy(crt[:] if ITEMS[j][0] == "r" else ckt[:, 1, :], ps_c[:, 1, :]).then_inc(piece_kept[1], 1)

            def tile_maxima(s, e):
                dve.wait_ge(scored, QT * s + QT)
                dve.tensor_reduce(mx8[:, e, :], ps_s[:, 0:TPP * H].rearrange("p (t h) -> p h t", h=H),
                                  AX.X, ALU.max).then_inc(mx_ready, 1)

            def head_maxima(s, e):
                dve.wait_ge(mx_turned, s + 1)
                dve.tensor_reduce(negm[:, e:e + 1], ps_m[0:H, 0:P], AX.X, ALU.max).then_inc(negm_ready, 1)
                dve.wait_ge(negm_ready, 2 * s + 1)
                dve.tensor_tensor(negm[:, e:e + 1], negm[:, e:e + 1], new_col[:, ds(s, 1)], ALU.max).then_inc(negm_ready, 1)
                dve.wait_ge(negm_ready, 2 * s + 2)
                dve.tensor_scalar(diag[:, e, :], ident[0:H, 0:H], negm[:, e:e + 1], -1.0, ALU.mult, ALU.mult).then_inc(diag_ready, 1)

            def shift(s, e):
                dve.wait_ge(negb_done, s + 1)
                dve.tensor_copy(negb[:, e, :], ps_m[:, P:P + H]).then_inc(negb_ready, 1)
                dve.wait_ge(negb_ready, s + 1)
                if exists(s - 2, DB):
                    dve.wait_ge(pv_done, s - 1)
                dve.tensor_tensor(pr[e][:, 0:TPP, :], ps_s[:, 0:TPP * H].rearrange("p (t h) -> p t h", h=H),
                                  negb[:, e, :].unsqueeze(1).broadcast_to([P, TPP, H]), ALU.add)
                dve.tensor_tensor(pr[e][0:1, TPP:TPP + 1, :], new_row[:, ds(s, 1), :], negb[0:1, e, :].unsqueeze(1),
                                  ALU.add).then_inc(shifted, 1)

            def denominators(s, e):
                dve.wait_ge(exp_ready, s + 1)
                dve.tensor_reduce(dsum[:, e, :], pr[e][:, 0:TPP, :].rearrange("p t h -> p h t"), AX.X, ALU.add).then_inc(dsum_ready, 1)

            def divide(s, e):
                dve.wait_ge(pv_done, s + 1)
                dve.reciprocal(rec[:, e, :], ps_o[:, H:2 * H]).then_inc(rec_ready, 1)
                dve.wait_ge(rec_ready, s + 1)
                dve.tensor_tensor(olat[:, :, ds(s, 1)], ps_o[:, 0:H].unsqueeze(2), rec[:, e, :].unsqueeze(2),
                                  ALU.mult).then_inc(olat_ready, 1)

            def body(i, e):
                for u in range(UNITS):
                    b, v = divmod(u, HU)
                    n = 2 * i + b
                    if v == 1 and exists(n - 1, NB):
                        gate_half(n - 1, 1 - b, 1, P, gate)
                        add_x(n - 1, 1 - b, P)
                    if v == 3 and exists(n - 1, NB):
                        variance(n - 1, 1 - b, P)
                    if v == 4 and exists(n - 1, NB):
                        normalise(n - 1, 1 - b, P)
                    if v == 9 and exists(n + 1, NB):
                        low(n + 1, 1 - b)
                    if v == 10:
                        gate_half(n, b, 0, P, gate)
                    if u % 4 == 3 and u // 2 < NI:
                        keep(i, u // 2)
                    if u == 10 and exists(i - 1, DB):
                        divide(i - 1, 1 - e)
                    if u == 22:
                        tile_maxima(i, e)
                    if u == 24:
                        head_maxima(i, e)
                    if u == 26:
                        shift(i, e)
                    if u == 28:
                        denominators(i, e)
            low(0, 0)
            dve.wait_ge(tab_in, 32)
            dve.wait_ge(gs_in, 16)
            peeled(dve, DB // 2, lambda i: [body(2 * i + e, e) for e in range(2)])
            gate_half(NB - 1, 1, 1, P, gate)
            divide(DB - 1, 1)
            dve.wait_ge(fin_pe, 1)
            dve.tensor_tensor(mixed[:, 0:DATT], ps_c[0:DB, 0, :], z[:, LA:LA + DATT], ALU.mult).then_inc(fin_dve, 1)
            dve.wait_ge(fin_pe, 2)
            split = ps_m[:, 0:KC * DB].rearrange("p (c b) -> p c b", c=KC)
            dve.tensor_copy(ms[0][:, :, 0:DB], split).then_inc(fin_dve, 1)
            dve.wait_ge(fin_dve, 2)
            dve.tensor_tensor(ms[1][:, :, 0:DB], split, ms[0][:, :, 0:DB].bitcast(F32), ALU.subtract).then_inc(fin_dve, 1)
            add_x(NB - 1, 1, P)
            variance(NB - 1, 1, P)
            normalise(NB - 1, 1, P)
            for k in range(2):
                gate_half(NB, 0, k, DB, gs)
            add_x(NB, 0, DB)
            variance(NB, 0, DB)
            normalise(NB, 0, DB)

        @block.tensor
        def _(pe):
            def turn(n, b):
                pe.wait_ge(gated, n + 1)
                if exists(n - 1, NB):
                    pe.wait_ge(lo_att, n)
                for c in range(GRP):
                    last = pe.transpose(ps_t[:, c * P:(c + 1) * P], ar[b][:, c * P:(c + 1) * P], ident[:])
                last.then_inc(turned, 1)

            def unit(n, part, v):
                k, c = divmod(v, KC)
                if c == 0 and exists(n - 1, NB + 1):
                    pe.wait_ge(y_sum, 3 * n - 2 + k)
                cols = slice(k * 512, (k + 1) * 512)
                last = mm3(pe, ps_y[:, k, :], [part[0][:, c, :], part[1][:, c, :]],
                           [wo[0][:, c, cols], wo[1][:, c, cols]], c == 0, c == KC - 1)
                if c == KC - 1:
                    last.then_inc(half_done, 1)

            def turn_piece(s, e, j):
                what, g = ITEMS[j]
                if j == 0:
                    pe.wait_ge(cache_in[e], 16 * (s - e) + 32)
                if j >= 2 or exists(s - 1, DB):
                    pe.wait_ge(piece_kept[j % 2], NI // 2 * s + j // 2)
                for k in range(GRP):
                    rows = (ck[e][:, g * GRP + k, :] if what == "t" else
                            cr[e][:, (g * QT // 2 + k) * GRP:(g * QT // 2 + k + 1) * GRP, :].rearrange("p g r -> p (g r)"))
                    last = pe.transpose(ps_c[:, j % 2, k * P:(k + 1) * P], rows, ident[:])
                last.then_inc(piece_turned, 1)

            def score(s, g):
                j = item_of[g]
                k = g % (QT // 2)
                if g == 0 and exists(s - 1, DB):
                    pe.wait_ge(shifted, s)
                if k == 0:
                    r = ITEMS.index(("r", g // (QT // 2)))
                    pe.wait_ge(piece_kept[r % 2], NI // 2 * s + r // 2 + 1)
                pe.wait_ge(piece_kept[j % 2], NI // 2 * s + j // 2 + 1)
                at = g * GRP * H
                pe.matmul(ps_s[:, at:at + GRP * H], crt[:, k * P:(k + 1) * P], qr[:, ds(s, 1), :, :].squeeze(1),
                          start=True, stop=False, skip_group_check=True)
                for x in range(GRP):
                    last = pe.matmul(ps_s[:, at + x * H:at + (x + 1) * H], ckt[:, j % 2, x * P:(x + 1) * P],
                                     qabs[:, ds(s, 1), :].squeeze(1), start=False, stop=(x == GRP - 1), skip_group_check=True)
                last.then_inc(scored, 1)

            def values(s, e, g):
                if g == 0:
                    pe.wait_ge(dsum_ready, s + 1)
                    if exists(s - 1, DB):
                        pe.wait_ge(olat_ready, s)
                for k in range(g * GRP, (g + 1) * GRP):
                    pe.matmul(ps_o[:, 0:H], ck[e][:, k, :], pr[e][:, k, :], start=(k == 0), stop=False)

            def new_value(s, e):
                pe.matmul(ps_o[:, 0:H], crow_s[:, e, :], pr[e][0:1, TPP, :], start=False, stop=True)
                pe.matmul(ps_o[:, H:2 * H], ones[:], dsum[:, e, :], start=True, stop=False)
                pe.matmul(ps_o[:, H:2 * H], ones[0:1, :], pr[e][0:1, TPP, :], start=False, stop=True).then_inc(pv_done, 1)

            def body(i, e):
                for u in range(UNITS):
                    b, v = divmod(u, HU)
                    n = 2 * i + b
                    if v == 0:
                        pe.wait_ge(lo_att, n + 1)
                        pe.wait_ge(lo_pool, n + 1)
                    unit(n, [mh[b], ml[b]], v)
                    if v == 6 and exists(n + 1, NB):
                        turn(n + 1, 1 - b)
                    if exists(i - 1, DB):
                        if u < QT:
                            values(i - 1, 1 - e, u)
                        if u == QT:
                            new_value(i - 1, 1 - e)
                    if u % 2 == 1:
                        j = u // 2
                        if j < NI:
                            turn_piece(i, e, j)
                        if 0 < j <= NI and ITEMS[j - 1][0] == "t":
                            score(i, ITEMS[j - 1][1])
                    if u == 23:
                        if exists(i - 1, DB):
                            pe.wait_ge(negb_ready, i)
                        pe.wait_ge(mx_ready, i + 1)
                        pe.transpose(ps_m[0:H, 0:P], mx8[:, e, :], ident[:]).then_inc(mx_turned, 1)
                    if u == 25:
                        pe.wait_ge(diag_ready, i + 1)
                        pe.matmul(ps_m[:, P:P + H], ones[0:H, :], diag[:, e, :], start=True, stop=True).then_inc(negb_done, 1)
            turn(0, 0)
            peeled(pe, DB // 2, lambda i: [body(2 * i + e, e) for e in range(2)])
            for g in range(QT):
                values(DB - 1, 1, g)
            new_value(DB - 1, 1)
            pe.wait_ge(olat_ready, DB)
            for h in range(H):
                last = pe.matmul(ps_c[0:DB, 0, h * VD:(h + 1) * VD], olat[:, h, :], wuv_s[:, h * VD:(h + 1) * VD], start=True, stop=True)
            last.then_inc(fin_pe, 1)
            pe.wait_ge(fin_dve, 1)
            for c in range(KC):
                last = pe.transpose(ps_m[:, c * DB:(c + 1) * DB], mixed[:, c * P:(c + 1) * P], ident[0:DB, 0:DB])
            last.then_inc(fin_pe, 1)
            pe.wait_ge(fin_dve, 3)
            for v in range(2 * KC):
                unit(NB, ms, v)




_INS = ["x_prompt", "x_sample", "c_prompt", "c_sample", "cache_ckv", "cache_krope", "state_pool", "page_table",
        "ada_w", "ada_b", "norm_w", "w_in", "q_norm_w", "w_uq", "kv_norm_w", "w_uk", "w_uv",
        "w_pool", "b_pool", "pool_scale", "w_out", "final_norm_w"]
_OUTS = [(1, S, D), (DB, 1, D), (1, 1, S, KVL), (1, 1, S, ROPE), (1, 1, PREV, DPOOL),
         (1, DB, 1, KVL), (1, DB, 1, ROPE), (1, DB, PREV, DPOOL)]


def _constants():
    f32 = np.float32
    inv = (f32(10000.0) ** (-np.arange(0, ROPE, 2, dtype=f32) / f32(ROPE))).astype(f32)

    def tables(pos):
        ang = (pos.astype(f32)[:, None] * inv[None, :]).astype(f32).astype(np.float64)
        cos, sin = np.cos(ang).astype(f32), np.sin(ang).astype(f32)
        return np.concatenate([cos, cos], 1), np.concatenate([-sin, sin], 1)

    cos, sin = tables(np.arange(S))
    cos_s, sin_s = tables(np.full(DB, NPG * PG))
    tok = np.arange(P)
    late = np.where(tok[None, :] <= tok[:, None], 0.0, MASKED)
    windows = 2 ** (np.arange(NG) + 1)
    return {
        "c_ident": np.eye(P, dtype=f32),
        "c_mask_q": late.astype(f32),
        "c_mask_k": np.ascontiguousarray(late.T).astype(f32),
        "c_rope_rows": np.ascontiguousarray(np.stack([cos, sin]).reshape(2, NB, P, ROPE).transpose(0, 2, 1, 3)),
        "c_rope_cols": np.ascontiguousarray(np.concatenate([np.ones((NOPE, S), f32), cos.T, sin.T])),
        "c_rope_sample": np.stack([cos_s, sin_s]),
        "c_count": (1.0 / np.minimum(tok[None, :16] + 1.0, windows[:, None])).astype(f32),
        "c_spread": np.where(tok[None, :] // QTR == np.arange(NPG)[:, None], float(QTR), 0.0).astype(f32),
        "c_quarter": (tok % QTR).astype(f32)[:, None],
    }


def kernel(**inputs):
    import numpy as _np
    import concourse.bacc as _bacc
    from concourse import mybir as _mybir
    from concourse.bass_utils import run_bass_kernel_spmd as _run

    nc = _bacc.Bacc("TRN2", target_bir_lowering=False, num_devices=1)
    arrays, tensors = {}, {}
    data = {name: _np.ascontiguousarray(inputs[name]) for name in _INS}
    data.update(_constants())
    for name, a in data.items():
        arrays[f"in_{name}_dram"] = a
        tensors[name] = nc.dram_tensor(f"in_{name}_dram", a.shape, _mybir.dt.from_np(a.dtype), kind="ExternalInput").ap()
    outs = [nc.dram_tensor(f"out_{i}_dram", shape, _mybir.dt.float32, kind="ExternalOutput").ap()
            for i, shape in enumerate(_OUTS)]
    build(nc, tensors, outs)
    r = _run(nc, [arrays], core_ids=[0])
    return tuple(r.results[0][f"out_{i}_dram"] for i in range(len(_OUTS)))
```

```python
from contextlib import ExitStack

import numpy as np

import concourse.bass as bass
from concourse import mybir

F32 = mybir.dt.float32
F32R = mybir.dt.float32r
BF16 = mybir.dt.bfloat16
I32 = mybir.dt.int32
U32 = mybir.dt.uint32
ALU = mybir.AluOpType
ACT = mybir.ActivationFunctionType
AX = mybir.AxisListType

P = 128
D = 1024
KC = D // P
S = 2048
NB = S // P
DB = 8
NC = DB + 1
H = 8
NOPE, ROPE, VD = 64, 32, 64
QK = NOPE + ROPE
QL, KVL = 256, 128
QC = QL // P
DATT = H * VD
DPOOL = 512
NG = 4
PREV = 15
OFF_KV, OFF_KR, OFF_GA = QL, QL + KVL, QL + KVL + ROPE
DIN = OFF_GA + DATT + 2 * DPOOL
LA = OFF_GA
LB = DIN - OFF_GA
OFF_U, OFF_GP = DATT, DATT + DPOOL
EPS = 1e-6
SCALE = QK ** -0.5
NPG, PG = 32, 128
QTR = 4
TPP = PG // QTR
MASKED = -1e30
BASE = 16896
GRP = 4
NGRP = NB // GRP


class Map:

    def __init__(self, nc, start):
        self.nc, self.at = nc, start

    def __call__(self, name, shape, dt):
        size = {F32: 4, F32R: 4, BF16: 2, I32: 4, U32: 4}[dt]
        n = int(np.prod(shape[1:])) * size
        t = self.nc.alloc_sbuf_tensor_at(name, list(shape), dt, offset=self.at)
        self.at += (n + 31) // 32 * 32
        assert self.at <= 229344, (name, self.at)
        return t


def exists(n, count):
    return not isinstance(n, int) or 0 <= n < count


def stage_semaphore(nc, sems, name):
    sems.append(nc.alloc_semaphore(name))
    return sems[-1]


def release(nc, sems):
    nc.clear_and_free_semaphores(sems)
    nc.all_engine_barrier()


def peeled(eng, count, body, tail=1):
    body(0)
    with eng.Fori(1, count - tail) as i:
        body(i)
    for i in range(count - tail, count):
        body(i)


def mm3(pe, out, lhs, rhs, first, last):
    pe.matmul(out, lhs[0], rhs[0], start=first, stop=False)
    pe.matmul(out, lhs[0], rhs[1], start=False, stop=False)
    return pe.matmul(out, lhs[1], rhs[0], start=False, stop=last)


def build(nc, t, o):
    x_blocks = t["x_prompt"].rearrange("a (n p) d -> p (a n) d", p=P)
    ckv_out = o[2].rearrange("a b (n p) k -> p (a b n) k", p=P)
    kr_out = o[3].rearrange("a b (n p) k -> p (a b n) k", p=P)
    w_in = t["w_in"].rearrange("a (c p) n -> p (a c) n", p=P)

    mod_d = nc.dram_tensor("mod_scratch", (NC, 3 * D), F32, kind="Internal").ap()
    zs_d = nc.dram_tensor("sample_z_scratch", (DB, DIN), F32, kind="Internal").ap()
    gate_att_d = nc.dram_tensor("gate_att_scratch", (S, DATT), F32, kind="Internal").ap()
    pool_d = nc.dram_tensor("pool_scratch", (NG, P, S), F32, kind="Internal").ap()
    att_d = nc.dram_tensor("att_scratch", (S, DATT), F32, kind="Internal").ap()
    gate_att_blocks = gate_att_d.rearrange("(n p) e -> p n e", p=P)

    keep = Map(nc, BASE)
    ident = keep("ident", [P, P], F32)
    identb = keep("identb", [P, P], BF16)
    mask_q = keep("mask_q", [P, P], BF16)
    mask_k = keep("mask_k", [P, P], BF16)
    ones = keep("ones", [P, P], F32)
    rstd = keep("rstd", [P, NB], F32)
    coef_a = keep("coef_a", [P, KC, NC], F32)
    coef_b = keep("coef_b", [P, KC, NC], F32)
    vec_t = keep("vec_t", [P, 16], F32)
    lat_t = keep("lat_t", [P, 3, S], F32)
    after_lat = keep.at
    hs = [keep("hs_hi", [P, KC, P], F32R), keep("hs_lo", [P, KC, P], F32R)]
    after_hs = keep.at

    m = Map(nc, after_hs)
    wa = [m("wa_hi", [P, KC, LA], F32R), m("wa_lo", [P, KC, LA], F32R)]
    after_wa = m.at
    with ExitStack() as ctx:
        sems = []
        ctx.callback(release, nc, sems)

        def psum(name, shape):
            return ctx.enter_context(nc.psum_tensor("mod_" + name, shape, F32))

        def sem(name):
            return stage_semaphore(nc, sems, "mod_" + name)

        NX = 3
        xt = m("mod_x", [P, NX, D], F32)
        xs = m("mod_xs", [DB, D], F32)
        wa_raw = m("wa_raw", [P, KC, LA], F32)
        c_sb = m("c_sb", [NC, D], F32)
        c_act = m("c_act", [P, KC, NC], F32)
        vecs = m("vecs", [16, P], F32)
        bias = m("ada_b_rows", [NC, 3 * D], F32)
        mod = m("mod_rows", [NC, 3 * D], F32)
        NA = 5
        ada = m("ada", [P, NA, 3 * D], F32)
        ss = m("x_ss", [P, NB], F32)
        ss_s = m("xs_ss", [DB, 1], F32)
        rstd_s = m("xs_rstd", [DB, 1], F32)
        masks = m("masks_f32", [P, 2, P], F32)
        junk_s = m("junk_s", [DB, D], F32)
        hs32 = m("hs32", [P, KC, DB], F32)
        ps_mod = psum("ps_mod", [P, 6, 512])
        ps_c = psum("ps_c", [P, 512])
        ps_t = psum("ps_t", [P, 512])

        const_in, masks_in, c_in, small_in, xs_in = sem("const_in"), sem("masks_in"), sem("c_in"), sem("small_in"), sem("xs_in")
        ada_in = [sem(f"ada_in{k}") for k in range(NA)]
        x_in = [sem(f"x_in{k}") for k in range(NX)]
        wa_in = sem("wa_in")
        c_turned, c_ready, vec_turned, vec_ready = sem("c_turned"), sem("c_ready"), sem("vec_turned"), sem("vec_ready")
        ada_used, mod_summed, mod_ready, mod_turned = sem("ada_used"), sem("mod_summed"), sem("mod_ready"), sem("mod_turned")
        x_squared, xs_squared, ss_zero, var_ready, sd_ready, rstd_ready = (
            sem("x_squared"), sem("xs_squared"), sem("ss_zero"), sem("var_ready"), sem("sd_ready"), sem("rstd_ready"))
        wa_hi_ready, wa_lo_ready = sem("wa_hi_ready"), sem("wa_lo_ready")
        hs_zero, xs_scaled, xs_turned, hs_done, coef_ready, mod_out = (
            sem("hs_zero"), sem("xs_scaled"), sem("xs_turned"), sem("hs_done"), sem("coef_ready"), sem("mod_out"))

        ada_rows = t["ada_w"].rearrange("a (c p) n -> p (a c) n", p=P)
        block = ctx.enter_context(nc.Block())

        @block.sync
        def _(sp):
            sp.dma_start(ident[:], t["c_ident"]).then_inc(const_in, 16)
            sp.dma_start(c_sb[0:DB, :], t["c_sample"]).then_inc(c_in, 16)
            sp.dma_start(c_sb[DB:NC, :], t["c_prompt"]).then_inc(c_in, 16)
            for k in range(KC):
                if k >= NA:
                    sp.wait_ge(ada_used, k - NA + 1)
                sp.dma_start(ada[:, k % NA, :], ada_rows[:, k, :]).then_inc(ada_in[k % NA], 16)
                if k == 0:
                    sp.dma_start(vecs[0:8, :], t["norm_w"].rearrange("a (c p) -> (a c) p", p=P)).then_inc(small_in, 16)
                    sp.dma_start(vecs[8:12, :], t["b_pool"][0]).then_inc(small_in, 16)
                    sp.dma_start(vecs[12:16, :], t["pool_scale"].rearrange("a (c p) -> (a c) p", p=P)).then_inc(small_in, 16)
                    sp.dma_start(bias[:], t["ada_b"].rearrange("a n -> (a n)").partition_broadcast(NC)).then_inc(small_in, 16)
                    sp.dma_start(masks[:, 0, :], t["c_mask_q"]).then_inc(masks_in, 16)
                    sp.dma_start(masks[:, 1, :], t["c_mask_k"]).then_inc(masks_in, 16)
            sp.wait_ge(mod_ready, 6)
            sp.dma_start(mod_d, mod[:]).then_inc(mod_out, 16)
            sp.wait_ge(mod_out, 16)

        @block.scalar
        def _(act):
            act.dma_start(xs[:], t["x_sample"].rearrange("b s d -> (b s) d")).then_inc(xs_in, 16)
            act.dma_start(wa_raw[:], w_in[:, :, 0:LA]).then_inc(wa_in, 16)
            for n in range(NX):
                act.dma_start(xt[:, n, :], x_blocks[:, n, :]).then_inc(x_in[n], 16)
            act.wait_ge(c_turned, 1)
            act.activation(c_act[:].rearrange("p c n -> p (c n)"), ps_c[:, 0:KC * NC], ACT.Silu).then_inc(c_ready, 1)
            act.wait_ge(ss_zero, 1)
            act.wait_ge(xs_in, 16)
            act.activation(junk_s[:], xs[:], ACT.Square, accum_out=ss_s[:]).then_inc(xs_squared, 1)
            act.wait_ge(var_ready, 1)
            act.activation(ss_s[:], ss_s[:], ACT.Sqrt).then_inc(sd_ready, 1)
            act.wait_ge(wa_in, 16)
            act.activation(wa[0][:], wa_raw[:], ACT.Copy).then_inc(wa_hi_ready, 1)
            for n in range(NB):
                act.wait_ge(x_in[n % NX], 16 * (n // NX + 1))
                act.activation(xt[:, n % NX, :], xt[:, n % NX, :], ACT.Square,
                               accum_out=ss[:, n:n + 1]).then_inc(x_squared, 1)
                if n >= 1 and n - 1 + NX < NB:
                    act.wait_ge(x_squared, n)
                    act.dma_start(xt[:, (n - 1) % NX, :], x_blocks[:, n - 1 + NX, :]).then_inc(x_in[(n - 1) % NX], 16)
            act.wait_ge(var_ready, 2)
            act.activation(ss[:], ss[:], ACT.Sqrt).then_inc(sd_ready, 1)

        @block.gpsimd
        def _(pool):
            pool.memset(ones[:], 1.0)
            for part in hs:
                last = pool.memset(part[:].bitcast(F32), 0.0)
            last.then_inc(hs_zero, 1)
            pool.wait_ge(const_in, 16)
            pool.tensor_copy(identb[:], ident[:])
            pool.wait_ge(masks_in, 32)
            pool.tensor_copy(mask_q[:], masks[:, 0, :])
            pool.tensor_copy(mask_k[:], masks[:, 1, :])
            pool.wait_ge(wa_hi_ready, 1)
            pool.tensor_tensor(wa[1][:], wa_raw[:], wa[0][:].bitcast(F32), ALU.subtract).then_inc(wa_lo_ready, 1)

        @block.vector
        def _(dve):
            dve.memset(ss[:], 0.0)
            dve.memset(ss_s[:], 0.0).then_inc(ss_zero, 1)
            dve.wait_ge(vec_turned, 1)
            dve.tensor_copy(vec_t[:], ps_t[:, 0:16]).then_inc(vec_ready, 1)
            dve.wait_ge(xs_squared, 1)
            dve.tensor_scalar(ss_s[:], ss_s[:], 1.0 / D, EPS, ALU.mult, ALU.add).then_inc(var_ready, 1)
            dve.wait_ge(sd_ready, 1)
            dve.reciprocal(rstd_s[:], ss_s[:]).then_inc(rstd_ready, 1)
            dve.wait_ge(rstd_ready, 1)
            dve.tensor_scalar(xs[:], xs[:], rstd_s[:], None, ALU.mult).then_inc(xs_scaled, 1)
            dve.wait_ge(small_in, 64)
            dve.wait_ge(mod_summed, 1)
            for g in range(6):
                dve.tensor_tensor(mod[:, g * 512:(g + 1) * 512], ps_mod[0:NC, g, :], bias[:, g * 512:(g + 1) * 512],
                                  ALU.add).then_inc(mod_ready, 1)
            dve.wait_ge(vec_ready, 1)
            dve.wait_ge(mod_turned, 1)
            turned = ps_c[:, 0:2 * KC * NC].rearrange("p (k c n) -> p k c n", k=2, c=KC)
            dve.tensor_copy(coef_b[:], turned[:, 0])
            dve.scalar_tensor_tensor(out=coef_a[:], in0=turned[:, 1], scalar=1.0,
                                     in1=vec_t[:, 0:KC].unsqueeze(2).broadcast_to([P, KC, NC]),
                                     op0=ALU.add, op1=ALU.mult).then_inc(coef_ready, 1)
            dve.wait_ge(coef_ready, 1)
            dve.wait_ge(xs_turned, 1)
            xs_t = ps_t[:, 64:64 + KC * DB].rearrange("p (c b) -> p c b", c=KC)
            dve.tensor_tensor(hs32[:], xs_t, coef_a[:, :, 0:DB], ALU.mult).then_inc(hs_done, 1)
            dve.wait_ge(hs_done, 1)
            dve.tensor_tensor(hs32[:], hs32[:], coef_b[:, :, 0:DB], ALU.add).then_inc(hs_done, 1)
            dve.wait_ge(hs_done, 2)
            dve.wait_ge(hs_zero, 1)
            dve.tensor_copy(hs[0][:, :, 0:DB], hs32[:]).then_inc(hs_done, 1)
            dve.wait_ge(hs_done, 3)
            dve.tensor_tensor(hs[1][:, :, 0:DB], hs32[:], hs[0][:, :, 0:DB].bitcast(F32), ALU.subtract).then_inc(hs_done, 1)
            dve.wait_ge(x_squared, NB)
            dve.tensor_scalar(ss[:], ss[:], 1.0 / D, EPS, ALU.mult, ALU.add).then_inc(var_ready, 1)
            dve.wait_ge(sd_ready, 2)
            dve.reciprocal(rstd[:], ss[:]).then_inc(rstd_ready, 1)

        @block.tensor
        def _(pe):
            pe.wait_ge(const_in, 16)
            pe.wait_ge(c_in, 32)
            for k in range(KC):
                last = pe.transpose(ps_c[:, k * NC:(k + 1) * NC], c_sb[:, k * P:(k + 1) * P], ident[0:NC, 0:NC])
            last.then_inc(c_turned, 1)
            pe.wait_ge(small_in, 64)
            pe.transpose(ps_t[:, 0:16], vecs[:], ident[0:16, 0:16]).then_inc(vec_turned, 1)
            pe.wait_ge(c_ready, 1)
            for k in range(KC):
                pe.wait_ge(ada_in[k % NA], 16 * (k // NA + 1))
                for g in range(6):
                    last = pe.matmul(ps_mod[0:NC, g, :], c_act[:, k, :], ada[:, k % NA, g * 512:(g + 1) * 512],
                                     start=(k == 0), stop=(k == KC - 1))
                last.then_inc(mod_summed if k == KC - 1 else ada_used, 1)
            pe.wait_ge(xs_scaled, 1)
            pe.wait_ge(vec_ready, 1)
            for k in range(KC):
                last = pe.transpose(ps_t[:, 64 + k * DB:64 + (k + 1) * DB], xs[:, k * P:(k + 1) * P], ident[0:DB, 0:DB])
            last.then_inc(xs_turned, 1)
            pe.wait_ge(mod_ready, 4)
            for k in range(2 * KC):
                last = pe.transpose(ps_c[:, k * NC:(k + 1) * NC], mod[:, k * P:(k + 1) * P], ident[0:NC, 0:NC])
            last.then_inc(mod_turned, 1)

    wb_at = Map(nc, after_wa)
    wb = [wb_at("wb_hi", [P, KC, LB], F32R), wb_at("wb_lo", [P, KC, LB], F32R)]
    ds = bass.ds
    with ExitStack() as ctx:
        sems = []
        ctx.callback(release, nc, sems)

        def psum(name, shape):
            return ctx.enter_context(nc.psum_tensor("lat_" + name, shape, F32))

        def sem(name):
            return stage_semaphore(nc, sems, "lat_" + name)

        m = Map(nc, wb_at.at)
        xt = m("lat_x", [P, 2, D], F32)
        h32 = m("lat_h32", [P, 2, D], F32)
        hb = [m("lat_h_hi", [P, 2, D], F32R), m("lat_h_lo", [P, 2, D], F32R)]
        wraw = m("lat_wraw", [P, LB], F32)
        lat = m("lat_rows", [P, 2, LA], F32)
        junk = m("lat_junk", [P, 2, OFF_KR], BF16)
        stat = m("lat_stat", [P, 2, 2], F32)
        rot = m("lat_rot", [P, 2, ROPE], F32)
        qn_w = m("qn_w", [P, QL], F32)
        kn_w = m("kn_w", [P, KVL], F32)
        cosk = m("cosk", [P, NB, ROPE], F32)
        sink = m("sink", [P, NB, ROPE], F32)
        zs = m("zs_a", [DB, LA], F32)
        ps_x = psum("ps_x", [P, 2, 2, 512])
        ps_z = psum("ps_z", [P, 2, 512])
        ps_l = psum("ps_l", [P, 512])
        ps_s = psum("ps_s", [P, 512])
        x_in = [sem("x_in0"), sem("x_in1")]
        tab_in, wb_in = sem("tab_in"), sem("wb_in")
        x_scaled, x_turned, h_ready, h_hi, h_lo = (
            sem("x_scaled"), sem("x_turned"), sem("h_ready"), sem("h_hi"), sem("h_lo"))
        z_done, ss_ready, var_ready, sd_ready, step_done = (
            sem("z_done"), sem("ss_ready"), sem("var_ready"), sem("sd_ready"), sem("step_done"))
        lat_ready, lat_turned, lat_kept = sem("lat_ready"), sem("lat_turned"), sem("lat_kept")
        lat_out = [sem("lat_out0"), sem("lat_out1")]
        wb_hi, wb_lo = sem("wb_hi_ready"), sem("wb_lo_ready")
        zs_done, zs_ready, zs_out = sem("zs_done"), sem("zs_ready"), sem("zs_out")
        NP2 = NB // 2
        block = ctx.enter_context(nc.Block())

        @block.sync
        def _(sp):
            for b in range(2):
                sp.dma_start(xt[:, b, :], x_blocks[:, b, :]).then_inc(x_in[b], 16)
            sp.dma_start(qn_w[:], t["q_norm_w"].rearrange("a n -> (a n)").partition_broadcast(P)).then_inc(tab_in, 16)
            sp.dma_start(kn_w[:], t["kv_norm_w"].rearrange("a n -> (a n)").partition_broadcast(P)).then_inc(tab_in, 16)
            sp.dma_start(cosk[:], t["c_rope_rows"][0]).then_inc(tab_in, 16)
            sp.dma_start(sink[:], t["c_rope_rows"][1]).then_inc(tab_in, 16)

            def body(i):
                for b in range(2):
                    n = 2 * i + b
                    if exists(n + 2, NB):
                        sp.wait_ge(x_turned, n + 1)
                        sp.dma_start(xt[:, b, :], x_blocks[:, ds(n + 2, 1), :]).then_inc(x_in[b], 16)
            peeled(sp, NP2, body)
            sp.wait_ge(zs_ready, 1)
            sp.dma_start(zs_d[:, 0:LA], zs[:]).then_inc(zs_out, 16)
            sp.wait_ge(zs_out, 16)

        @block.scalar
        def _(act):
            def scale_x(n, b):
                act.wait_ge(x_in[b], 16 * (n // 2 + 1) if isinstance(n, int) else 8 * (n - b) + 16)
                act.activation(xt[:, b, :], xt[:, b, :], ACT.Copy, scale=rstd[:, ds(n, 1)]).then_inc(x_scaled, 1)

            def h_high(n, b):
                act.wait_ge(h_ready, n + 1)
                if exists(n - 2, NB):
                    act.wait_ge(z_done, n - 1)
                act.activation(hb[0][:, b, :], h32[:, b, :], ACT.Copy).then_inc(h_hi, 1)

            def keep_lat(n, b):
                act.wait_ge(lat_turned, n + 1)
                act.activation(lat_t[:, :, ds(n * P, P)], ps_l[:, 0:3 * P].rearrange("p (c s) -> p c s", c=3),
                               ACT.Copy).then_inc(lat_kept, 1)
                act.dma_start(ckv_out[:, ds(n, 1), :], lat[:, b, OFF_KV:OFF_KR].unsqueeze(1)).then_inc(lat_out[b], 16)
                act.dma_start(kr_out[:, ds(n, 1), :], lat[:, b, OFF_KR:LA].unsqueeze(1)).then_inc(lat_out[b], 16)

            def body(i):
                for b in range(2):
                    n = 2 * i + b
                    if exists(n + 3, NB):
                        scale_x(n + 3, 1 - b)
                    if exists(n + 2, NB):
                        h_high(n + 2, b)
                    act.wait_ge(z_done, n + 1)
                    if exists(n - 2, NB):
                        act.wait_ge(var_ready, n - 1)
                    act.activation(junk[:, b, 0:QL], ps_z[:, b, 0:QL], ACT.Square, accum_out=stat[:, b, 0:1])
                    act.activation(junk[:, b, OFF_KV:OFF_KR], ps_z[:, b, OFF_KV:OFF_KR], ACT.Square,
                                   accum_out=stat[:, b, 1:2]).then_inc(ss_ready, 1)
                    if exists(n - 1, NB):
                        keep_lat(n - 1, 1 - b)
                    act.wait_ge(var_ready, n + 1)
                    act.activation(stat[:, b, :], stat[:, b, :], ACT.Sqrt).then_inc(sd_ready, 1)
                act.wait_ge(wb_in, 16 * i + 16)
                act.activation(wb[0][:, ds(i, 1), :], wraw[:].unsqueeze(1), ACT.Copy).then_inc(wb_hi, 1)
            scale_x(0, 0)
            scale_x(1, 1)
            h_high(0, 0)
            h_high(1, 1)
            scale_x(2, 0)
            peeled(act, NP2, body, tail=2)
            keep_lat(NB - 1, 1)
            for b in range(2):
                act.wait_ge(lat_out[b], 16 * NB)

        @block.gpsimd
        def _(pool):
            def h_low(n, b):
                pool.wait_ge(h_hi, n + 1)
                pool.tensor_tensor(hb[1][:, b, :], h32[:, b, :], hb[0][:, b, :].bitcast(F32), ALU.subtract).then_inc(h_lo, 1)

            def body(i):
                for b in range(2):
                    if exists(2 * i + b + 2, NB):
                        h_low(2 * i + b + 2, b)
                pool.wait_ge(wb_hi, i + 1)
                pool.tensor_tensor(wb[1][:, ds(i, 1), :], wraw[:].unsqueeze(1), wb[0][:, ds(i, 1), :].bitcast(F32),
                                   ALU.subtract).then_inc(wb_lo, 1)
                if exists(i + 1, KC):
                    pool.wait_ge(wb_lo, i + 1)
                    load_weights(i + 1)

            def load_weights(i):
                pool.dma_start(wraw[:].unsqueeze(1), w_in[:, ds(i, 1), LA:DIN]).then_inc(wb_in, 16)
            load_weights(0)
            h_low(0, 0)
            h_low(1, 1)
            peeled(pool, NP2, body)

        @block.vector
        def _(dve):
            def h_values(n, b):
                dve.wait_ge(x_turned, n + 1)
                if exists(n - 2, NB):
                    dve.wait_ge(h_lo, n - 1)
                for c in range(KC):
                    last = dve.tensor_scalar(h32[:, b, c * P:(c + 1) * P], ps_x[:, b, c // 4, (c % 4) * P:(c % 4 + 1) * P],
                                             coef_a[:, c, DB:NC], coef_b[:, c, DB:NC], ALU.mult, ALU.add)
                last.then_inc(h_ready, 1)

            def body(i):
                for b in range(2):
                    n = 2 * i + b
                    if exists(n + 2, NB):
                        h_values(n + 2, b)
                    dve.wait_ge(ss_ready, n + 1)
                    dve.tensor_scalar(stat[:, b, 0:1], stat[:, b, 0:1], 1.0 / QL, EPS, ALU.mult, ALU.add)
                    dve.tensor_scalar(stat[:, b, 1:2], stat[:, b, 1:2], 1.0 / KVL, EPS, ALU.mult, ALU.add).then_inc(var_ready, 1)
                    if exists(n - 2, NB):
                        dve.wait_ge(lat_turned, n - 1)
                        dve.wait_ge(lat_out[b], 32 * i if b == 0 else 32 * i)
                    z = ps_z[:, b, :]
                    dve.tensor_tensor(lat[:, b, OFF_KR:LA], z[:, OFF_KR:LA], cosk[:, ds(n, 1), :].squeeze(1), ALU.mult)
                    dve.tensor_tensor(rot[:, b, 0:16], z[:, OFF_KR + 16:LA], sink[:, ds(n, 1), 0:16].squeeze(1), ALU.mult)
                    dve.tensor_tensor(rot[:, b, 16:32], z[:, OFF_KR:OFF_KR + 16], sink[:, ds(n, 1), 16:32].squeeze(1),
                                      ALU.mult).then_inc(step_done, 1)
                    dve.wait_ge(step_done, 2 * n + 1)
                    dve.tensor_tensor(lat[:, b, OFF_KR:LA], lat[:, b, OFF_KR:LA], rot[:, b, :], ALU.add)
                    dve.wait_ge(sd_ready, n + 1)
                    dve.reciprocal(stat[:, b, :], stat[:, b, :]).then_inc(step_done, 1)
                    dve.wait_ge(step_done, 2 * n + 2)
                    dve.scalar_tensor_tensor(out=lat[:, b, 0:QL], in0=z[:, 0:QL], scalar=stat[:, b, 0:1], in1=qn_w[:],
                                             op0=ALU.mult, op1=ALU.mult)
                    dve.scalar_tensor_tensor(out=lat[:, b, OFF_KV:OFF_KR], in0=z[:, OFF_KV:OFF_KR], scalar=stat[:, b, 1:2],
                                             in1=kn_w[:], op0=ALU.mult, op1=ALU.mult).then_inc(lat_ready, 1)
            dve.wait_ge(tab_in, 64)
            h_values(0, 0)
            h_values(1, 1)
            peeled(dve, NP2, body)
            dve.wait_ge(zs_done, 1)
            dve.tensor_copy(zs[:], ps_s[0:DB, 0:LA]).then_inc(zs_ready, 1)

        @block.tensor
        def _(pe):
            def turn_x(n, b):
                pe.wait_ge(x_scaled, n + 1)
                if exists(n - 2, NB):
                    pe.wait_ge(h_ready, n - 1)
                for c in range(KC):
                    last = pe.transpose(ps_x[:, b, c // 4, (c % 4) * P:(c % 4 + 1) * P], xt[:, b, c * P:(c + 1) * P], ident[:])
                last.then_inc(x_turned, 1)

            def turn_lat(n, b):
                pe.wait_ge(lat_ready, n + 1)
                if exists(n - 1, NB):
                    pe.wait_ge(lat_kept, n)
                for c in range(3):
                    last = pe.transpose(ps_l[:, c * P:(c + 1) * P], lat[:, b, c * P:(c + 1) * P], ident[:])
                last.then_inc(lat_turned, 1)

            def body(i):
                for b in range(2):
                    n = 2 * i + b
                    if exists(n + 2, NB):
                        turn_x(n + 2, b)
                    pe.wait_ge(h_lo, n + 1)
                    if exists(n - 2, NB):
                        pe.wait_ge(lat_ready, n - 1)
                    for c in range(KC):
                        cols = slice(c * P, (c + 1) * P)
                        last = mm3(pe, ps_z[:, b, 0:LA], [hb[0][:, b, cols], hb[1][:, b, cols]],
                                   [wa[0][:, c, :], wa[1][:, c, :]], c == 0, c == KC - 1)
                    last.then_inc(z_done, 1)
                    if exists(n - 1, NB):
                        turn_lat(n - 1, 1 - b)
            turn_x(0, 0)
            turn_x(1, 1)
            peeled(pe, NP2, body)
            turn_lat(NB - 1, 1)
            for c in range(KC):
                last = mm3(pe, ps_s[:, 0:LA], [hs[0][:, c, :], hs[1][:, c, :]],
                           [wa[0][:, c, :], wa[1][:, c, :]], c == 0, c == KC - 1)
            last.then_inc(zs_done, 1)

    T = 2 * P
    NS = S // T
    with ExitStack() as ctx:
        sems = []
        ctx.callback(release, nc, sems)

        def psum(name, shape):
            return ctx.enter_context(nc.psum_tensor("mix_" + name, shape, F32))

        def sem(name):
            return stage_semaphore(nc, sems, "mix_" + name)

        m = Map(nc, after_hs)
        u_ext = m("u_ext", [P, NG, PREV + T], F32)
        win = m("win", [P, 2, 2, PREV + T], F32)
        pooled = m("pooled", [P, NG, T], F32)
        gate_p = m("gate_p", [P, NG, T], F32)
        mixed = m("mixed", [P, NG, T], F32)
        gate_a = m("gate_a", [P, 2, DATT], F32)
        assert m.at <= after_wa
        m = Map(nc, wb_at.at)
        hb = [m("mix_h_hi", [P, 2, KC, T], F32R), m("mix_h_lo", [P, 2, KC, T], F32R)]
        xt = m("mix_x", [P, 2, D], F32)
        h32 = m("mix_h32", [P, D], F32)
        w_pool = m("w_pool", [P, NG, P], F32)
        count = m("count", [P, NG, 16], F32)
        early = m("early", [P, 16], F32)
        prev = m("prev", [PREV, DPOOL], F32)
        zs_b = xt[0:DB].rearrange("p b d -> p (b d)")[:, 0:LB]
        ps_x = psum("ps_x", [P, 2, 512])
        ps_u = psum("ps_u", [P, 2, 512])
        ps_a = psum("ps_a", [P, 2, 512])
        ps_y = psum("ps_y", [P, 2, 512])
        ps_z = [ps_a[:, 0, :], ps_a[:, 1, :]]
        x_in = [sem("x_in0"), sem("x_in1")]
        tab_in = sem("tab_in")
        x_scaled, x_turned, h_ready, h_hi, h_lo = (
            sem("x_scaled"), sem("x_turned"), sem("h_ready"), sem("h_hi"), sem("h_lo"))
        u_done, u_kept, win_step, win_ready, pooled_ready, halo_ready = (
            sem("u_done"), sem("u_kept"), sem("win_step"), sem("win_ready"), sem("pooled_ready"), sem("halo_ready"))
        a_done, a_kept, y_done, y_step, mixed_ready = (
            sem("a_done"), sem("a_kept"), sem("y_done"), sem("y_step"), sem("mixed_ready"))
        early_step = sem("early_step")
        mixed_out = [sem(f"mixed_out{g}") for g in range(NG)]
        a_out = [sem("a_out0"), sem("a_out1")]
        zs_done, zs_ready, zs_out, prev_done, prev_ready = (
            sem("zs_done"), sem("zs_ready"), sem("zs_out"), sem("prev_done"), sem("prev_ready"))
        HALF = NS // 2
        LEVELS = sum(g + 1 for g in range(NG))
        block = ctx.enter_context(nc.Block())

        @block.sync
        def _(sp):
            for b in range(2):
                sp.dma_start(xt[:, b, :], x_blocks[:, b, :]).then_inc(x_in[b], 16)
            sp.dma_start(w_pool[:], t["w_pool"].rearrange("a g c d -> c (a g) d")).then_inc(tab_in, 16)
            sp.dma_start(count[:].rearrange("p g s -> p (g s)"),
                         t["c_count"].rearrange("g s -> (g s)").partition_broadcast(P)).then_inc(tab_in, 16)

            def load_x(n, b):
                sp.wait_ge(x_turned, n - 1)
                sp.dma_start(xt[:, b, :], x_blocks[:, ds(n, 1), :]).then_inc(x_in[b], 16)

            def body(s, e):
                for b in range(2):
                    if exists(s + 2, NS):
                        load_x(2 * s + 4 + b, b)
                for b in range(2):
                    sp.wait_ge(a_kept, 2 * s + b + 1)
                    sp.dma_start(gate_att_blocks[:, ds(2 * s + b, 1), :], gate_a[:, b, :].unsqueeze(1)).then_inc(a_out[b], 16)
                for g in range(NG):
                    sp.wait_ge(mixed_ready, 4 * s + g + 1)
                    sp.dma_start(pool_d[g][:, ds(s * T, T)], mixed[:, g, :]).then_inc(mixed_out[g], 16)
            for b in range(2):
                load_x(2 + b, b)
            peeled(sp, HALF, lambda i: [body(2 * i + e, e) for e in range(2)])
            sp.wait_ge(zs_ready, 3)
            sp.dma_start(zs_d[:, LA:DIN], zs_b).then_inc(zs_out, 16)
            sp.wait_ge(prev_ready, 1)
            sp.dma_start(o[4].rearrange("a b r c -> (a b r) c"), prev[:]).then_inc(zs_out, 16)
            sp.wait_ge(zs_out, 32)
            for b in range(2):
                sp.wait_ge(a_out[b], 16 * NS)
            for g in range(NG):
                sp.wait_ge(mixed_out[g], 16 * NS)

        @block.scalar
        def _(act):
            def scale_x(n, b):
                act.wait_ge(x_in[b], 8 * (n - b) + 16)
                act.activation(xt[:, b, :], xt[:, b, :], ACT.Copy, scale=rstd[:, ds(n, 1)]).then_inc(x_scaled, 1)

            def h_high(s, e, b):
                act.wait_ge(h_ready, 2 * s + b + 1)
                if exists(s - 2, NS):
                    act.wait_ge(a_done, 2 * (s - 1))
                act.activation(hb[0][:, e, :, b * P:(b + 1) * P], h32[:].rearrange("p (c s) -> p c s", c=KC),
                               ACT.Copy).then_inc(h_hi, 1)

            def keep_u(s, g):
                act.wait_ge(u_done, 4 * s + g + 1)
                act.wait_ge(halo_ready, 4 * s + g + 1)
                act.activation(u_ext[:, g, PREV:], ps_u[:, g % 2, 0:T], ACT.Copy)
                if exists(s - 1, NS):
                    act.wait_ge(mixed_ready, 4 * (s - 1) + g + 1)
                act.activation(gate_p[:, g, :], ps_u[:, g % 2, T:2 * T], ACT.Silu).then_inc(u_kept, 1)

            def body(s, e):
                for b in range(2):
                    if exists(s + 1, NS):
                        h_high(s + 1, 1 - e, b)
                    keep_u(s, 2 * b)
                    keep_u(s, 2 * b + 1)
                for b in range(2):
                    if exists(s + 2, NS):
                        scale_x(2 * s + 4 + b, b)
                for b in range(2):
                    act.wait_ge(a_done, 2 * s + b + 1)
                    if exists(s - 1, NS):
                        act.wait_ge(a_out[b], 16 * s)
                    act.activation(gate_a[:, b, :], ps_a[:, b, :], ACT.Silu).then_inc(a_kept, 1)
            for b in range(2):
                scale_x(b, b)
            for b in range(2):
                h_high(0, 0, b)
            for b in range(2):
                scale_x(2 + b, b)
            peeled(act, HALF, lambda i: [body(2 * i + e, e) for e in range(2)])

        @block.gpsimd
        def _(pool):
            steps = [0]

            def h_low(s, e, b):
                pool.wait_ge(h_hi, 2 * s + b + 1)
                pool.tensor_tensor(hb[1][:, e, :, b * P:(b + 1) * P], h32[:].rearrange("p (c s) -> p c s", c=KC),
                                   hb[0][:, e, :, b * P:(b + 1) * P].bitcast(F32), ALU.subtract).then_inc(h_lo, 1)

            def window(s, g, done):
                pool.wait_ge(u_kept, 4 * s + g + 1)
                if g >= 2:
                    pool.wait_ge(pooled_ready, 4 * s + g - 1)
                elif exists(s - 1, NS):
                    pool.wait_ge(pooled_ready, 4 * (s - 1) + g + 3)
                src = u_ext[:, g, :]
                for level in range(g + 1):
                    shift = 1 << level
                    width = T + (1 << (g + 1)) - 2 * shift
                    if level:
                        pool.wait_ge(win_step, s * LEVELS + done + level)
                    dst = win[:, g % 2, level % 2, PREV + T - width:]
                    last = pool.tensor_tensor(dst, src[:, PREV + T - width:PREV + T],
                                              src[:, PREV + T - width - shift:PREV + T - shift], ALU.add)
                    last.then_inc(win_step, 1)
                    src = win[:, g % 2, level % 2, :]

            def body(s, e):
                done = 0
                for b in range(2):
                    if exists(s + 1, NS):
                        h_low(s + 1, 1 - e, b)
                    for g in (2 * b, 2 * b + 1):
                        window(s, g, done)
                        done += g + 1
            pool.memset(u_ext[:], 0.0).then_inc(halo_ready, NG)
            for b in range(2):
                h_low(0, 0, b)
            peeled(pool, HALF, lambda i: [body(2 * i + e, e) for e in range(2)])

        @block.vector
        def _(dve):
            def h_values(n):
                dve.wait_ge(x_turned, n + 1)
                if exists(n - 1, NB):
                    dve.wait_ge(h_lo, n)
                for c in range(KC):
                    last = dve.tensor_scalar(h32[:, c * P:(c + 1) * P], ps_x[:, c // 4, (c % 4) * P:(c % 4 + 1) * P],
                                             coef_a[:, c, DB:NC], coef_b[:, c, DB:NC], ALU.mult, ALU.add)
                last.then_inc(h_ready, 1)

            def pooled_values(s, g, done):
                dve.wait_ge(win_step, s * LEVELS + done)
                if exists(s - 1, NS):
                    dve.wait_ge(y_done, 4 * (s - 1) + g + 1)
                total = win[:, g % 2, g % 2, PREV:]
                first = isinstance(s, int) and s == 0
                if first:
                    dve.tensor_tensor(early[:], total[:, 0:16], count[:, g, :], ALU.mult).then_inc(early_step, 1)
                    dve.wait_ge(early_step, 2 * g + 1)
                    dve.tensor_tensor(pooled[:, g, 0:16], early[:], u_ext[:, g, PREV:PREV + 16],
                                      ALU.subtract).then_inc(early_step, 1)
                    dve.wait_ge(early_step, 2 * g + 2)
                z = 16 if first else 0
                dve.scalar_tensor_tensor(out=pooled[:, g, z:], in0=total[:, z:], scalar=1.0 / (2 << g),
                                         in1=u_ext[:, g, PREV + z:], op0=ALU.mult, op1=ALU.subtract).then_inc(pooled_ready, 1)
                dve.wait_ge(pooled_ready, 4 * s + g + 1)
                if exists(s + 1, NS):
                    dve.tensor_copy(u_ext[:, g, 0:PREV], u_ext[:, g, T:]).then_inc(halo_ready, 1)

            def mix(s, g):
                dve.wait_ge(y_done, 4 * s + g + 1)
                if exists(s - 1, NS):
                    dve.wait_ge(mixed_out[g], 16 * s)
                dve.tensor_scalar(mixed[:, g, :], ps_y[:, g % 2, 0:T], vec_t[:, 8 + g:9 + g], vec_t[:, 12 + g:13 + g],
                                  ALU.add, ALU.mult).then_inc(y_step, 1)
                dve.wait_ge(y_step, 4 * s + g + 1)
                dve.tensor_tensor(mixed[:, g, :], mixed[:, g, :], gate_p[:, g, :], ALU.mult).then_inc(mixed_ready, 1)

            def body(s, e):
                done = 0
                for b in range(2):
                    if exists(s + 1, NS):
                        h_values(2 * s + 2 + b)
                    for g in (2 * b, 2 * b + 1):
                        done += g + 1
                        pooled_values(s, g, done)
                for g in range(NG):
                    mix(s, g)
            dve.wait_ge(tab_in, 32)
            for b in range(2):
                h_values(b)
            peeled(dve, HALF, lambda i: [body(2 * i + e, e) for e in range(2)])
            for k in range(3):
                dve.wait_ge(zs_done, k + 1)
                dve.tensor_copy(zs_b[:, k * 512:(k + 1) * 512], ps_z[k % 2][0:DB, :]).then_inc(zs_ready, 1)
            dve.wait_ge(prev_done, 1)
            dve.tensor_copy(prev[:], ps_y[0:PREV, 0, :]).then_inc(prev_ready, 1)

        @block.tensor
        def _(pe):
            def turn_x(n, b):
                pe.wait_ge(x_scaled, n + 1)
                if exists(n - 1, NB):
                    pe.wait_ge(h_ready, n)
                for c in range(KC):
                    last = pe.transpose(ps_x[:, c // 4, (c % 4) * P:(c % 4 + 1) * P], xt[:, b, c * P:(c + 1) * P], ident[:])
                last.then_inc(x_turned, 1)

            def group(s, e, g):
                if g >= 2:
                    pe.wait_ge(u_kept, 4 * s + g - 1)
                elif exists(s - 1, NS):
                    pe.wait_ge(u_kept, 4 * (s - 1) + g + 3)
                for off, at in ((OFF_U, 0), (OFF_GP, T)):
                    cols = slice(off + g * P, off + (g + 1) * P)
                    for c in range(KC):
                        last = mm3(pe, ps_u[:, g % 2, at:at + T], [wb[0][:, c, cols], wb[1][:, c, cols]],
                                   [hb[0][:, e, c, :], hb[1][:, e, c, :]], c == 0, c == KC - 1)
                last.then_inc(u_done, 1)

            def body(s, e):
                pe.wait_ge(h_lo, 2 * s + 2)
                for b in range(2):
                    if exists(s + 1, NS):
                        turn_x(2 * s + 2 + b, b)
                    group(s, e, 2 * b)
                    group(s, e, 2 * b + 1)
                for b in range(2):
                    if exists(s - 1, NS):
                        pe.wait_ge(a_kept, 2 * (s - 1) + b + 1)
                    for c in range(KC):
                        cols = slice(b * P, (b + 1) * P)
                        last = mm3(pe, ps_a[:, b, :], [hb[0][:, e, c, cols], hb[1][:, e, c, cols]],
                                   [wb[0][:, c, 0:DATT], wb[1][:, c, 0:DATT]], c == 0, c == KC - 1)
                    last.then_inc(a_done, 1)
                for g in range(NG):
                    pe.wait_ge(pooled_ready, 4 * s + g + 1)
                    if g >= 2:
                        pe.wait_ge(y_step, 4 * s + g - 1)
                    elif exists(s - 1, NS):
                        pe.wait_ge(y_step, 4 * (s - 1) + g + 3)
                    pe.matmul(ps_y[:, g % 2, 0:T], w_pool[:, g, :], pooled[:, g, :], start=True, stop=True).then_inc(y_done, 1)
            for b in range(2):
                turn_x(b, b)
            peeled(pe, HALF, lambda i: [body(2 * i + e, e) for e in range(2)])
            pe.wait_ge(a_kept, NB)
            for k in range(3):
                if k == 2:
                    pe.wait_ge(zs_ready, 1)
                for c in range(KC):
                    cols = slice(k * 512, (k + 1) * 512)
                    last = mm3(pe, ps_z[k % 2], [hs[0][:, c, :], hs[1][:, c, :]],
                               [wb[0][:, c, cols], wb[1][:, c, cols]], c == 0, c == KC - 1)
                last.then_inc(zs_done, 1)
            pe.wait_ge(y_step, 4 * NS)
            for g in range(NG):
                last = pe.transpose(ps_y[0:PREV, 0, g * P:(g + 1) * P], u_ext[:, g, T:], ident[:])
            last.then_inc(prev_done, 1)

    VW = VD + 1
    tiles = [(I, j) for I in range(NGRP) for j in range(GRP * I + GRP)]
    chunks = [(I, r, c) for I in range(NGRP) for r in range(GRP) for c in range(I + 1)]
    NT, NCH = len(tiles), len(chunks)
    assert NT % 4 == 0 and NCH % 2 == 0

    def tile_cols(k):
        I, j = tiles[k]
        c0 = max(0, j - GRP * I) * P
        return c0, GRP * P - c0

    def side_work():
        side = [[] for _ in range(NT)]
        for k, c in ((1, 0), (3, 1), (5, 2), (8, 3)):
            side[k].append(("prepare", c))
        start = 6
        for n in range(NCH):
            k = start + n * (NT - start) // NCH
            if n:
                k = max(k, last_k)
            last_k = k
            side[k].append(("maxima", n))
            if n + 1 == NCH or chunks[n + 1][0] != chunks[n][0]:
                I = chunks[n][0]
                if I < NGRP - 1:
                    side[max(k + 2, 9)].append(("turn", I))
        return side
    side = side_work()

    def first_work():
        steps, nv = [], 0
        for n in range(NCH):
            while nv * NCH < n * NB:
                steps.append(("values", nv))
                nv += 1
            steps.append(("maxima", n))
            if n + 1 < NCH and chunks[n + 1][0] != chunks[n][0]:
                steps.append(("turn", chunks[n][0]))
        return steps + [("values", n) for n in range(nv, NB)]
    first = first_work()
    LASTG = NGRP - 1
    LAG = 2
    LAST = [max(k for k in range(NT) if tiles[k][0] == I) for I in range(NGRP)]
    group_end = {k: tiles[k][0] for k in range(NT) if k + 1 == NT or tiles[k + 1][0] != tiles[k][0]}

    def ended(h, k, after):
        t = k - after
        return (0, group_end[t]) if t in group_end else (-1, group_end[t + NT]) if t + NT in group_end else None

    with ExitStack() as ctx:
        sems = []
        ctx.callback(release, nc, sems)

        def psum(name, shape):
            return ctx.enter_context(nc.psum_tensor("att_" + name, shape, F32))

        def sem(name):
            return stage_semaphore(nc, sems, "att_" + name)

        lat_lo = nc.alloc_sbuf_tensor_at("lat_lo", [P, 3, S], F32R, offset=after_lat - 3 * S * 4)
        m = Map(nc, after_lat)
        lat_hi = m("lat_hi", [P, 3, S], F32R)
        v = m("v", [P, NB, H, VW], F32)
        q = [[m(f"q_hi{e}", [P, S], F32R), m(f"q_lo{e}", [P, S], F32R)] for e in range(2)]
        kk = [[m(f"k_hi{e}", [P, S], F32R), m(f"k_lo{e}", [P, S], F32R)] for e in range(2)]
        rope = m("rope", [P, S], F32)
        q32 = m("q32", [P, 2, 512], F32)
        rot = m("att_rot", [P, 512], F32)
        wq_raw = m("wq_raw", [P, QC, P], F32)
        wk_raw = m("wk_raw", [P, VD], F32)
        wq = [m("wq_hi", [P, QC, P], F32R), m("wq_lo", [P, QC, P], F32R)]
        wk = [m("wk_hi", [P, P], F32R), m("wk_lo", [P, P], F32R)]
        mx = m("mx", [P, 2, GRP, NGRP], F32)
        negm = m("negm", [P, 2, GRP], F32)
        rec = m("rec", [P, 2, GRP], F32)
        att = m("att", [P, 2, GRP, VD], F32)
        VS = NB * VW + P - VW
        vh = [[m(f"v_hi{e}", [P, VS], F32R), m(f"v_lo{e}", [P, VS], F32R)] for e in range(2)]
        ot = m("o_cols", [P, 512], F32)
        early_map = Map(nc, m.at)
        pt = m("pt", [P, 2, 512], F32)
        ph = [m("pt_hi", [P, 4, 512], F32R), m("pt_lo", [P, 4, 512], F32R)]
        wv = [early_map("wv_hi", [P, DATT], F32R), early_map("wv_lo", [P, DATT], F32R)]
        wv_raw = early_map("wv_raw", [P, DATT], F32)
        kr = early_map("kr_rows", [P, NB, ROPE], F32)
        kr_cols = early_map("kr_cols", [P, S], F32)
        ps_s, ps_p, ps_o = psum("ps_s", [P, 2, 512]), psum("ps_p", [P, 2, 512]), psum("ps_o", [P, 2, 512])
        ps_q, ps_k = psum("ps_q", [P, 512]), psum("ps_k", [P, 512])

        kr_in, wv_in, rope_in, wq_in = sem("kr_in"), sem("wv_in"), sem("rope_in"), sem("wq_in")
        lat_hi_ready, filled = sem("lat_hi_ready"), sem("filled")
        lat_lo_ready = [sem("lat_lo_ready0"), sem("lat_lo_ready1")]
        wv_hi_ready, wv_ready, wq_hi_ready, wq_ready = sem("wv_hi_ready"), sem("wv_ready"), sem("wq_hi_ready"), sem("wq_ready")
        kr_turned, kr_copied, kr_hi_ready, kr_lo_ready, v_done, v_kept = (
            sem("kr_turned"), sem("kr_copied"), sem("kr_hi_ready"), sem("kr_lo_ready"), sem("v_done"), sem("v_kept"))
        q_done, k_done, q_read, q32_ready, q_hi_ready, q_lo_ready, k_hi_ready, k_kept = (
            sem("q_done"), sem("k_done"), sem("q_read"), sem("q32_ready"), sem("q_hi_ready"), sem("q_lo_ready"),
            sem("k_hi_ready"), sem("k_kept"))
        chunk_done, chunk_read, negm_ready, m_turned, m_kept = (
            sem("chunk_done"), sem("chunk_read"), sem("negm_ready"), sem("m_turned"), sem("m_kept"))
        scores_done, exp_done, pv_done, rec_ready, att_ready = (
            sem("scores_done"), sem("exp_done"), sem("pv_done"), sem("rec_ready"), sem("att_ready"))
        p_lo_ready = [sem("p_lo_ready0"), sem("p_lo_ready1")]
        vh_hi_ready, vh_ready, ot_ready, ot_turned = sem("vh_hi_ready"), sem("vh_ready"), sem("ot_ready"), sem("ot_turned")
        att_out = [sem("att_out0"), sem("att_out1")]
        wuq = t["w_uq"].rearrange("a (c p) h d -> p (a c) h d", p=P)
        wuk = t["w_uk"].rearrange("a k h d -> k (a h) d")
        att_groups = att_d.rearrange("(g r p) (h d) -> p g r h d", p=P, r=GRP, h=H)
        HP = H // 2
        block = ctx.enter_context(nc.Block())

        @block.sync
        def _(sp):
            def load_weights(g):
                one = ds(g, 1)
                sp.dma_start(wq_raw[:, :, 0:QK].unsqueeze(2), wuq[:, :, one, :]).then_inc(wq_in, 16)
                sp.dma_start(wq_raw[:, :, QK:QK + 16].unsqueeze(2), wuq[:, :, one, NOPE + 16:QK]).then_inc(wq_in, 16)
                sp.dma_start(wq_raw[:, :, QK + 16:P].unsqueeze(2), wuq[:, :, one, NOPE:NOPE + 16]).then_inc(wq_in, 16)
                sp.dma_start(wk_raw[:].unsqueeze(1), wuk[:, one, :]).then_inc(wq_in, 16)

            def store(h, I):
                sp.wait_ge(att_ready, NGRP * h + I + 1)
                sp.dma_start(att_groups[:, I, :, ds(h, 1), :].squeeze(2), att[:, I % 2]).then_inc(att_out[I % 2], 16)

            def body(h, e):
                if exists(h + 2, H):
                    sp.wait_ge(wq_ready, h + 2)
                    load_weights(h + 2)
                for I in range(NGRP):
                    store(h, I)
            load_weights(0)
            sp.dma_start(kr[:], kr_out).then_inc(kr_in, 16)
            sp.dma_start(wv_raw[:], t["w_uv"].rearrange("a k h d -> (a k) (h d)")).then_inc(wv_in, 16)
            sp.dma_start(rope[:], t["c_rope_cols"]).then_inc(rope_in, 16)
            sp.wait_ge(wq_ready, 1)
            load_weights(1)
            peeled(sp, HP, lambda i: [body(2 * i + e, e) for e in range(2)])
            for e in range(2):
                sp.wait_ge(att_out[e], 16 * H * NGRP // 2)

        @block.scalar
        def _(act):
            def prepare(g, slot, c):
                cols = slice(c * 512, (c + 1) * 512)
                act.wait_ge(k_done, NGRP * g + c + 1)
                act.activation(kk[slot][0][0:NOPE, cols], ps_k[0:NOPE, :], ACT.Copy).then_inc(k_hi_ready, 1)
                act.wait_ge(q32_ready, NGRP * g + c + 1)
                act.activation(q[slot][0][0:QK, cols], q32[0:QK, c % 2, :], ACT.Copy).then_inc(q_hi_ready, 1)

            def keep_max(g, slot, I):
                act.wait_ge(m_turned, NGRP * g + I + 1)
                act.activation(q[slot][0][QK:QK + 1, I * 512:(I + 1) * 512], ps_k[0:1, :], ACT.Copy).then_inc(m_kept, 1)

            def weights_high(g):
                act.wait_ge(wq_in, 64 * g + 64)
                if exists(g - 1, H):
                    act.wait_ge(k_done, NGRP * g)
                act.activation(wq[0][:], wq_raw[:], ACT.Copy)
                act.activation(wk[0][:, 0:NOPE], wk_raw[:], ACT.Copy).then_inc(wq_hi_ready, 1)

            def exponentials(h, k):
                c0, n = tile_cols(k)
                act.wait_ge(scores_done, NT * h + k + 1)
                if exists(NT * h + k - 2, NT * H):
                    act.wait_ge(p_lo_ready[k % 2], NT // 2 * h + k // 2)
                if exists(NT * h + k - 4, NT * H):
                    act.wait_ge(pv_done, NT * h + k - 3)
                act.activation(pt[:, k % 2, 0:n], ps_s[:, k % 2, 0:n], ACT.Exp, scale=SCALE)
                act.activation(ph[0][:, k % 4, 0:n], ps_s[:, k % 2, 0:n], ACT.Exp, scale=SCALE).then_inc(exp_done, 1)

            def values_high(g, slot):
                if exists(g - 2, H):
                    act.wait_ge(pv_done, NT * (g - 1))
                act.activation(vh[slot][0][:, 0:NB * VW].rearrange("p (n c) -> p n c", c=VW), v[:, :, ds(g, 1), :].squeeze(2),
                               ACT.Copy).then_inc(vh_hi_ready, 1)

            def keep_out(h, I):
                act.wait_ge(pv_done, NT * h + LAST[I] + 1)
                if exists(NGRP * h + I - 1, NGRP * H):
                    act.wait_ge(ot_turned, NGRP * h + I)
                act.activation(ot[0:VW, :], ps_o[0:VW, I % 2, :], ACT.Copy).then_inc(ot_ready, 1)

            def body(h, e):
                for k in range(NT):
                    exponentials(h, k)
                    if k == 1:
                        keep_max(h, e, LASTG)
                    if exists(h + 1, H):
                        for what, n in side[k]:
                            if what == "prepare":
                                prepare(h + 1, 1 - e, n)
                            elif what == "turn":
                                keep_max(h + 1, 1 - e, n)
                    if k == NT // 2 and exists(h + 2, H):
                        weights_high(h + 2)
                    if k == 14 and exists(h + 1, H):
                        values_high(h + 1, 1 - e)
                    end = ended(h, k, LAG)
                    if end and exists(h + end[0], H):
                        keep_out(h + end[0], end[1])
            weights_high(0)
            for c in range(NGRP):
                act.activation(lat_hi[:, :, c * 512:(c + 1) * 512], lat_t[:, :, c * 512:(c + 1) * 512],
                               ACT.Copy).then_inc(lat_hi_ready, 1)
                if c == 0:
                    act.wait_ge(wv_in, 16)
                    act.activation(wv[0][:], wv_raw[:], ACT.Copy).then_inc(wv_hi_ready, 1)
            act.wait_ge(filled, 1)
            for c in range(NGRP):
                cols = slice(c * 512, (c + 1) * 512)
                act.wait_ge(kr_turned, c + 1)
                act.activation(kr_cols[NOPE:QK, cols], (ps_s if c < 2 else ps_p)[0:ROPE, c % 2, :], ACT.Copy).then_inc(kr_copied, 1)
                act.wait_ge(kr_copied, c + 1)
                for e in range(2):
                    last = act.activation(kk[e][0][NOPE:QK, cols], kr_cols[NOPE:QK, cols], ACT.Copy)
                last.then_inc(kr_hi_ready, 1)
                prepare(0, 0, c)
            weights_high(1)
            for what, n in first:
                if what == "values":
                    act.wait_ge(v_done, n + 1)
                    act.activation(v[:, n, :, 0:VD], ps_o[:, n % 2, :].rearrange("p (h d) -> p h d", h=H),
                                   ACT.Copy).then_inc(v_kept, 1)
                elif what == "turn":
                    keep_max(0, 0, n)
            act.wait_ge(v_kept, NB)
            values_high(0, 0)
            peeled(act, HP, lambda i: [body(2 * i + e, e) for e in range(2)])
            keep_out(H - 1, LASTG)

        @block.gpsimd
        def _(pool):
            def weights_low(g):
                pool.wait_ge(wq_hi_ready, g + 1)
                pool.tensor_tensor(wq[1][:], wq_raw[:], wq[0][:].bitcast(F32), ALU.subtract)
                pool.tensor_tensor(wk[1][:, 0:NOPE], wk_raw[:], wk[0][:, 0:NOPE].bitcast(F32),
                                   ALU.subtract).then_inc(wq_ready, 1)

            def low_latents(c):
                cols = slice(c * 512, (c + 1) * 512)
                pool.wait_ge(lat_hi_ready, c + 1)
                pool.tensor_tensor(lat_lo[:, :, cols], lat_t[:, :, cols], lat_hi[:, :, cols].bitcast(F32),
                                   ALU.subtract).then_inc(lat_lo_ready[1], 1)

            def q_low(g, slot, c):
                cols = slice(c * 512, (c + 1) * 512)
                pool.wait_ge(q_hi_ready, NGRP * g + c + 1)
                pool.tensor_tensor(q[slot][1][0:QK, cols], q32[0:QK, c % 2, :], q[slot][0][0:QK, cols].bitcast(F32),
                                   ALU.subtract).then_inc(q_lo_ready, 1)

            def values_low(g, slot):
                pool.wait_ge(vh_hi_ready, g + 1)
                hi, lo = (part[:, 0:NB * VW].rearrange("p (n c) -> p n c", c=VW) for part in vh[slot])
                pool.tensor_tensor(lo, v[:, :, ds(g, 1), :].squeeze(2), hi.bitcast(F32), ALU.subtract).then_inc(vh_ready, 1)

            def split(h, k):
                n = tile_cols(k)[1]
                pool.wait_ge(exp_done, NT * h + k + 1)
                pool.tensor_tensor(ph[1][:, k % 4, 0:n], pt[:, k % 2, 0:n], ph[0][:, k % 4, 0:n].bitcast(F32),
                                   ALU.subtract).then_inc(p_lo_ready[1], 1)

            def body(h, e):
                for k in range(NT):
                    if k % 2:
                        split(h, k)
                    if exists(h + 1, H):
                        for what, n in side[k]:
                            if what == "prepare":
                                q_low(h + 1, 1 - e, n)
                        if k == 14:
                            values_low(h + 1, 1 - e)
                    if k == NT // 2 and exists(h + 2, H):
                        weights_low(h + 2)
            for e in range(2):
                last = pool.memset(kk[e][0][:].bitcast(F32), 1.0)
            last.then_inc(filled, 1)
            for part in wk:
                pool.memset(part[:, NOPE:P].bitcast(F32), 0.0)
            for e in range(2):
                for part in vh[e]:
                    pool.memset(part[:, NB * VW:].bitcast(F32), 0.0)
            pool.memset(v[:, :, :, VD:VW], 1.0).then_inc(filled, 1)
            weights_low(0)
            low_latents(1)
            pool.wait_ge(wv_hi_ready, 1)
            pool.tensor_tensor(wv[1][:], wv_raw[:], wv[0][:].bitcast(F32), ALU.subtract).then_inc(wv_ready, 1)
            low_latents(3)
            for c in range(NGRP):
                q_low(0, 0, c)
            weights_low(1)
            values_low(0, 0)
            peeled(pool, HP, lambda i: [body(2 * i + e, e) for e in range(2)])

        @block.vector
        def _(dve):
            def prepare(g, slot, c):
                cols = slice(c * 512, (c + 1) * 512)
                dve.wait_ge(q_done, NGRP * g + c + 1)
                if exists(NGRP * g + c - 2, NGRP * H):
                    dve.wait_ge(q_lo_ready, NGRP * g + c - 1)
                if exists(NGRP * g + c - 1, NGRP * H):
                    dve.wait_ge(q32_ready, NGRP * g + c)
                dve.tensor_tensor(rot[NOPE:QK, :], ps_q[QK:P, :], rope[QK:P, cols], ALU.mult)
                dve.tensor_tensor(q32[0:QK, c % 2, :], ps_q[0:QK, :], rope[0:QK, cols], ALU.mult).then_inc(q_read, 1)
                dve.wait_ge(q_read, NGRP * g + c + 1)
                dve.tensor_tensor(q32[NOPE:QK, c % 2, :], q32[NOPE:QK, c % 2, :], rot[NOPE:QK, :], ALU.add).then_inc(q32_ready, 1)
                dve.wait_ge(k_hi_ready, NGRP * g + c + 1)
                dve.tensor_tensor(kk[slot][1][0:NOPE, cols], ps_k[0:NOPE, :], kk[slot][0][0:NOPE, cols].bitcast(F32),
                                  ALU.subtract).then_inc(k_kept, 1)

            def maxima(g, n):
                I, r, c = chunks[n]
                width = 512 if c < I else (r + 1) * P
                if r == 0 and c == 0 and exists(NGRP * g + I - 2, NGRP * H):
                    dve.wait_ge(negm_ready, NGRP * g + I - 1)
                dve.wait_ge(chunk_done, NCH * g + n + 1)
                dve.tensor_reduce(mx[:, I % 2, r, c:c + 1], ps_p[:, n % 2, 0:width], AX.X, ALU.max).then_inc(chunk_read, 1)
                if r == GRP - 1 and c == I:
                    dve.wait_ge(chunk_read, NCH * g + n + 1)
                    if exists(NGRP * g + I - 2, NGRP * H):
                        dve.wait_ge(m_turned, NGRP * g + I - 1)
                    dve.tensor_reduce(negm[:, I % 2, :], mx[:, I % 2, :, 0:I + 1], AX.X, ALU.max,
                                      negate=True).then_inc(negm_ready, 1)

            def split(h, k):
                n = tile_cols(k)[1]
                dve.wait_ge(exp_done, NT * h + k + 1)
                dve.tensor_tensor(ph[1][:, k % 4, 0:n], pt[:, k % 2, 0:n], ph[0][:, k % 4, 0:n].bitcast(F32),
                                  ALU.subtract).then_inc(p_lo_ready[0], 1)

            def finish(h, I):
                dve.wait_ge(ot_turned, NGRP * h + I + 1)
                sums = ps_o[:, I % 2, 0:GRP * VW].rearrange("p (r c) -> p r c", r=GRP)
                dve.reciprocal(rec[:, I % 2, :].unsqueeze(2), sums[:, :, VD:VW]).then_inc(rec_ready, 1)
                dve.wait_ge(rec_ready, NGRP * h + I + 1)
                if exists(NGRP * h + I - 2, NGRP * H):
                    dve.wait_ge(att_out[I % 2], 16 * (2 * h + I // 2))
                dve.tensor_tensor(att[:, I % 2], sums[:, :, 0:VD], rec[:, I % 2, :].unsqueeze(2).broadcast_to([P, GRP, VD]),
                                  ALU.mult).then_inc(att_ready, 1)

            def body(h, e):
                for k in range(NT):
                    if exists(h + 1, H):
                        for what, n in side[k]:
                            if what == "prepare":
                                prepare(h + 1, 1 - e, n)
                            elif what == "maxima":
                                maxima(h + 1, n)
                    if k % 2 == 0:
                        split(h, k)
                    end = ended(h, k, LAG + 3)
                    if end and exists(h + end[0], H):
                        finish(h + end[0], end[1])
            for c in range(0, NGRP, 2):
                cols = slice(c * 512, (c + 1) * 512)
                dve.wait_ge(lat_hi_ready, c + 1)
                dve.tensor_tensor(lat_lo[:, :, cols], lat_t[:, :, cols], lat_hi[:, :, cols].bitcast(F32),
                                  ALU.subtract).then_inc(lat_lo_ready[0], 1)
            dve.wait_ge(rope_in, 16)
            for c in range(NGRP):
                prepare(0, 0, c)

            def rotary_low(e):
                dve.wait_ge(kr_hi_ready, NGRP)
                dve.tensor_tensor(kk[e][1][NOPE:QK, :], kr_cols[NOPE:QK, :], kk[e][0][NOPE:QK, :].bitcast(F32),
                                  ALU.subtract).then_inc(kr_lo_ready, 1)
            for what, n in first:
                if what == "maxima":
                    maxima(0, n)
            for e in range(2):
                rotary_low(e)
            peeled(dve, HP, lambda i: [body(2 * i + e, e) for e in range(2)])
            finish(H - 1, LASTG)

        @block.tensor
        def _(pe):
            def prepare(g, slot, c):
                cols = slice(c * 512, (c + 1) * 512)
                pe.wait_ge(wq_ready, g + 1)
                if exists(NGRP * g + c - 1, NGRP * H):
                    pe.wait_ge(q_read, NGRP * g + c)
                for j in range(QC):
                    last = mm3(pe, ps_q[:], [wq[0][:, j, :], wq[1][:, j, :]], [lat_hi[:, j, cols], lat_lo[:, j, cols]],
                               j == 0, j == QC - 1)
                last.then_inc(q_done, 1)
                if exists(NGRP * g + c - 1, NGRP * H):
                    pe.wait_ge(k_kept, NGRP * g + c)
                if exists(g - 1, H):
                    pe.wait_ge(m_kept, NGRP * g)
                mm3(pe, ps_k[:], [wk[0][:], wk[1][:]], [lat_hi[:, QC, cols], lat_lo[:, QC, cols]],
                    True, True).then_inc(k_done, 1)

            def maxima(g, slot, n):
                I, r, c = chunks[n]
                width = 512 if c < I else (r + 1) * P
                at = (GRP * I + r) * P
                if r == 0 and c == 0:
                    pe.wait_ge(q_hi_ready, NGRP * g + I + 1)
                    pe.wait_ge(k_hi_ready, NGRP * g + I + 1)
                if exists(NCH * g + n - 2, NCH * H):
                    pe.wait_ge(chunk_read, NCH * g + n - 1)
                last = pe.matmul(ps_p[:, n % 2, 0:width], q[slot][0][0:QK, at:at + P],
                                 kk[slot][0][0:QK, c * 512:c * 512 + width], start=True, stop=(c < I))
                if c == I:
                    last = pe.matmul(ps_p[:, n % 2, width - P:width], identb[:], mask_q[:], start=False, stop=True)
                last.then_inc(chunk_done, 1)

            def turn(g, I):
                pe.wait_ge(negm_ready, NGRP * g + I + 1)
                pe.wait_ge(k_kept, NGRP * g + NGRP)
                if exists(NGRP * g + I - 1, NGRP * H):
                    pe.wait_ge(m_kept, NGRP * g + I)
                for r in range(GRP):
                    last = pe.transpose(ps_k[0:1, r * P:(r + 1) * P], negm[:, I % 2, r:r + 1], ident[:])
                last.then_inc(m_turned, 1)

            def scores(h, slot, k):
                I, j = tiles[k]
                c0, n = tile_cols(k)
                cols = slice(I * 512 + c0, (I + 1) * 512)
                keys = slice(j * P, (j + 1) * P)
                out = ps_s[:, k % 2, 0:n]
                if j == 0:
                    pe.wait_ge(m_kept, NGRP * h + I + 1)
                    if I == 0:
                        pe.wait_ge(q_lo_ready, NGRP * h + NGRP)
                if exists(NT * h + k - 2, NT * H):
                    pe.wait_ge(exp_done, NT * h + k - 1)
                pe.matmul(out, kk[slot][0][0:QK + 1, keys], q[slot][0][0:QK + 1, cols], start=True, stop=False)
                pe.matmul(out, kk[slot][0][0:QK, keys], q[slot][1][0:QK, cols], start=False, stop=False)
                last = pe.matmul(out, kk[slot][1][0:QK, keys], q[slot][0][0:QK, cols], start=False, stop=(j < GRP * I))
                if j >= GRP * I:
                    last = pe.matmul(ps_s[:, k % 2, 0:P], identb[:], mask_k[:], start=False, stop=True)
                last.then_inc(scores_done, 1)

            def values(h, e, k):
                I, j = tiles[k]
                c0, n = tile_cols(k)
                pe.wait_ge(exp_done, NT * h + k + 1)
                pe.wait_ge(p_lo_ready[k % 2], NT // 2 * h + k // 2 + 1)
                if k == 0:
                    pe.wait_ge(vh_ready, h + 1)
                if j == 0 and exists(NGRP * h + I - 2, NGRP * H):
                    pe.wait_ge(att_ready, NGRP * h + I - 1)
                block = slice(j * VW, j * VW + P)
                mm3(pe, ps_o[:, I % 2, c0:c0 + n], [part[:, block] for part in vh[e]], [part[:, k % 4, 0:n] for part in ph],
                    j == 0, j == GRP * I + GRP - 1).then_inc(pv_done, 1)

            def turn_out(h, I):
                pe.wait_ge(ot_ready, NGRP * h + I + 1)
                for r in range(GRP):
                    last = pe.transpose(ps_o[:, I % 2, r * VW:(r + 1) * VW], ot[0:VW, r * P:(r + 1) * P], ident[0:VW, 0:VW])
                last.then_inc(ot_turned, 1)

            def body(h, e):
                for k in range(NT):
                    scores(h, e, k)
                    if k == 1:
                        turn(h, LASTG)
                    if exists(h + 1, H):
                        for what, n in side[k]:
                            if what == "prepare":
                                prepare(h + 1, 1 - e, n)
                            elif what == "maxima":
                                maxima(h + 1, 1 - e, n)
                            else:
                                turn(h + 1, n)
                    if k >= LAG:
                        values(h, e, k - LAG)
                    elif exists(h - 1, H):
                        values(h - 1, 1 - e, NT + k - LAG)
                    end = ended(h, k, LAG + 2)
                    if end and exists(h + end[0], H):
                        turn_out(h + end[0], end[1])
            pe.wait_ge(kr_in, 16)
            for n in range(NB):
                c = n // GRP
                last = pe.transpose((ps_s if c < 2 else ps_p)[0:ROPE, c % 2, (n % GRP) * P:(n % GRP + 1) * P], kr[:, n, :], ident[:])
                if n % GRP == GRP - 1:
                    last.then_inc(kr_turned, 1)
            for c in range(NGRP):
                pe.wait_ge(lat_lo_ready[c % 2], c // 2 + 1)
                prepare(0, 0, c)
            pe.wait_ge(wv_ready, 1)
            pe.wait_ge(kr_hi_ready, NGRP)
            for what, n in first:
                if what == "values":
                    if n >= 2:
                        pe.wait_ge(v_kept, n - 1)
                    cols = slice(n * P, (n + 1) * P)
                    mm3(pe, ps_o[:, n % 2, :], [lat_hi[:, QC, cols], lat_lo[:, QC, cols]], [wv[0][:], wv[1][:]],
                        True, True).then_inc(v_done, 1)
                elif what == "maxima":
                    maxima(0, 0, n)
                else:
                    turn(0, n)
            pe.wait_ge(filled, 2)
            pe.wait_ge(v_kept, NB)
            pe.wait_ge(kr_lo_ready, 2)
            peeled(pe, HP, lambda i: [body(2 * i + e, e) for e in range(2)])
            for k in range(NT - LAG, NT):
                values(H - 1, 1, k)
            turn_out(H - 1, LASTG)

    stay = Map(nc, after_lat)
    wo = [stay("wo_hi", [P, KC, D], F32R), stay("wo_lo", [P, KC, D], F32R)]
    ms = [stay("ms_hi", [P, KC, P], F32R), stay("ms_lo", [P, KC, P], F32R)]
    ck = [stay(f"ck{e}", [P, TPP, KVL], F32) for e in range(2)]
    cr = [stay(f"cr{e}", [P, TPP, ROPE], F32) for e in range(2)]
    wuv_s = stay("s_wuv", [P, DATT], F32)
    crow = stay("s_crow", [1, DB, KVL], F32)
    qabs = stay("s_qabs", [P, DB, H], F32)
    qr = stay("s_qr", [P, DB, GRP, H], F32)
    new_row = stay("s_new_row", [1, DB, H], F32)
    new_col = stay("s_new_col", [H, DB], F32)
    page_x = stay("s_page_x", [P, DB], U32)
    m2 = Map(nc, after_lat - 3 * S * 4)
    z = m2("s_z", [DB, DIN], F32)
    mixed = m2("s_mixed", [DB, D], F32)
    cache_in = [nc.alloc_semaphore("cache_in0"), nc.alloc_semaphore("cache_in1")]
    QT = TPP // GRP
    ckv_q = t["cache_ckv"].rearrange("a n (c s) k -> (a n c) (s k)", c=QTR)
    kr_q = t["cache_krope"].rearrange("a n (c s) k -> (a n c) (s k)", c=QTR)
    NQ = t["cache_ckv"].shape[1] * QTR

    def gather(pool, n, e):
        for tile, rows in ((ck[e], ckv_q), (cr[e], kr_q)):
            pool.indirect_dma_start(tile[:].rearrange("p s k -> p (s k)"), None, rows,
                                    bass.IndirectOffsetOnAxis(ap=page_x[:, n:n + 1], axis=0),
                                    bounds_check=NQ - 1, oob_is_err=True).then_inc(cache_in[e], 16)

    with ExitStack() as ctx:
        sems = []
        ctx.callback(release, nc, sems)

        def psum(name, shape):
            return ctx.enter_context(nc.psum_tensor("smp_" + name, shape, F32))

        def sem(name):
            return stage_semaphore(nc, sems, "smp_" + name)

        m = Map(nc, stay.at)
        NW = 4
        wo_raw = m("wo_raw", [P, NW, D], F32)
        state = m("state", [DB, sum((2 << g) - 1 for g in range(NG)), P], F32)
        ms2 = Map(nc, m2.at)
        junk = ms2("s_junk", [DB, OFF_KR], F32)
        lat = ms2("s_lat", [DB, LA], F32)
        rot = ms2("s_rot", [DB, H, ROPE], F32)
        wsum = ms2("s_wsum", [DB, DPOOL], F32)
        assert ms2.at <= after_lat
        wuq_s = m("s_wuq", [P, QC, H * QK], F32)
        wuk_s = m("s_wuk", [P, H * NOPE], F32)
        wp_s = m("s_wpool", [P, NG, P], F32)
        rows = m("s_rows", [DB, 2, DPOOL], F32)
        qn_w = m("s_qn_w", [DB, QL + KVL], F32)
        tab = m("s_tab", [DB, 2, ROPE], F32)
        stat = m("s_stat", [DB, 2], F32)
        lat_c = m("s_lat_c", [P, 3, DB], F32)
        krt = m("s_krt", [ROPE, DB], F32)
        qrow = m("s_q", [DB, H, QK], F32)
        qn_c = m("s_qn_c", [NOPE, H, DB], F32)
        wuk_t = m("s_wuk_t", [NOPE, H, P], F32)
        page_i = m("s_page_i", [DB, NPG], I32)
        page_f = m("s_page_f", [DB, NPG], F32)
        page_c = m("s_page_c", [NPG, DB], F32)
        spread = m("s_spread", [NPG, P], F32)
        quarter = m("s_quarter", [P, 1], F32)
        pool_c = m("s_pool_c", [P, NG, DB], F32)
        ps_t = psum("ps_t", [P, 2, 512])
        ps_r = psum("ps_r", [P, 512])
        ps_s = psum("ps_s", [P, 2, 512])
        ps_m = psum("ps_m", [P, 512])
        ps_o = psum("ps_o", [P, 512])
        ps_a = psum("ps_a", [P, 512])

        z_in, tab_in, w_in2, state_in, page_in, crow_in = (
            sem("z_in"), sem("tab_in"), sem("w_in"), sem("state_in"), sem("page_in"), sem("crow_in"))
        wo_in = [sem(f"wo_in{k}") for k in range(NW)]
        page_turned = sem("page_turned")
        page_step, page_ready, ss_ready, var_ready, sd_ready, rot_step, lat_ready, kr_ready, silu_ready = (
            sem("page_step"), sem("page_ready"), sem("ss_ready"), sem("var_ready"), sem("sd_ready"), sem("rot_step"),
            sem("lat_ready"), sem("kr_ready"), sem("silu_ready"))
        setup_pe, setup_dve, out_done, zeroed = sem("setup_pe"), sem("setup_dve"), sem("out_done"), sem("zeroed")
        pool_pe, pool_dve = sem("pool_pe"), sem("pool_dve")
        wo_hi_ready = sem("wo_hi_ready")
        wo_lo_ready = [sem("wo_lo_ready0"), sem("wo_lo_ready1")]
        w_out = t["w_out"].rearrange("a (c p) n -> p (a c) n", p=P)
        prev = t["state_pool"].rearrange("a b s c -> (a b) s c")
        u_col = LA + OFF_U
        block = ctx.enter_context(nc.Block())

        @block.sync
        def _(sp):
            sp.dma_start(z[:], zs_d).then_inc(z_in, 16)
            sp.dma_start(page_i[:], t["page_table"]).then_inc(page_in, 16)
            sp.dma_start(spread[:], t["c_spread"]).then_inc(page_in, 16)
            sp.dma_start(quarter[:], t["c_quarter"]).then_inc(page_in, 16)
            sp.dma_start(qn_w[:, 0:QL], t["q_norm_w"].rearrange("a n -> (a n)").partition_broadcast(DB)).then_inc(tab_in, 16)
            sp.dma_start(qn_w[:, QL:], t["kv_norm_w"].rearrange("a n -> (a n)").partition_broadcast(DB)).then_inc(tab_in, 16)
            sp.dma_start(tab[:], t["c_rope_sample"].rearrange("t b r -> b t r")).then_inc(tab_in, 16)
            sp.dma_start(rows[:, 0, :], t["b_pool"].rearrange("a g c -> (a g c)").partition_broadcast(DB)).then_inc(tab_in, 16)
            sp.dma_start(rows[:, 1, :], t["pool_scale"].rearrange("a c -> (a c)").partition_broadcast(DB)).then_inc(tab_in, 16)
            at = 0
            for g in range(NG):
                w = 2 << g
                sp.dma_start(state[:, at:at + w - 1, :], prev[:, PREV + 1 - w:, g * P:(g + 1) * P]).then_inc(state_in, 16)
                at += w - 1
            sp.dma_start(o[7].rearrange("a b s c -> (a b) s c")[:, 0:PREV - 1, :], prev[:, 1:, :]).then_inc(out_done, 16)
            sp.dma_start(o[7].rearrange("a b s c -> (a b) s c")[:, PREV - 1:, :],
                         zs_d[:, u_col:u_col + DPOOL].unsqueeze(1)).then_inc(out_done, 16)
            sp.wait_ge(lat_ready, 1)
            sp.dma_start(o[5].rearrange("a b s k -> (a b s) k"), lat[:, OFF_KV:OFF_KR]).then_inc(out_done, 16)
            sp.dma_start(o[6].rearrange("a b s k -> (a b s) k"), lat[:, OFF_KR:LA]).then_inc(out_done, 16)
            sp.wait_ge(out_done, 64)
            sp.dma_start(crow[:], o[5].rearrange("a b s k -> (a s) b k")).then_inc(crow_in, 16)
            sp.wait_ge(crow_in, 16)

        @block.gpsimd
        def _(pool):
            pool.wait_ge(page_ready, 1)
            gather(pool, 0, 0)
            pool.memset(qr[:], 0.0)
            for part in ms:
                last = pool.memset(part[:].bitcast(F32), 0.0)
            last.then_inc(zeroed, 1)
            for n in range(0, KC, 2):
                pool.wait_ge(wo_hi_ready, n + 1)
                pool.tensor_tensor(wo[1][:, n, :], wo_raw[:, n % NW, :], wo[0][:, n, :].bitcast(F32),
                                   ALU.subtract).then_inc(wo_lo_ready[0], 1)

        @block.scalar
        def _(act):
            def load(n):
                act.dma_start(wo_raw[:, n % NW, :], w_out[:, n, :]).then_inc(wo_in[n % NW], 16)
            load(0)
            act.dma_start(wuq_s[:], t["w_uq"].rearrange("a (c p) h d -> p (a c) (h d)", p=P)).then_inc(w_in2, 16)
            load(1)
            act.dma_start(wuk_s[:], t["w_uk"].rearrange("a k h d -> (a k) (h d)")).then_inc(w_in2, 16)
            act.dma_start(wp_s[:], t["w_pool"].rearrange("a g c d -> c (a g) d")).then_inc(w_in2, 16)
            act.dma_start(wuv_s[:], t["w_uv"].rearrange("a k h d -> (a k) (h d)")).then_inc(w_in2, 16)
            for n in range(2, NW):
                load(n)
            act.wait_ge(z_in, 16)
            act.activation(junk[:, 0:QL], z[:, 0:QL], ACT.Square, accum_out=stat[:, 0:1])
            act.activation(junk[:, OFF_KV:OFF_KR], z[:, OFF_KV:OFF_KR], ACT.Square, accum_out=stat[:, 1:2]).then_inc(ss_ready, 1)
            act.wait_ge(var_ready, 1)
            act.activation(stat[:], stat[:], ACT.Sqrt).then_inc(sd_ready, 1)
            act.activation(z[:, LA:LA + DATT], z[:, LA:LA + DATT], ACT.Silu)
            act.activation(z[:, LA + OFF_GP:DIN], z[:, LA + OFF_GP:DIN], ACT.Silu).then_inc(silu_ready, 1)
            for n in range(KC):
                act.wait_ge(wo_in[n % NW], 16 * (n // NW + 1))
                act.activation(wo[0][:, n, :], wo_raw[:, n % NW, :], ACT.Copy).then_inc(wo_hi_ready, 1)
                if n >= 2 and n - 2 + NW < KC:
                    act.wait_ge(wo_lo_ready[n % 2], n // 2)
                    load(n - 2 + NW)

        @block.vector
        def _(dve):
            step = [0]

            def kept(ins):
                step[0] += 1
                ins.then_inc(setup_dve, 1)
                return step[0]

            def split(n):
                dve.wait_ge(wo_hi_ready, n + 1)
                dve.tensor_tensor(wo[1][:, n, :], wo_raw[:, n % NW, :], wo[0][:, n, :].bitcast(F32),
                                  ALU.subtract).then_inc(wo_lo_ready[1], 1)

            dve.wait_ge(page_in, 48)
            dve.tensor_copy(page_f[:], page_i[:]).then_inc(page_step, 1)
            dve.wait_ge(page_turned, 1)
            dve.tensor_copy(page_c[:], ps_o[0:NPG, 0:DB]).then_inc(page_step, 1)
            dve.wait_ge(page_turned, 2)
            dve.tensor_scalar(page_x[:], ps_o[:, DB:2 * DB], quarter[:], None, ALU.add).then_inc(page_ready, 1)
            dve.wait_ge(ss_ready, 1)
            dve.tensor_scalar(stat[:, 0:1], stat[:, 0:1], 1.0 / QL, EPS, ALU.mult, ALU.add)
            dve.tensor_scalar(stat[:, 1:2], stat[:, 1:2], 1.0 / KVL, EPS, ALU.mult, ALU.add).then_inc(var_ready, 1)
            dve.wait_ge(tab_in, 80)
            dve.tensor_tensor(lat[:, OFF_KR:LA], z[:, OFF_KR:LA], tab[:, 0, :], ALU.mult)
            dve.tensor_tensor(rot[:, 0, 0:16], z[:, OFF_KR + 16:LA], tab[:, 1, 0:16], ALU.mult)
            dve.tensor_tensor(rot[:, 0, 16:32], z[:, OFF_KR:OFF_KR + 16], tab[:, 1, 16:32], ALU.mult).then_inc(rot_step, 1)
            dve.wait_ge(rot_step, 1)
            dve.tensor_tensor(lat[:, OFF_KR:LA], lat[:, OFF_KR:LA], rot[:, 0, :], ALU.add).then_inc(rot_step, 1)
            dve.wait_ge(sd_ready, 1)
            dve.reciprocal(stat[:], stat[:]).then_inc(kr_ready, 1)
            dve.wait_ge(kr_ready, 1)
            dve.scalar_tensor_tensor(out=lat[:, 0:QL], in0=z[:, 0:QL], scalar=stat[:, 0:1], in1=qn_w[:, 0:QL],
                                     op0=ALU.mult, op1=ALU.mult)
            dve.scalar_tensor_tensor(out=lat[:, OFF_KV:OFF_KR], in0=z[:, OFF_KV:OFF_KR], scalar=stat[:, 1:2], in1=qn_w[:, QL:],
                                     op0=ALU.mult, op1=ALU.mult).then_inc(lat_ready, 1)
            dve.wait_ge(setup_pe, 1)
            dve.tensor_copy(lat_c[:], ps_m[:, 0:3 * DB].rearrange("p (c b) -> p c b", c=3))
            kept(dve.tensor_copy(krt[:], ps_m[0:ROPE, 3 * DB:4 * DB]))
            dve.wait_ge(state_in, 16 * NG)
            u = z[:, u_col:u_col + DPOOL]
            at = 0
            for g in range(NG):
                w = 2 << g
                cols = slice(g * P, (g + 1) * P)
                last = dve.tensor_reduce(wsum[:, cols], state[:, at:at + w - 1, :].rearrange("b s c -> b c s"), AX.X, ALU.add)
                at += w - 1
            last.then_inc(pool_dve, 1)
            dve.wait_ge(pool_dve, 1)
            dve.tensor_tensor(wsum[:], wsum[:], u, ALU.add).then_inc(pool_dve, 1)
            dve.wait_ge(pool_dve, 2)
            for g in range(NG):
                cols = slice(g * P, (g + 1) * P)
                last = dve.scalar_tensor_tensor(out=wsum[:, cols], in0=wsum[:, cols], scalar=1.0 / (2 << g), in1=u[:, cols],
                                                op0=ALU.mult, op1=ALU.subtract)
            last.then_inc(pool_dve, 1)
            split(1)
            dve.wait_ge(setup_pe, 2)
            kept(dve.tensor_copy(qrow[:].rearrange("b h d -> b (h d)").rearrange("b (k n) -> b k n", k=2),
                                 ps_s[0:DB, :, 0:H * QK // 2]))
            dve.wait_ge(setup_dve, 2)
            dve.tensor_tensor(rot[:, :, 0:16], qrow[:, :, NOPE + 16:QK],
                              tab[:, 1, 0:16].unsqueeze(1).broadcast_to([DB, H, 16]), ALU.mult)
            kept(dve.tensor_tensor(rot[:, :, 16:32], qrow[:, :, NOPE:NOPE + 16],
                                   tab[:, 1, 16:32].unsqueeze(1).broadcast_to([DB, H, 16]), ALU.mult))
            dve.wait_ge(setup_dve, 3)
            kept(dve.tensor_tensor(qrow[:, :, NOPE:QK], qrow[:, :, NOPE:QK],
                                   tab[:, 0, :].unsqueeze(1).broadcast_to([DB, H, ROPE]), ALU.mult))
            dve.wait_ge(setup_dve, 4)
            kept(dve.tensor_tensor(qrow[:, :, NOPE:QK], qrow[:, :, NOPE:QK], rot[:], ALU.add))
            dve.wait_ge(setup_pe, 3)
            kept(dve.tensor_copy(wuk_t[:].rearrange("p h k -> p (h k)").rearrange("p (a n) -> p a n", a=2), ps_t[0:NOPE]))
            dve.wait_ge(pool_pe, 1)
            dve.tensor_copy(pool_c[:], ps_a[:, 0:NG * DB].rearrange("p (g b) -> p g b", g=NG)).then_inc(pool_dve, 1)
            dve.wait_ge(setup_pe, 4)
            dve.tensor_copy(qn_c[:], ps_o[0:NOPE, 0:H * DB].rearrange("p (h b) -> p h b", h=H))
            dve.wait_ge(zeroed, 1)
            for g in range(GRP):
                last = dve.tensor_copy(qr[g * ROPE:(g + 1) * ROPE, :, g, :],
                                       ps_o[0:ROPE, H * DB:2 * H * DB].rearrange("p (h b) -> p b h", h=H))
            kept(last)
            dve.wait_ge(pool_pe, 2)
            dve.tensor_tensor(mixed[:, DATT:], ps_a[0:DB, :], rows[:, 0, :], ALU.add).then_inc(pool_dve, 1)
            split(3)
            dve.wait_ge(setup_pe, 5)
            kept(dve.tensor_copy(qabs[:], ps_m[:, 0:H * DB].rearrange("p (h b) -> p b h", h=H)))
            dve.wait_ge(pool_dve, 5)
            dve.tensor_tensor(mixed[:, DATT:], mixed[:, DATT:], rows[:, 1, :], ALU.mult).then_inc(pool_dve, 1)
            dve.wait_ge(pool_dve, 6)
            dve.wait_ge(silu_ready, 1)
            dve.tensor_tensor(mixed[:, DATT:], mixed[:, DATT:], z[:, LA + OFF_GP:DIN], ALU.mult).then_inc(pool_dve, 1)
            dve.wait_ge(setup_pe, 6)
            dve.tensor_copy(new_row[:], ps_a[0:1, 0:DB * H].rearrange("p (b h) -> p b h", b=DB))
            kept(dve.tensor_copy(new_col[:], ps_r[0:H, 0:DB]))

            split(5)
            split(7)

        @block.tensor
        def _(pe):
            pe.wait_ge(page_step, 1)
            pe.transpose(ps_o[0:NPG, 0:DB], page_f[:], ident[0:DB, 0:DB]).then_inc(page_turned, 1)
            pe.wait_ge(page_step, 2)
            pe.matmul(ps_o[:, DB:2 * DB], spread[:], page_c[:], start=True, stop=True).then_inc(page_turned, 1)
            pe.wait_ge(lat_ready, 1)
            for c in range(3):
                pe.transpose(ps_m[:, c * DB:(c + 1) * DB], lat[:, c * P:(c + 1) * P], ident[0:DB, 0:DB])
            pe.transpose(ps_m[0:ROPE, 3 * DB:4 * DB], lat[:, OFF_KR:LA], ident[0:DB, 0:DB]).then_inc(setup_pe, 1)
            pe.wait_ge(w_in2, 64)
            pe.wait_ge(setup_dve, 1)
            for k in range(2):
                for c in range(QC):
                    last = pe.matmul(ps_s[0:DB, k, 0:H * QK // 2], lat_c[:, c, :],
                                     wuq_s[:, c, k * H * QK // 2:(k + 1) * H * QK // 2], start=(c == 0), stop=(c == QC - 1))
            last.then_inc(setup_pe, 1)
            for h in range(H):
                last = pe.transpose(ps_t[0:NOPE, h // 4, (h % 4) * P:(h % 4 + 1) * P], wuk_s[:, h * NOPE:(h + 1) * NOPE], ident[:])
            last.then_inc(setup_pe, 1)
            pe.wait_ge(pool_dve, 3)
            for g in range(NG):
                last = pe.transpose(ps_a[:, g * DB:(g + 1) * DB], wsum[:, g * P:(g + 1) * P], ident[0:DB, 0:DB])
            last.then_inc(pool_pe, 1)
            pe.wait_ge(setup_dve, 5)
            for h in range(H):
                pe.transpose(ps_o[0:NOPE, h * DB:(h + 1) * DB], qrow[:, h, 0:NOPE], ident[0:DB, 0:DB])
                last = pe.transpose(ps_o[0:ROPE, (H + h) * DB:(H + h + 1) * DB], qrow[:, h, NOPE:QK], ident[0:DB, 0:DB])
            last.then_inc(setup_pe, 1)
            pe.wait_ge(pool_dve, 4)
            for g in range(NG):
                last = pe.matmul(ps_a[0:DB, g * P:(g + 1) * P], pool_c[:, g, :], wp_s[:, g, :], start=True, stop=True)
            last.then_inc(pool_pe, 1)
            pe.wait_ge(setup_dve, 7)
            for h in range(H):
                last = pe.matmul(ps_m[:, h * DB:(h + 1) * DB], wuk_t[:, h, :], qn_c[:, h, :], start=True, stop=True)
            last.then_inc(setup_pe, 1)
            pe.wait_ge(setup_dve, 8)
            pe.wait_ge(pool_dve, 5)
            for n in range(DB):
                pe.matmul(ps_a[0:1, n * H:(n + 1) * H], lat_c[:, QC, n:n + 1], qabs[:, n, :], start=True, stop=False)
                pe.matmul(ps_a[0:1, n * H:(n + 1) * H], krt[:, n:n + 1], qr[0:ROPE, n, 0, :], start=False, stop=True)
                pe.matmul(ps_r[0:H, n:n + 1], qabs[:, n, :], lat_c[:, QC, n:n + 1], start=True, stop=False)
                last = pe.matmul(ps_r[0:H, n:n + 1], qr[0:ROPE, n, 0, :], krt[:, n:n + 1], start=False, stop=True)
            last.then_inc(setup_pe, 1)

    ITEMS = [("r", 0), ("t", 0), ("t", 1), ("t", 2), ("t", 3), ("r", 1), ("t", 4), ("t", 5), ("t", 6), ("t", 7)]
    NI = len(ITEMS)
    assert QT == 8 and NI % 2 == 0 and NB == 2 * DB
    item_of = {n: j for j, (what, n) in enumerate(ITEMS) if what == "t"}

    def scored_before(j):
        what, n = ITEMS[j]
        if what == "r":
            return QT // 2 * n
        return max([g + 1 for g, i in item_of.items() if i < j and i % 2 == j % 2] +
                   [g + 1 - QT for g, i in item_of.items() if i > j and i % 2 == j % 2])

    UNITS = 4 * KC
    HU = UNITS // 2

    def sample_units(s):
        last = isinstance(s, int) and s == DB - 1
        stride = 1 if last else 2
        names = ("tile_maxima", "turn_maxima", "head_maxima", "spread", "shift", "exp", "sum")
        at = dict(zip(names, range(stride * NI + 2, UNITS)))
        if last:
            at.update(values=19, new=27, divide=28, project=29, mix=30, turn_mixed=31)
        return stride, at
    with ExitStack() as ctx:
        sems = []
        ctx.callback(release, nc, sems)

        def psum(name, shape):
            return ctx.enter_context(nc.psum_tensor("out_" + name, shape, F32))

        def sem(name):
            return stage_semaphore(nc, sems, "out_" + name)

        mo2 = Map(nc, m2.at)
        gs = mo2("out_gate_s", [DB, D], F32)
        crt = mo2("crt", [P, 512], F32)
        pr = [mo2(f"pr{e}", [P, TPP + 1, H], F32) for e in range(2)]
        mx8 = mo2("s_mx8", [P, 2, H], F32)
        negm = mo2("s_negm", [H, 2], F32)
        diag = mo2("s_diag", [H, 2, H], F32)
        crow_s = mo2("s_crow_s", [1, 2, KVL], F32)
        negb = mo2("s_negb", [P, 2, H], F32)
        dsum = mo2("s_dsum", [P, 2, H], F32)
        rec = mo2("s_rec", [P, 2, H], F32)
        olat = mo2("s_olat", [P, H, DB], F32)
        assert mo2.at <= after_lat
        m = Map(nc, stay.at)
        ckt = m("ckt", [P, 2, 512], F32)
        gate = m("gate", [P, D], F32)
        fn_w = m("fn_w", [P, D], F32)
        ar = [m(f"att_rows{b}", [P, DATT], F32) for b in range(2)]
        ga = [m(f"gate_rows{b}", [P, DATT], F32) for b in range(2)]
        pc = [m(f"pool_cols{b}", [P, NG, P], F32) for b in range(2)]
        xr = [m(f"x_rows{b}", [P, D], F32) for b in range(2)]
        mh = [m(f"mixed_hi{b}", [P, KC, P], F32R) for b in range(2)]
        ml = [m(f"mixed_lo{b}", [P, KC, P], F32R) for b in range(2)]
        y = [m(f"y{b}", [P, D], F32) for b in range(2)]
        junk = m("out_junk", [P, 2, D], BF16)
        stat = m("out_stat", [P, 2], F32)
        ps_t = psum("ps_t", [P, 512])
        ps_y = psum("ps_y", [P, 2, 512])
        ps_c = psum("ps_c", [P, 2, 512])
        ps_s = psum("ps_s", [P, 512])
        ps_m = psum("ps_m", [P, 512])
        ps_o = psum("ps_o", [P, 512])
        tab_in, gs_in = sem("tab_in"), sem("gs_in")
        r_in = [sem("rows_in0"), sem("rows_in1")]
        x_in = [sem("x_in0"), sem("x_in1")]
        gated, turned, hi_ready, lo_att, lo_pool = sem("gated"), sem("turned"), sem("hi_ready"), sem("lo_att"), sem("lo_pool")
        half_done, y_sum, ss_ready, var_ready, sd_ready, r_ready, y_ready = (
            sem("half_done"), sem("y_sum"), sem("ss_ready"), sem("var_ready"), sem("sd_ready"), sem("r_ready"), sem("y_ready"))
        y_out = [sem("y_out0"), sem("y_out1")]
        piece_turned, piece_kept, scored = sem("piece_turned"), [sem("piece_kept0"), sem("piece_kept1")], sem("scored")
        mx_ready, mx_turned, negm_ready, diag_ready, negb_done, negb_ready = (
            sem("mx_ready"), sem("mx_turned"), sem("negm_ready"), sem("diag_ready"), sem("negb_done"), sem("negb_ready"))
        shifted, exp_ready, dsum_ready, pv_done, rec_ready, olat_ready = (
            sem("shifted"), sem("exp_ready"), sem("dsum_ready"), sem("pv_done"), sem("rec_ready"), sem("olat_ready"))
        fin_pe, fin_dve = sem("fin_pe"), sem("fin_dve")
        att_blocks = att_d.rearrange("(n p) e -> p n e", p=P)
        pool_cols = pool_d.rearrange("g p s -> p g s")
        y_blocks = o[0].rearrange("a (n p) d -> p (a n) d", p=P)
        block = ctx.enter_context(nc.Block())

        @block.sync
        def _(sp):
            def load(n, b):
                sp.dma_start(ar[b][:].unsqueeze(1), att_blocks[:, ds(n, 1), :]).then_inc(r_in[b], 16)
                sp.dma_start(ga[b][:].unsqueeze(1), gate_att_blocks[:, ds(n, 1), :]).then_inc(r_in[b], 16)
                sp.dma_start(pc[b][:], pool_cols[:, :, ds(n * P, P)]).then_inc(r_in[b], 16)

            def load_x(n, b):
                sp.dma_start(xr[b][:].unsqueeze(1), x_blocks[:, ds(n, 1), :]).then_inc(x_in[b], 16)

            def body(i):
                for b in range(2):
                    n = 2 * i + b
                    if exists(n + 2, NB):
                        sp.wait_ge(lo_pool, n + 1)
                        sp.wait_ge(turned, n + 1)
                        load(n + 2, b)
                        sp.wait_ge(y_sum, 3 * n + 3)
                        load_x(n + 2, b)
            for b in range(2):
                load(b, b)
            sp.dma_start(gate[:], mod_d[DB, 2 * D:].partition_broadcast(P)).then_inc(tab_in, 16)
            sp.dma_start(fn_w[:], t["final_norm_w"].partition_broadcast(P)).then_inc(tab_in, 16)
            for b in range(2):
                load_x(b, b)
            sp.dma_start(gs[:], mod_d[0:DB, 2 * D:]).then_inc(gs_in, 16)
            peeled(sp, DB, body)
            sp.wait_ge(y_sum, 3 * NB - 3)
            sp.dma_start(xr[0][0:DB, :], t["x_sample"].rearrange("b s d -> (b s) d")).then_inc(x_in[0], 16)
            sp.wait_ge(y_ready, NB + 1)
            sp.dma_start(o[1].rearrange("b s d -> (b s) d"), y[0][0:DB, :]).then_inc(y_out[0], 16)
            sp.wait_ge(y_out[0], 16 * (DB + 1))
            sp.wait_ge(y_out[1], 16 * DB)

        @block.scalar
        def _(act):
            def high(n, b):
                act.wait_ge(turned, n + 1)
                if exists(n - 2, NB):
                    act.wait_ge(half_done, 2 * n - 2)
                act.activation(mh[b][:, 0:GRP, :], ps_t[:].rearrange("p (c s) -> p c s", c=GRP), ACT.Copy)
                act.activation(mh[b][:, GRP:, :], pc[b][:], ACT.Copy).then_inc(hi_ready, 1)

            def squares(n, b, rows):
                act.wait_ge(y_sum, 3 * n + 3)
                act.activation(junk[0:rows, b, :], y[b][0:rows, :], ACT.Square, accum_out=stat[0:rows, b:b + 1]).then_inc(ss_ready, 1)

            def root(n, b, rows):
                act.wait_ge(var_ready, n + 1)
                act.activation(stat[0:rows, b:b + 1], stat[0:rows, b:b + 1], ACT.Sqrt).then_inc(sd_ready, 1)

            def store(n, b):
                act.wait_ge(y_ready, n + 1)
                act.dma_start(y_blocks[:, ds(n, 1), :], y[b][:].unsqueeze(1)).then_inc(y_out[b], 16)

            def keep(s, j):
                act.wait_ge(piece_turned, NI * s + j + 1)
                if scored_before(j) > 0 or exists(s - 1, DB):
                    act.wait_ge(scored, QT * s + scored_before(j))
                act.activation(crt[:] if ITEMS[j][0] == "r" else ckt[:, 0, :], ps_c[:, 0, :], ACT.Copy).then_inc(piece_kept[0], 1)

            def body(i, e):
                stride, at = sample_units(i)
                for u in range(UNITS):
                    b, v = divmod(u, HU)
                    n = 2 * i + b
                    if v == 2 and exists(n - 1, NB):
                        squares(n - 1, 1 - b, P)
                    if v == 3 and exists(n - 1, NB):
                        root(n - 1, 1 - b, P)
                    if v == 6 and exists(n - 1, NB):
                        store(n - 1, 1 - b)
                    if v == 8 and exists(n + 1, NB):
                        high(n + 1, 1 - b)
                    j, rest = divmod(u - 1, stride)
                    if rest == 0 and 0 <= j < NI and j % 2 == 0:
                        keep(i, j)
                    if u == at["exp"]:
                        act.wait_ge(shifted, i + 1)
                        act.activation(crow_s[:, e, :], crow[:, ds(i, 1), :].squeeze(1), ACT.Copy)
                        act.activation(pr[e][:, 0:TPP, :], pr[e][:, 0:TPP, :], ACT.Exp, scale=SCALE)
                        act.activation(pr[e][0:1, TPP, :], pr[e][0:1, TPP, :], ACT.Exp, scale=SCALE).then_inc(exp_ready, 1)
            high(0, 0)
            peeled(act, DB // 2, lambda i: [body(2 * i + e, e) for e in range(2)])
            squares(NB - 1, 1, P)
            root(NB - 1, 1, P)
            store(NB - 1, 1)
            squares(NB, 0, DB)
            root(NB, 0, DB)

        @block.gpsimd
        def _(pool):
            def gated_rows(n, b):
                pool.wait_ge(r_in[b], 24 * (n - b) + 48)
                pool.tensor_tensor(ar[b][:], ar[b][:], ga[b][:], ALU.mult).then_inc(gated, 1)

            def low(n, b):
                pool.wait_ge(hi_ready, n + 1)
                pool.tensor_tensor(ml[b][:, GRP:, :], pc[b][:], mh[b][:, GRP:, :].bitcast(F32), ALU.subtract).then_inc(lo_pool, 1)

            for b in range(2):
                gated_rows(b, b)
            low(0, 0)
            gather(pool, 1, 1)
            for n in range(NB):
                s = n // 2
                if n % 2 == 1 and 1 <= s < DB - 1:
                    pool.wait_ge(cache_in[(s + 1) % 2], 16 * (s - 1 - (s - 1) % 2) + 32)
                    pool.wait_ge(pv_done, s)
                    gather(pool, s + 1, (s + 1) % 2)
                if n + 1 < NB:
                    low(n + 1, (n + 1) % 2)
                if n + 2 < NB:
                    gated_rows(n + 2, n % 2)

        @block.vector
        def _(dve):
            def low(n, b):
                dve.wait_ge(hi_ready, n + 1)
                dve.tensor_tensor(ml[b][:, 0:GRP, :], ps_t[:].rearrange("p (c s) -> p c s", c=GRP),
                                  mh[b][:, 0:GRP, :].bitcast(F32), ALU.subtract).then_inc(lo_att, 1)

            def gate_half(n, b, k, rows, g_rows):
                dve.wait_ge(half_done, 2 * n + k + 1)
                if k == 0 and exists(n - 2, NB):
                    dve.wait_ge(y_out[b], 8 * (n - b))
                cols = slice(k * 512, (k + 1) * 512)
                dve.tensor_tensor(y[b][0:rows, cols], ps_y[0:rows, k, :], g_rows[:, cols], ALU.mult).then_inc(y_sum, 1)

            def add_x(n, b, rows):
                dve.wait_ge(x_in[b], 8 * (n - b) + 16)
                dve.wait_ge(y_sum, 3 * n + 2)
                dve.tensor_tensor(y[b][0:rows, :], y[b][0:rows, :], xr[b][0:rows, :], ALU.add).then_inc(y_sum, 1)

            def variance(n, b, rows):
                dve.wait_ge(ss_ready, n + 1)
                dve.tensor_scalar(stat[0:rows, b:b + 1], stat[0:rows, b:b + 1], 1.0 / D, EPS, ALU.mult, ALU.add).then_inc(var_ready, 1)

            def normalise(n, b, rows):
                dve.wait_ge(sd_ready, n + 1)
                dve.reciprocal(stat[0:rows, b:b + 1], stat[0:rows, b:b + 1]).then_inc(r_ready, 1)
                dve.wait_ge(r_ready, n + 1)
                dve.scalar_tensor_tensor(out=y[b][0:rows, :], in0=y[b][0:rows, :], scalar=stat[0:rows, b:b + 1], in1=fn_w[0:rows, :],
                                         op0=ALU.mult, op1=ALU.mult).then_inc(y_ready, 1)

            def keep(s, j):
                dve.wait_ge(piece_turned, NI * s + j + 1)
                if scored_before(j) > 0 or exists(s - 1, DB):
                    dve.wait_ge(scored, QT * s + scored_before(j))
                dve.tensor_copy(crt[:] if ITEMS[j][0] == "r" else ckt[:, 1, :], ps_c[:, 1, :]).then_inc(piece_kept[1], 1)

            def tile_maxima(s, e):
                dve.wait_ge(scored, QT * s + QT)
                dve.tensor_reduce(mx8[:, e, :], ps_s[:, 0:TPP * H].rearrange("p (t h) -> p h t", h=H),
                                  AX.X, ALU.max).then_inc(mx_ready, 1)

            def head_maxima(s, e):
                dve.wait_ge(mx_turned, s + 1)
                dve.tensor_reduce(negm[:, e:e + 1], ps_m[0:H, 0:P], AX.X, ALU.max).then_inc(negm_ready, 1)
                dve.wait_ge(negm_ready, 2 * s + 1)
                dve.tensor_tensor(negm[:, e:e + 1], negm[:, e:e + 1], new_col[:, ds(s, 1)], ALU.max).then_inc(negm_ready, 1)
                dve.wait_ge(negm_ready, 2 * s + 2)
                dve.tensor_scalar(diag[:, e, :], ident[0:H, 0:H], negm[:, e:e + 1], -1.0, ALU.mult, ALU.mult).then_inc(diag_ready, 1)

            def shift(s, e):
                dve.wait_ge(negb_done, s + 1)
                dve.tensor_copy(negb[:, e, :], ps_m[:, P:P + H]).then_inc(negb_ready, 1)
                dve.wait_ge(negb_ready, s + 1)
                if exists(s - 2, DB):
                    dve.wait_ge(pv_done, s - 1)
                dve.tensor_tensor(pr[e][:, 0:TPP, :], ps_s[:, 0:TPP * H].rearrange("p (t h) -> p t h", h=H),
                                  negb[:, e, :].unsqueeze(1).broadcast_to([P, TPP, H]), ALU.add)
                dve.tensor_tensor(pr[e][0:1, TPP:TPP + 1, :], new_row[:, ds(s, 1), :], negb[0:1, e, :].unsqueeze(1),
                                  ALU.add).then_inc(shifted, 1)

            def denominators(s, e):
                dve.wait_ge(exp_ready, s + 1)
                dve.tensor_reduce(dsum[:, e, :], pr[e][:, 0:TPP, :].rearrange("p t h -> p h t"), AX.X, ALU.add).then_inc(dsum_ready, 1)

            def divide(s, e):
                dve.wait_ge(pv_done, s + 1)
                dve.reciprocal(rec[:, e, :], ps_o[:, H:2 * H]).then_inc(rec_ready, 1)
                dve.wait_ge(rec_ready, s + 1)
                dve.tensor_tensor(olat[:, :, ds(s, 1)], ps_o[:, 0:H].unsqueeze(2), rec[:, e, :].unsqueeze(2),
                                  ALU.mult).then_inc(olat_ready, 1)

            def body(i, e):
                stride, at = sample_units(i)
                for u in range(UNITS):
                    b, v = divmod(u, HU)
                    n = 2 * i + b
                    if v == 1 and exists(n - 1, NB):
                        gate_half(n - 1, 1 - b, 1, P, gate)
                        add_x(n - 1, 1 - b, P)
                    if v == 3 and exists(n - 1, NB):
                        variance(n - 1, 1 - b, P)
                    if v == 4 and exists(n - 1, NB):
                        normalise(n - 1, 1 - b, P)
                    if v == 9 and exists(n + 1, NB):
                        low(n + 1, 1 - b)
                    if v == 10:
                        gate_half(n, b, 0, P, gate)
                    j, rest = divmod(u - 1, stride)
                    if rest == 0 and 0 <= j < NI and j % 2:
                        keep(i, j)
                    if u == 2 * QT + 2 and exists(i - 1, DB):
                        divide(i - 1, 1 - e)
                    if u == at["tile_maxima"]:
                        tile_maxima(i, e)
                    if u == at["head_maxima"]:
                        head_maxima(i, e)
                    if u == at["shift"]:
                        shift(i, e)
                    if u == at["sum"]:
                        denominators(i, e)
                    if u == at.get("divide"):
                        divide(i, e)
                    if u == at.get("mix"):
                        dve.wait_ge(fin_pe, 1)
                        dve.tensor_tensor(mixed[:, 0:DATT], ps_c[0:DB, 0, :], z[:, LA:LA + DATT], ALU.mult).then_inc(fin_dve, 1)
            low(0, 0)
            dve.wait_ge(tab_in, 32)
            dve.wait_ge(gs_in, 16)
            peeled(dve, DB // 2, lambda i: [body(2 * i + e, e) for e in range(2)])
            dve.wait_ge(fin_pe, 2)
            split = ps_m[:, 0:KC * DB].rearrange("p (c b) -> p c b", c=KC)
            dve.tensor_copy(ms[0][:, :, 0:DB], split).then_inc(fin_dve, 1)
            dve.wait_ge(fin_dve, 2)
            dve.tensor_tensor(ms[1][:, :, 0:DB], split, ms[0][:, :, 0:DB].bitcast(F32), ALU.subtract).then_inc(fin_dve, 1)
            gate_half(NB - 1, 1, 1, P, gate)
            add_x(NB - 1, 1, P)
            variance(NB - 1, 1, P)
            normalise(NB - 1, 1, P)
            for k in range(2):
                gate_half(NB, 0, k, DB, gs)
            add_x(NB, 0, DB)
            variance(NB, 0, DB)
            normalise(NB, 0, DB)

        @block.tensor
        def _(pe):
            def turn(n, b):
                pe.wait_ge(gated, n + 1)
                if exists(n - 1, NB):
                    pe.wait_ge(lo_att, n)
                for c in range(GRP):
                    last = pe.transpose(ps_t[:, c * P:(c + 1) * P], ar[b][:, c * P:(c + 1) * P], ident[:])
                last.then_inc(turned, 1)

            def unit(n, part, v):
                k, c = divmod(v, KC)
                if c == 0 and exists(n - 1, NB + 1):
                    pe.wait_ge(y_sum, 3 * n - 2 + k)
                cols = slice(k * 512, (k + 1) * 512)
                last = mm3(pe, ps_y[:, k, :], [part[0][:, c, :], part[1][:, c, :]],
                           [wo[0][:, c, cols], wo[1][:, c, cols]], c == 0, c == KC - 1)
                if c == KC - 1:
                    last.then_inc(half_done, 1)

            def turn_piece(s, e, j):
                what, g = ITEMS[j]
                if j == 0:
                    pe.wait_ge(cache_in[e], 16 * (s - e) + 32)
                if j >= 2 or exists(s - 1, DB):
                    pe.wait_ge(piece_kept[j % 2], NI // 2 * s + j // 2)
                for k in range(GRP):
                    rows = (ck[e][:, g * GRP + k, :] if what == "t" else
                            cr[e][:, (g * QT // 2 + k) * GRP:(g * QT // 2 + k + 1) * GRP, :].rearrange("p g r -> p (g r)"))
                    last = pe.transpose(ps_c[:, j % 2, k * P:(k + 1) * P], rows, ident[:])
                last.then_inc(piece_turned, 1)

            def score(s, g):
                j = item_of[g]
                k = g % (QT // 2)
                if g == 0 and exists(s - 1, DB):
                    pe.wait_ge(shifted, s)
                if k == 0:
                    r = ITEMS.index(("r", g // (QT // 2)))
                    pe.wait_ge(piece_kept[r % 2], NI // 2 * s + r // 2 + 1)
                pe.wait_ge(piece_kept[j % 2], NI // 2 * s + j // 2 + 1)
                at = g * GRP * H
                pe.matmul(ps_s[:, at:at + GRP * H], crt[:, k * P:(k + 1) * P], qr[:, ds(s, 1), :, :].squeeze(1),
                          start=True, stop=False, skip_group_check=True)
                for x in range(GRP):
                    last = pe.matmul(ps_s[:, at + x * H:at + (x + 1) * H], ckt[:, j % 2, x * P:(x + 1) * P],
                                     qabs[:, ds(s, 1), :].squeeze(1), start=False, stop=(x == GRP - 1), skip_group_check=True)
                last.then_inc(scored, 1)

            def values(s, e, g):
                if g == 0:
                    pe.wait_ge(dsum_ready, s + 1)
                    if exists(s - 1, DB):
                        pe.wait_ge(olat_ready, s)
                for k in range(g * GRP, (g + 1) * GRP):
                    pe.matmul(ps_o[:, 0:H], ck[e][:, k, :], pr[e][:, k, :], start=(k == 0), stop=False)

            def new_value(s, e):
                pe.matmul(ps_o[:, 0:H], crow_s[:, e, :], pr[e][0:1, TPP, :], start=False, stop=True)
                pe.matmul(ps_o[:, H:2 * H], ones[:], dsum[:, e, :], start=True, stop=False)
                pe.matmul(ps_o[:, H:2 * H], ones[0:1, :], pr[e][0:1, TPP, :], start=False, stop=True).then_inc(pv_done, 1)

            def project(h_range):
                pe.wait_ge(olat_ready, DB)
                for h in h_range:
                    last = pe.matmul(ps_c[0:DB, 0, h * VD:(h + 1) * VD], olat[:, h, :], wuv_s[:, h * VD:(h + 1) * VD],
                                     start=True, stop=True)
                last.then_inc(fin_pe, 1)

            def turn_mixed():
                pe.wait_ge(fin_dve, 1)
                for c in range(KC):
                    last = pe.transpose(ps_m[:, c * DB:(c + 1) * DB], mixed[:, c * P:(c + 1) * P], ident[0:DB, 0:DB])
                last.then_inc(fin_pe, 1)

            def body(i, e):
                stride, at = sample_units(i)
                for u in range(UNITS):
                    b, v = divmod(u, HU)
                    n = 2 * i + b
                    if v == 0:
                        pe.wait_ge(lo_att, n + 1)
                        pe.wait_ge(lo_pool, n + 1)
                    unit(n, [mh[b], ml[b]], v)
                    if v == 6 and exists(n + 1, NB):
                        turn(n + 1, 1 - b)
                    if exists(i - 1, DB):
                        if u % 2 == 0 and u // 2 < QT:
                            values(i - 1, 1 - e, u // 2)
                        if u == 2 * QT:
                            new_value(i - 1, 1 - e)
                    j, rest = divmod(u - 1, stride)
                    if rest == 0:
                        if 0 <= j < NI:
                            turn_piece(i, e, j)
                        if 0 < j <= NI and ITEMS[j - 1][0] == "t":
                            score(i, ITEMS[j - 1][1])
                    if u == at["turn_maxima"]:
                        if exists(i - 1, DB):
                            pe.wait_ge(negb_ready, i)
                        pe.wait_ge(mx_ready, i + 1)
                        pe.transpose(ps_m[0:H, 0:P], mx8[:, e, :], ident[:]).then_inc(mx_turned, 1)
                    if u == at["spread"]:
                        pe.wait_ge(diag_ready, i + 1)
                        pe.matmul(ps_m[:, P:P + H], ones[0:H, :], diag[:, e, :], start=True, stop=True).then_inc(negb_done, 1)
                    if "values" in at and 0 <= u - at["values"] < QT:
                        values(i, e, u - at["values"])
                    if u == at.get("new"):
                        new_value(i, e)
                    if u == at.get("project"):
                        project(range(H))
                    if u == at.get("turn_mixed"):
                        turn_mixed()
            turn(0, 0)
            peeled(pe, DB // 2, lambda i: [body(2 * i + e, e) for e in range(2)])
            pe.wait_ge(fin_dve, 3)
            for v in range(2 * KC):
                unit(NB, ms, v)




_INS = ["x_prompt", "x_sample", "c_prompt", "c_sample", "cache_ckv", "cache_krope", "state_pool", "page_table",
        "ada_w", "ada_b", "norm_w", "w_in", "q_norm_w", "w_uq", "kv_norm_w", "w_uk", "w_uv",
        "w_pool", "b_pool", "pool_scale", "w_out", "final_norm_w"]
_OUTS = [(1, S, D), (DB, 1, D), (1, 1, S, KVL), (1, 1, S, ROPE), (1, 1, PREV, DPOOL),
         (1, DB, 1, KVL), (1, DB, 1, ROPE), (1, DB, PREV, DPOOL)]


def _constants():
    f32 = np.float32
    inv = (f32(10000.0) ** (-np.arange(0, ROPE, 2, dtype=f32) / f32(ROPE))).astype(f32)

    def tables(pos):
        ang = (pos.astype(f32)[:, None] * inv[None, :]).astype(f32).astype(np.float64)
        cos, sin = np.cos(ang).astype(f32), np.sin(ang).astype(f32)
        return np.concatenate([cos, cos], 1), np.concatenate([-sin, sin], 1)

    cos, sin = tables(np.arange(S))
    cos_s, sin_s = tables(np.full(DB, NPG * PG))
    tok = np.arange(P)
    late = np.where(tok[None, :] <= tok[:, None], 0.0, MASKED)
    windows = 2 ** (np.arange(NG) + 1)
    return {
        "c_ident": np.eye(P, dtype=f32),
        "c_mask_q": late.astype(f32),
        "c_mask_k": np.ascontiguousarray(late.T).astype(f32),
        "c_rope_rows": np.ascontiguousarray(np.stack([cos, sin]).reshape(2, NB, P, ROPE).transpose(0, 2, 1, 3)),
        "c_rope_cols": np.ascontiguousarray(np.concatenate([np.ones((NOPE, S), f32), cos.T, sin.T])),
        "c_rope_sample": np.stack([cos_s, sin_s]),
        "c_count": (1.0 / np.minimum(tok[None, :16] + 1.0, windows[:, None])).astype(f32),
        "c_spread": np.where(tok[None, :] // QTR == np.arange(NPG)[:, None], float(QTR), 0.0).astype(f32),
        "c_quarter": (tok % QTR).astype(f32)[:, None],
    }


def kernel(**inputs):
    import numpy as _np
    import concourse.bacc as _bacc
    from concourse import mybir as _mybir
    from concourse.bass_utils import run_bass_kernel_spmd as _run

    nc = _bacc.Bacc("TRN2", target_bir_lowering=False, num_devices=1)
    arrays, tensors = {}, {}
    data = {name: _np.ascontiguousarray(inputs[name]) for name in _INS}
    data.update(_constants())
    for name, a in data.items():
        arrays[f"in_{name}_dram"] = a
        tensors[name] = nc.dram_tensor(f"in_{name}_dram", a.shape, _mybir.dt.from_np(a.dtype), kind="ExternalInput").ap()
    outs = [nc.dram_tensor(f"out_{i}_dram", shape, _mybir.dt.float32, kind="ExternalOutput").ap()
            for i, shape in enumerate(_OUTS)]
    build(nc, tensors, outs)
    r = _run(nc, [arrays], core_ids=[0])
    return tuple(r.results[0][f"out_{i}_dram"] for i in range(len(_OUTS)))
```
